# Optimizing a Trainium2 kernel written in Bass

```python
import math
import jax, jax.numpy as jnp
from jax import lax
import numpy as np

D_MODEL = 1024
BATCH = 1
SEQ = 128
DEPTH = 2
DEC_BATCH = 1
DEC_SEQ = 512
PAST_LEN = 128

F32 = jnp.float32
GRID_W = 64
POS_BASE = 10000.0
N_DIR = 2
N_EVEN = (DEPTH + 1) // 2
N_ODD = DEPTH // 2
N_MOD = 6
CHUNK = 64
SHORT_CONV = 3
NORM_EPS = 1e-6

A_HEAD_DIM = 128
A_WIDTH = D_MODEL // 2
A_HEADS = A_WIDTH // A_HEAD_DIM
A_FGATE_LO = 3.0
A_FGATE_HI = 6.0
A_COLS = (A_WIDTH, A_WIDTH, A_WIDTH, A_WIDTH, 2 * N_DIR * A_HEADS)
A_IN = sum(A_COLS)

B_HEAD_DIM = 64
B_WIDTH = D_MODEL // 2
B_HEADS = B_WIDTH // B_HEAD_DIM
B_DECAY_RANK = 64
B_AAA_RANK = 64
B_GATE_RANK = 128
B_DECAY_SCALE = 0.606531
B_W0_LO = -6.5
B_W0_HI = -1.5
B_LN_EPS = 64e-5
B_COLS = (B_WIDTH, B_WIDTH, B_WIDTH, N_DIR * B_DECAY_RANK, B_AAA_RANK, B_GATE_RANK)
B_IN = sum(B_COLS)
EVEN_IN = A_IN + B_IN

C_INNER = 2 * D_MODEL
C_HEAD_DIM = 64
C_HEADS = C_INNER // C_HEAD_DIM
C_GROUPS = 8
C_STATE = 128
C_BC = C_GROUPS * C_STATE
C_XBC = C_INNER + 2 * C_BC
ODD_COLS = (C_INNER, C_XBC, N_DIR * C_HEADS)
ODD_IN = sum(ODD_COLS)

FFN_HIDDEN = ((8 * D_MODEL + 3 * 256 - 1) // (3 * 256)) * 256

kernel_name = 'bidir_mlstm_rwkv7_ssd_flow_step'

def split_last(x, sizes):
    return jnp.split(x, np.cumsum(sizes)[:-1].tolist(), axis=-1)

def rev(z, axis, backward):
    return jnp.flip(z, axis) if backward else z

def rms_norm(x, w):
    xf = x.astype(F32)
    y = xf * lax.rsqrt(jnp.mean(xf * xf, -1, keepdims=True) + NORM_EPS) * w.astype(F32)
    return y.astype(x.dtype)

def head_norm(x, w, b, eps):
    xf = x.astype(F32)
    xc = xf - jnp.mean(xf, -1, keepdims=True)
    y = xc * lax.rsqrt(jnp.mean(xc * xc, -1, keepdims=True) + eps) * w.astype(F32)
    return y if b is None else y + b.astype(F32)

def centred_dwconv(x, w, b):
    pad = w.shape[0] // 2
    y = lax.conv_general_dilated(x, w[:, None, :].astype(x.dtype), window_strides=(1,), padding=[(pad, pad)],
                                 dimension_numbers=('NWC', 'WIO', 'NWC'), feature_group_count=x.shape[-1])
    return y + b

def centred_shift(p, mu):
    prev = jnp.pad(p, ((0, 0), (1, 0), (0, 0)))[:, :-1]
    nxt = jnp.pad(p, ((0, 0), (0, 1), (0, 0)))[:, 1:]
    return p + mu * (0.5 * (prev + nxt) - p)

def to_heads(z, nh):
    b, t, w = z.shape
    return z.reshape(b, t, nh, w // nh).transpose(0, 2, 1, 3)

def grid_pos_embed(rows, dim):
    r = jnp.repeat(jnp.arange(rows, dtype=F32), GRID_W)
    col = jnp.tile(jnp.arange(GRID_W, dtype=F32), rows)
    nf = dim // 4
    freq = jnp.exp(-math.log(POS_BASE) * jnp.arange(nf, dtype=F32) / nf)
    ar, ac = r[:, None] * freq, col[:, None] * freq
    return jnp.concatenate([jnp.sin(ar), jnp.cos(ar), jnp.sin(ac), jnp.cos(ac)], -1)

def modulation(cvec, w, b):
    m = jax.nn.silu(cvec) @ w + b
    return [z[:, None, :] for z in jnp.split(m, N_MOD, axis=-1)]

def swiglu(h, w_in, w_out):
    gate, up = jnp.split(h @ w_in, 2, axis=-1)
    return (jax.nn.silu(gate) * up) @ w_out

def mlstm_chunkwise(q, k, v, log_i, log_f, c0, n0, m0):
    bsz, nh, t, dh = q.shape
    nc = t // CHUNK
    qc, kc, vc = (z.reshape(bsz, nh, nc, CHUNK, dh) for z in (q, k, v))
    li = log_i.reshape(bsz, nh, nc, CHUNK)
    b = jnp.cumsum(log_f.reshape(bsz, nh, nc, CHUNK), axis=-1)
    b_end = b[..., -1]
    e = b_end[..., None] - b + li
    m_loc = jnp.max(e, -1)
    w_loc = jnp.exp(e - m_loc[..., None])
    c_loc = jnp.einsum('bhcs,bhcsk,bhcsv->bhckv', w_loc, kc, vc)
    n_loc = jnp.einsum('bhcs,bhcsk->bhck', w_loc, kc)

    def step(carry, inp):
        c, n, m = carry
        be, ml, cl, nl = inp
        m_new = jnp.maximum(be + m, ml)
        dec, sc = jnp.exp(be + m - m_new), jnp.exp(ml - m_new)
        c_new = dec[..., None, None] * c + sc[..., None, None] * cl
        n_new = dec[..., None] * n + sc[..., None] * nl
        return (c_new, n_new, m_new), (c, n, m)

    xs = tuple(jnp.moveaxis(z, 2, 0) for z in (b_end, m_loc, c_loc, n_loc))
    (cf, nf, mf), (cs, ns, ms) = lax.scan(step, (c0, n0, m0), xs)
    cs, ns, ms = jnp.moveaxis(cs, 0, 2), jnp.moveaxis(ns, 0, 2), jnp.moveaxis(ms, 0, 2)
    g = b + ms[..., None]
    causal = jnp.tril(jnp.ones((CHUNK, CHUNK), bool))
    d = jnp.where(causal, b[..., :, None] - b[..., None, :] + li[..., None, :], -jnp.inf)
    m_out = jnp.maximum(g, jnp.max(d, -1))
    w_intra = jnp.exp(d - m_out[..., None])
    w_inter = jnp.exp(g - m_out)
    s = jnp.einsum('bhctk,bhcsk->bhcts', qc, kc) * w_intra
    num = jnp.einsum('bhcts,bhcsv->bhctv', s, vc) + w_inter[..., None] * jnp.einsum('bhctk,bhckv->bhctv', qc, cs)
    den = jnp.sum(s, -1) + w_inter * jnp.einsum('bhctk,bhck->bhct', qc, ns)
    h = num / jnp.maximum(jnp.abs(den), jnp.exp(-m_out))[..., None]
    return h.reshape(bsz, nh, t, dh), (cf, nf, mf)

def rwkv7_scan(r, decay, k, v, kk, a, s0):
    def step(s, inp):
        r_t, w_t, k_t, v_t, kk_t, a_t = inp
        s_kk = jnp.einsum('bhvk,bhk->bhv', s, kk_t)
        s = (s * w_t[:, :, None, :] - s_kk[..., :, None] * (kk_t * a_t)[:, :, None, :]
             + v_t[..., :, None] * k_t[:, :, None, :])
        return s, jnp.einsum('bhvk,bhk->bhv', s, r_t)

    xs = tuple(jnp.moveaxis(z, 1, 0) for z in (r, decay, k, v, kk, a))
    s_final, y = lax.scan(step, s0, xs)
    return jnp.moveaxis(y, 0, 1), s_final

def ssd_chunkwise(x, dt, a, bm, cm, s0):
    bsz, t, nh, hp = x.shape
    ng, nst = bm.shape[2], bm.shape[3]
    hr = nh // ng
    nc = t // CHUNK
    xc = x.reshape(bsz, nc, CHUNK, ng, hr, hp)
    dtc = dt.reshape(bsz, nc, CHUNK, ng, hr)
    bc = bm.reshape(bsz, nc, CHUNK, ng, nst)
    cc = cm.reshape(bsz, nc, CHUNK, ng, nst)
    cum = jnp.cumsum(dtc * a.reshape(ng, hr), axis=2)
    causal = jnp.tril(jnp.ones((CHUNK, CHUNK), bool))[:, :, None, None]
    seg = jnp.exp(jnp.where(causal, cum[:, :, :, None] - cum[:, :, None, :], -jnp.inf))
    dx = dtc[..., None] * xc
    cb = jnp.einsum('bctgn,bcsgn->bctsg', cc, bc)
    y_diag = jnp.einsum('bctsg,bctsgr,bcsgrp->bctgrp', cb, seg, dx)
    decay_end = jnp.exp(cum[:, :, -1:] - cum)
    s_loc = jnp.einsum('bclgn,bclgr,bclgrp->bcgrpn', bc, decay_end, dx)
    chunk_decay = jnp.exp(cum[:, :, -1])

    def step(s, inp):
        cd, sl = inp
        return cd[..., None, None] * s + sl, s

    s_fin, s_start = lax.scan(step, s0.reshape(bsz, ng, hr, hp, nst),
                              (jnp.moveaxis(chunk_decay, 1, 0), jnp.moveaxis(s_loc, 1, 0)))
    s_start = jnp.moveaxis(s_start, 0, 1)
    y_off = jnp.einsum('bctgn,bcgrpn,bctgr->bctgrp', cc, s_start, jnp.exp(cum))
    y = (y_diag + y_off).reshape(bsz, t, nh, hp)
    return y, s_fin.reshape(bsz, nh, hp, nst)

def even_mixer(h, init_state, w_in, a_conv_w, a_conv_b, a_gate_b, a_norm_w,
               b_mu, b_w0, b_w_up, b_a0, b_a_up, b_g_up, b_k_k, b_k_a, b_u, b_ln_w, b_ln_b, w_out):
    c0, n0, m0, s0 = init_state
    bsz, t, _ = h.shape
    proj = h @ w_in
    pa, pb = proj[..., :A_IN], proj[..., A_IN:]
    aq, ak, av, ao, agate = split_last(pa, A_COLS)
    qk = jax.nn.silu(centred_dwconv(jnp.concatenate([aq, ak], -1), a_conv_w, a_conv_b))
    aq, ak = jnp.split(qk.astype(F32), 2, axis=-1)
    q = to_heads(aq, A_HEADS)
    k = to_heads(ak, A_HEADS) * (A_HEAD_DIM ** -0.5)
    v = to_heads(av.astype(F32), A_HEADS)
    gates = (agate.reshape(bsz, t, 2, N_DIR, A_HEADS) + a_gate_b).astype(F32)
    log_i = jnp.moveaxis(gates[:, :, 0], 1, -1)
    log_f = jax.nn.log_sigmoid(jnp.moveaxis(gates[:, :, 1], 1, -1))
    ha = jnp.zeros_like(q)
    st_a = []
    for d in range(N_DIR):
        bw = d == 1
        hd, st = mlstm_chunkwise(rev(q, 2, bw), rev(k, 2, bw), rev(v, 2, bw), rev(log_i[:, d], 2, bw),
                                 rev(log_f[:, d], 2, bw), c0[:, d], n0[:, d], m0[:, d])
        ha = ha + rev(hd, 2, bw)
        st_a.append(st)
    ha = head_norm(ha, a_norm_w.reshape(A_HEADS, 1, A_HEAD_DIM), None, NORM_EPS)
    ya = ha.transpose(0, 2, 1, 3).reshape(bsz, t, A_WIDTH).astype(h.dtype) * jax.nn.sigmoid(ao)
    pb = centred_shift(pb, b_mu).astype(F32)
    br, bk, bv, bw_lo, ba_lo, bg_lo = split_last(pb, B_COLS)
    a = jax.nn.sigmoid(b_a0.astype(F32) + ba_lo @ b_a_up.astype(F32))
    g = jax.nn.sigmoid(bg_lo) @ b_g_up.astype(F32)
    kk = (bk * b_k_k).reshape(bsz, t, B_HEADS, B_HEAD_DIM)
    kk = kk / jnp.maximum(jnp.sqrt(jnp.sum(kk * kk, -1, keepdims=True)), 1e-12)
    kb = bk * (1.0 + (a - 1.0) * b_k_a)
    shp = (bsz, t, B_HEADS, B_HEAD_DIM)
    r, kb, vb, ah = br.reshape(shp), kb.reshape(shp), bv.reshape(shp), a.reshape(shp)
    yb = jnp.zeros_like(r)
    bonus = jnp.zeros_like(r)
    st_b = []
    for d, w_lo in enumerate(jnp.split(bw_lo, N_DIR, axis=-1)):
        bw = d == 1
        decay = jnp.exp(-B_DECAY_SCALE * jax.nn.sigmoid(b_w0[d] + jnp.tanh(w_lo) @ b_w_up[d].astype(F32))).reshape(shp)
        yd, sd = rwkv7_scan(*(rev(z, 1, bw) for z in (r, decay, kb, vb, kk, ah)), s0[:, d])
        yb = yb + rev(yd, 1, bw)
        bonus = bonus + jnp.sum(r * kb * b_u[d].reshape(B_HEADS, B_HEAD_DIM), -1, keepdims=True) * vb
        st_b.append(sd)
    yb = head_norm(yb, b_ln_w.reshape(B_HEADS, B_HEAD_DIM), b_ln_b.reshape(B_HEADS, B_HEAD_DIM), B_LN_EPS) + bonus
    yb = (yb.reshape(bsz, t, B_WIDTH) * g).astype(h.dtype)
    out = jnp.concatenate([ya, yb], axis=-1) @ w_out
    new_state = (jnp.stack([s[0] for s in st_a], 1), jnp.stack([s[1] for s in st_a], 1),
                 jnp.stack([s[2] for s in st_a], 1), jnp.stack(st_b, 1))
    return out, new_state

def odd_mixer(h, s0, w_in, conv_w, conv_b, dt_bias, a_log, d_skip, norm_w, w_out):
    bsz, t, _ = h.shape
    z, xbc, dt_raw = split_last(h @ w_in, ODD_COLS)
    xbc = jax.nn.silu(centred_dwconv(xbc, conv_w, conv_b)).astype(F32)
    xs, bm, cm = split_last(xbc, (C_INNER, C_BC, C_BC))
    xs = xs.reshape(bsz, t, C_HEADS, C_HEAD_DIM)
    bm = bm.reshape(bsz, t, C_GROUPS, C_STATE)
    cm = cm.reshape(bsz, t, C_GROUPS, C_STATE)
    dt_raw = dt_raw.reshape(bsz, t, N_DIR, C_HEADS).astype(F32)
    y = xs * d_skip.astype(F32)[:, None]
    st = []
    for d in range(N_DIR):
        bw = d == 1
        dt = jax.nn.softplus(dt_raw[:, :, d] + dt_bias[d].astype(F32))
        a = -jnp.exp(a_log[d].astype(F32))
        yd, sd = ssd_chunkwise(rev(xs, 1, bw), rev(dt, 1, bw), a, rev(bm, 1, bw), rev(cm, 1, bw), s0[:, d])
        y = y + rev(yd, 1, bw)
        st.append(sd)
    y = y.reshape(bsz, t, C_INNER) * jax.nn.silu(z.astype(F32))
    y = rms_norm(y, norm_w).astype(h.dtype)
    return y @ w_out, jnp.stack(st, 1)

def block(x, mods, nw, fw_in, fw_out, mixer, params, init_state):
    sh1, sc1, g1, sh2, sc2, g2 = mods
    h = rms_norm(x, nw[0]) * (1 + sc1) + sh1
    out, state = mixer(h, init_state, *params)
    x = x + g1 * out
    h = rms_norm(x, nw[1]) * (1 + sc2) + sh2
    x = x + g2 * swiglu(h, fw_in, fw_out)
    return x, state

def setup_inputs(seed: int = 0) -> dict:
    key = jax.random.key(seed)
    keys = iter(jax.random.split(key, 64))

    def nrm(shape, scale):
        return scale * jax.random.normal(next(keys), shape, F32)

    def unif(shape, lo, hi):
        return jax.random.uniform(next(keys), shape, F32, lo, hi)

    d = D_MODEL
    gate_b = jnp.stack([nrm((N_EVEN, N_DIR, A_HEADS), 0.1),
                        jnp.linspace(A_FGATE_LO, A_FGATE_HI, A_HEADS, dtype=F32) + nrm((N_EVEN, N_DIR, A_HEADS), 0.1)],
                       axis=1)
    dt0 = jnp.exp(unif((N_ODD, N_DIR, C_HEADS), math.log(1e-3), math.log(1e-1)))
    return {
        'x_prompt': nrm((BATCH, SEQ, d), 1.0),
        'x_sample': nrm((DEC_BATCH, DEC_SEQ, d), 1.0),
        'state_mlstm_c': nrm((DEC_BATCH, N_EVEN, N_DIR, A_HEADS, A_HEAD_DIM, A_HEAD_DIM), 0.3),
        'state_mlstm_n': nrm((DEC_BATCH, N_EVEN, N_DIR, A_HEADS, A_HEAD_DIM), 0.3),
        'state_mlstm_m': nrm((DEC_BATCH, N_EVEN, N_DIR, A_HEADS), 1.0),
        'state_rwkv': nrm((DEC_BATCH, N_EVEN, N_DIR, B_HEADS, B_HEAD_DIM, B_HEAD_DIM), 0.3),
        'state_ssd': nrm((DEC_BATCH, N_ODD, N_DIR, C_HEADS, C_HEAD_DIM, C_STATE), 0.3),
        'c': nrm((DEC_BATCH, d), 1.0),
        'c_ctx': nrm((d,), 1.0),
        'mod_w': nrm((DEPTH, d, N_MOD * d), 0.5 * d ** -0.5),
        'mod_b': nrm((DEPTH, N_MOD * d), 0.02),
        'norm_w': 1.0 + nrm((DEPTH, 2, d), 0.02),
        'ffn_w_in': nrm((DEPTH, d, 2 * FFN_HIDDEN), d ** -0.5),
        'ffn_w_out': nrm((DEPTH, FFN_HIDDEN, d), FFN_HIDDEN ** -0.5),
        'ev_w_in': nrm((N_EVEN, d, EVEN_IN), d ** -0.5),
        'ev_a_conv_w': nrm((N_EVEN, SHORT_CONV, 2 * A_WIDTH), SHORT_CONV ** -0.5),
        'ev_a_conv_b': nrm((N_EVEN, 2 * A_WIDTH), 0.02),
        'ev_a_gate_b': gate_b,
        'ev_a_norm_w': 1.0 + nrm((N_EVEN, A_WIDTH), 0.02),
        'ev_b_mu': unif((N_EVEN, B_IN), 0.0, 1.0),
        'ev_b_w0': jnp.linspace(B_W0_LO, B_W0_HI, B_WIDTH, dtype=F32) + nrm((N_EVEN, N_DIR, B_WIDTH), 0.1),
        'ev_b_w_up': nrm((N_EVEN, N_DIR, B_DECAY_RANK, B_WIDTH), 0.1 * B_DECAY_RANK ** -0.5),
        'ev_b_a0': nrm((N_EVEN, B_WIDTH), 0.1),
        'ev_b_a_up': nrm((N_EVEN, B_AAA_RANK, B_WIDTH), 0.1 * B_AAA_RANK ** -0.5),
        'ev_b_g_up': nrm((N_EVEN, B_GATE_RANK, B_WIDTH), B_GATE_RANK ** -0.5),
        'ev_b_k_k': 0.85 + nrm((N_EVEN, B_WIDTH), 0.02),
        'ev_b_k_a': 1.0 + nrm((N_EVEN, B_WIDTH), 0.02),
        'ev_b_u': nrm((N_EVEN, N_DIR, B_WIDTH), 0.1),
        'ev_b_ln_w': 1.0 + nrm((N_EVEN, B_WIDTH), 0.02),
        'ev_b_ln_b': nrm((N_EVEN, B_WIDTH), 0.02),
        'ev_w_out': nrm((N_EVEN, A_WIDTH + B_WIDTH, d), (A_WIDTH + B_WIDTH) ** -0.5),
        'od_w_in': nrm((N_ODD, d, ODD_IN), d ** -0.5),
        'od_conv_w': nrm((N_ODD, SHORT_CONV, C_XBC), SHORT_CONV ** -0.5),
        'od_conv_b': nrm((N_ODD, C_XBC), 0.02),
        'od_dt_bias': dt0 + jnp.log(-jnp.expm1(-dt0)),
        'od_a_log': jnp.log(unif((N_ODD, N_DIR, C_HEADS), 1.0, 16.0)),
        'od_d': 1.0 + nrm((N_ODD, C_HEADS), 0.1),
        'od_norm_w': 1.0 + nrm((N_ODD, C_INNER), 0.02),
        'od_w_out': nrm((N_ODD, C_INNER, d), C_INNER ** -0.5),
        'final_norm_w': 1.0 + nrm((d,), 0.02),
    }

def reference(x_prompt, x_sample, state_mlstm_c, state_mlstm_n, state_mlstm_m, state_rwkv, state_ssd,
              c, c_ctx, mod_w, mod_b, norm_w, ffn_w_in, ffn_w_out,
              ev_w_in, ev_a_conv_w, ev_a_conv_b, ev_a_gate_b, ev_a_norm_w,
              ev_b_mu, ev_b_w0, ev_b_w_up, ev_b_a0, ev_b_a_up, ev_b_g_up, ev_b_k_k, ev_b_k_a, ev_b_u,
              ev_b_ln_w, ev_b_ln_b, ev_w_out,
              od_w_in, od_conv_w, od_conv_b, od_dt_bias, od_a_log, od_d, od_norm_w, od_w_out,
              final_norm_w):
    out_dtype = x_prompt.dtype
    rows = x_sample.shape[1] // GRID_W
    xs = x_sample + grid_pos_embed(rows, D_MODEL).astype(x_sample.dtype)
    xp = x_prompt
    bp = x_prompt.shape[0]
    zero_even = (jnp.zeros((bp, N_DIR, A_HEADS, A_HEAD_DIM, A_HEAD_DIM), F32),
                 jnp.zeros((bp, N_DIR, A_HEADS, A_HEAD_DIM), F32),
                 jnp.zeros((bp, N_DIR, A_HEADS), F32),
                 jnp.zeros((bp, N_DIR, B_HEADS, B_HEAD_DIM, B_HEAD_DIM), F32))
    zero_odd = jnp.zeros((bp, N_DIR, C_HEADS, C_HEAD_DIM, C_STATE), F32)
    ev_states, od_states = [], []
    for l in range(DEPTH):
        mods_p = modulation(c_ctx[None, :], mod_w[l], mod_b[l])
        mods_s = modulation(c, mod_w[l], mod_b[l])
        if l % 2 == 0:
            e = l // 2
            params = (ev_w_in[e], ev_a_conv_w[e], ev_a_conv_b[e], ev_a_gate_b[e], ev_a_norm_w[e],
                      ev_b_mu[e], ev_b_w0[e], ev_b_w_up[e], ev_b_a0[e], ev_b_a_up[e], ev_b_g_up[e],
                      ev_b_k_k[e], ev_b_k_a[e], ev_b_u[e], ev_b_ln_w[e], ev_b_ln_b[e], ev_w_out[e])
            cached = (state_mlstm_c[:, e].astype(F32), state_mlstm_n[:, e].astype(F32),
                      state_mlstm_m[:, e].astype(F32), state_rwkv[:, e].astype(F32))
            xp, st = block(xp, mods_p, norm_w[l], ffn_w_in[l], ffn_w_out[l], even_mixer, params, zero_even)
            xs, _ = block(xs, mods_s, norm_w[l], ffn_w_in[l], ffn_w_out[l], even_mixer, params, cached)
            ev_states.append(st)
        else:
            o = l // 2
            params = (od_w_in[o], od_conv_w[o], od_conv_b[o], od_dt_bias[o], od_a_log[o], od_d[o],
                      od_norm_w[o], od_w_out[o])
            xp, st = block(xp, mods_p, norm_w[l], ffn_w_in[l], ffn_w_out[l], odd_mixer, params, zero_odd)
            xs, _ = block(xs, mods_s, norm_w[l], ffn_w_in[l], ffn_w_out[l], odd_mixer, params,
                          state_ssd[:, o].astype(F32))
            od_states.append(st)
    y_prompt = rms_norm(xp, final_norm_w)
    y_sample = rms_norm(xs, final_norm_w)
    new_mlstm_c = jnp.stack([s[0] for s in ev_states], 1).astype(out_dtype)
    new_mlstm_n = jnp.stack([s[1] for s in ev_states], 1).astype(out_dtype)
    new_mlstm_m = jnp.stack([s[2] for s in ev_states], 1).astype(out_dtype)
    new_rwkv = jnp.stack([s[3] for s in ev_states], 1).astype(out_dtype)
    new_ssd = jnp.stack(od_states, 1).astype(out_dtype)
    return (y_prompt, y_sample, new_mlstm_c, new_mlstm_n, new_mlstm_m, new_rwkv, new_ssd)


_drawn_inputs = setup_inputs


def setup_inputs(seed=0):
    import zlib

    import numpy as np

    out = dict(_drawn_inputs(seed))
    spreads = {}
    factors = {'state_mlstm_c': 5.244,
     'state_mlstm_n': 8.0,
     'state_mlstm_m': 8.0,
     'state_rwkv': 8.0,
     'ev_a_norm_w': 8.0,
     'ev_b_w_up': 7.264,
     'ev_b_ln_w': 8.0,
     'ev_b_ln_b': 8.0,
     'od_d': 4.354,
     'od_norm_w': 8.0}
    for name, (base, spread) in spreads.items():
        noise = np.random.default_rng([zlib.crc32(name.encode()), seed]).standard_normal(out[name].shape)
        drawn = base * np.exp(spread * noise) if base else spread * noise
        out[name] = __import__('jax').numpy.asarray(drawn.astype(out[name].dtype))
    for name, factor in factors.items():
        out[name] = (out[name] * factor).astype(out[name].dtype)
    return out
```

```python
from contextlib import ExitStack, contextmanager

import concourse.bass as bass
from concourse import mybir

ALU = mybir.AluOpType
ACT = mybir.ActivationFunctionType
AX_X = mybir.AxisListType.X
F32 = mybir.dt.float32

P = 128
DM = 1024
KD = DM // P
LATN, CTXN = 512, 128
T = LATN + CTXN
LAT, CTX = slice(0, LATN), slice(LATN, T)
PAD = 644
PLAT, PCTX = slice(1, 1 + LATN), slice(LATN + 2, LATN + 2 + CTXN)
NCH = T // P
CT = NCH - 1
AH = 4
FFN = 2816
KF = FFN // P
CI = 2048
KC = CI // P
NG = 8
EPS = 1e-6
LN_EPS = 64e-5
DECAY = 0.606531
R64 = 64


def chunk(c):
    return slice(c * P, (c + 1) * P)


def pchunk(c):
    a = 1 + c * P if c < CT else PCTX.start
    return slice(a, a + P)


def p64(c):
    a = 1 + c * R64 if c < 8 else PCTX.start + (c - 8) * R64
    return slice(a, a + R64)


C_ID, C_ONE, C_UP, C_LO, C_BLK = 0, 128, 256, 384, 512
C_LVL = 640
C_MK = C_LVL + 2 * 6 * 64
C_I64 = C_MK + 2 * 2 * 64
C_RST = C_I64 + 64
C_POSR = C_RST + T
C_POSC = C_POSR + 4 * 8
NCONST = C_POSC + 4 * 64

V_MODB, V_NORM = 0, 96
V_CW, V_CB, V_AN, V_MU, V_W0, V_A0, V_KK, V_KA, V_U, V_LW, V_LB, V_FIN = (
    128, 152, 160, 164, 179, 187, 191, 195, 199, 207, 211, 215)
V_OCW, V_OCB = 256, 352
V_ONW, V_C, V_N = 384, 400, 416
NVT = 4


class Count:

    def __init__(self, eng, sem, n=0):
        self.eng, self.sem, self.n, self.turn = eng, sem, n, 0

    def next(self, by=1):
        self.n += by
        self.eng.wait_ge(self.sem, self.turn + self.n)

    def done(self, ins):
        ins.then_inc(self.sem, 1)
        self.next()


@contextmanager
def turns(eng, n, counts):
    start = [c.n for c, _ in counts]
    with eng.Fori(0, n) as i:
        for c, per in counts:
            c.turn = i * per
        yield i
    for (c, per), s in zip(counts, start):
        assert c.n - s == per, (c.sem, c.n - s, per)
        c.n, c.turn = s + n * per, 0


def build(nc, a, outs):
    with ExitStack() as ctx:
        _build(ctx, nc, a, outs)


def _build(ctx, nc, a, outs):
    V, A, E = nc.vector, nc.scalar, nc.tensor

    def sb(name, shape):
        return ctx.enter_context(nc.sbuf_tensor(name, shape, F32))

    def sem(name):
        return ctx.enter_context(nc.semaphore(name))

    const = sb("const", [P, NCONST])
    ident, ones = const[:, C_ID:C_ID + P], const[:, C_ONE:C_ONE + P]
    upper, lower = const[:, C_UP:C_UP + P], const[:, C_LO:C_LO + P]
    blk = const[:, C_BLK:C_BLK + P]
    lvl = const[:, C_LVL:C_MK].rearrange("p (d l t) -> p d l t", d=2, l=6)
    mk = const[:, C_MK:C_I64].rearrange("p (d m t) -> p d m t", d=2, m=2)
    i64 = const[:, C_I64:C_RST]
    rst = const[:, C_RST:C_POSR]
    posr = const[:, C_POSR:C_POSC].rearrange("p (f r) -> p f r", f=4)
    posc = const[:, C_POSC:NCONST].rearrange("p (f r) -> p f r", f=4)
    vec = sb("vec", [P, NVT * P])
    mod = sb("mod", [P, 96, 2])
    x = sb("x", [P, KD, T])
    ring = sb("ring", [P, 4, KD, P])
    amp = sb("amp", [P, KD, 2])
    rstd = sb("rstd", [P, T])
    small = sb("small", [P, 16])
    cs_T = sb("cs_T", [P, KD, 2])
    dsk = sb("dsk", [P, KC])
    NAR = 39000
    arena = sb("arena", [P, NAR])
    top = [0]

    def take(*shape):
        n = 1
        for s in shape:
            n *= s
        v = arena[:, top[0]:top[0] + n]
        top[0] += n
        assert top[0] <= NAR, top[0]
        if len(shape) == 2:
            v = v.rearrange("p (a b) -> p a b", a=shape[0])
        elif len(shape) == 3:
            v = v.rearrange("p (a b c) -> p a b c", a=shape[0], b=shape[1])
        elif len(shape) == 4:
            v = v.rearrange("p (a b c d) -> p a b c d", a=shape[0], b=shape[1], c=shape[2])
        return v

    bank = ctx.enter_context(nc.psum_tensor("bank", [P, 8, 512], F32))
    pair = [bank[:, 0:2, :].rearrange("p b n -> p (b n)"), bank[:, 2:4, :].rearrange("p b n -> p (b n)")]
    pairs = pair + [bank[:, 4:6, :].rearrange("p b n -> p (b n)"), bank[:, 6:8, :].rearrange("p b n -> p (b n)")]

    w_ready = [sem(f"w_ready{s}") for s in range(4)]
    unit_done = sem("unit_done")
    psum_free = [sem(f"psum_free{s}") for s in range(2)]
    act_chain, dve_chain = sem("act_chain"), sem("dve_chain")
    at_end = {e: sem(f"{e}_stage_end") for e in ("pe", "act", "dve")}
    loaded, stored = sem("loaded"), sem("stored")
    stage_no = {"pe": 0, "act": 0, "dve": 0}
    eng_of = {}
    la, lv = Count(None, act_chain), Count(None, dve_chain)

    def fence(me):
        eng = eng_of[me]
        eng.drain().then_inc(at_end[me], 1)
        stage_no[me] += 1
        for e in at_end:
            eng.wait_ge(at_end[e], stage_no[me])

    nloads = [0]

    def load(dst, src):
        eng_of["act"].dma_start(dst, src).then_inc(loaded, 16)
        nloads[0] += 1

    nstores = [0]

    def store(dst, src):
        eng_of["act"].dma_start(dst, src).then_inc(stored, 16)
        nstores[0] += 1

    stages = []
    unit0, out0 = [0], [0]

    def fetch(sp, s, q, src, kt, cols):
        sp.wait_ge(unit_done, q * 4 + s + 1)
        sp.dma_start(ring[:, s, 0:kt, 0:cols], src).then_inc(w_ready[s], 16)

    def unit(s, q, pr, v, rhs, kt, m=P, first=True, last=True):
        pe = eng_of["pe"]
        pe.wait_ge(w_ready[s], q * 16 + 16)
        if first:
            pe.wait_ge(psum_free[pr], v + 1)
        for k in range(kt):
            st, en = first and k == 0, last and k == kt - 1
            E.matmul(pair[pr][0:m, 0:LATN], ring[:, s, k, 0:m], rhs[:, k, LAT], start=st, stop=en)
            mm = E.matmul(pair[pr][0:m, LATN:T], ring[:, s, k, 0:m], rhs[:, k, CTX], start=st, stop=en)
        mm.then_inc(unit_done, 1)

    def unit_wait(eng, q, s):
        eng.wait_ge(unit_done, q * 4 + s + 1 + 4)

    def stage_load():
        rows = take(NVT, P)
        xin = take(NCH, DM)
        d_all = take(2 * KC)
        vt_s, x_s, c_s = sem("vectors_transposed"), sem("x_transposed"), sem("bank_copied")
        cs = take(2, 2, 8)

        def act(act):
            load(const[:, :], a["consts"])
            act.wait_ge(c_s, 1)

            def put(row, src, n):
                t, r = row // P, row % P
                load(rows[r:r + n, t, :], src)
            put(V_MODB, a["mod_b"].rearrange("l (r c) -> (l r) c", c=P), 96)
            put(V_NORM, a["norm_w"].rearrange("l j (r c) -> (l j r) c", c=P), 32)
            put(V_CW, a["ev_a_conv_w"].rearrange("e w (r c) -> (e w r) c", c=P), 24)
            put(V_CB, a["ev_a_conv_b"].rearrange("e (r c) -> (e r) c", c=P), 8)
            put(V_AN, a["ev_a_norm_w"].rearrange("e (r c) -> (e r) c", c=P), 4)
            put(V_MU, a["ev_b_mu"][0, 0:13 * P].rearrange("(r c) -> r c", c=P), 13)
            put(V_MU + 13, a["ev_b_mu"][0, 13 * P + 64:14 * P + 64].rearrange("(r c) -> r c", c=P), 1)
            load(rows[(V_MU + 14) % P:(V_MU + 14) % P + 1, 1, 0:64],
                 a["ev_b_mu"][0, 13 * P:13 * P + 64].rearrange("(r c) -> r c", c=64))
            put(V_W0, a["ev_b_w0"].rearrange("e d (r c) -> (e d r) c", c=P), 8)
            for v, n in ((V_A0, "ev_b_a0"), (V_KK, "ev_b_k_k"), (V_KA, "ev_b_k_a"), (V_LW, "ev_b_ln_w"), (V_LB, "ev_b_ln_b")):
                put(v, a[n].rearrange("e (r c) -> (e r) c", c=P), 4)
            put(V_U, a["ev_b_u"].rearrange("e d (r c) -> (e d r) c", c=P), 8)
            put(V_FIN, a["final_norm_w"].rearrange("(r c) -> r c", c=P), 8)
            put(V_OCW, a["od_conv_w"].rearrange("e w (r c) -> (e w r) c", c=P), 96)
            put(V_OCB, a["od_conv_b"].rearrange("e (r c) -> (e r) c", c=P), 32)
            put(V_ONW, a["od_norm_w"].rearrange("e (r c) -> (e r) c", c=P), 16)
            put(V_C, a["c_ctx"].rearrange("(r c) -> r c", c=P), 8)
            put(V_C + 8, a["c"].rearrange("b (r c) -> (b r) c", c=P), 8)
            put(V_N, a["state_mlstm_n"].rearrange("b e d h k -> (b e d h) k"), 8)
            load(xin[:, 0:4, :], a["x_sample"].rearrange("b (c p) f -> p (b c) f", p=P))
            load(xin[:, 4, :], a["x_prompt"].rearrange("b p f -> p (b f)"))
            load(small[0:16, 0:1], a["ev_a_gate_b"].rearrange("e t d h -> (e t d h)").rearrange("(r c) -> r c", c=1))
            load(small[0:64, 1:2], a["od_dt_bias"].rearrange("e d h -> (e d h)").rearrange("(r c) -> r c", c=1))
            load(small[0:64, 2:3], a["od_a_log"].rearrange("e d h -> (e d h)").rearrange("(r c) -> r c", c=1))
            load(small[:, 3:11], a["state_mlstm_m"].rearrange("b e d h -> (b e d h)").partition_broadcast(P))
            load(d_all, a["od_d"][0].partition_broadcast(P))
            act.wait_ge(loaded, 16 * nloads[0])
            for e in range(2):
                A.activation(dsk[64 * e:64 * e + 64, :], d_all[64 * e:64 * e + 64, e::2], ACT.Copy)
            act.wait_ge(c_s, 2)
            for s in range(2):
                la.done(A.activation(cs_T[:, :, s], vec[:, V_C + 8 * s:V_C + 8 * s + 8], ACT.Silu))

        def dve(dve):
            V.memset(rows[:, :, :], 0.0).then_inc(c_s, 1)
            dve.wait_ge(vt_s, 1)
            V.tensor_copy(vec[:, :], bank[:, 4, :]).then_inc(c_s, 1)
            lv.done(V.memset(rstd[:, :], 0.0))
            for f in range(KD):
                pr = pairs[f % 2]
                dve.wait_ge(x_s, f + 1)
                if f < 4:
                    pos = posr[:, f, :].unsqueeze(2).to_broadcast([P, 8, 64])
                else:
                    pos = posc[:, f - 4, :].unsqueeze(1).to_broadcast([P, 8, 64])
                V.tensor_tensor(x[:, f, LAT].rearrange("p (r c) -> p r c", r=8),
                                pr[:, LAT].rearrange("p (r c) -> p r c", r=8), pos, ALU.add)
                V.tensor_copy(x[:, f, CTX], pr[:, CTX]).then_inc(c_s, 1)

        def pe(pe):
            pe.wait_ge(c_s, 1)
            pe.wait_ge(loaded, 16 * nloads[0])
            for t in range(NVT):
                mm = E.transpose(bank[:, 4, t * P:(t + 1) * P], rows[:, t, :], ident)
            mm.then_inc(vt_s, 1)
            for f in range(KD):
                if f >= 2:
                    pe.wait_ge(c_s, f + 1)
                for c in range(NCH):
                    mm = E.transpose(pairs[f % 2][:, c * P:(c + 1) * P], xin[:, c, f * P:(f + 1) * P], ident)
                mm.then_inc(x_s, 1)

        return pe, act, dve


    def stage_mod():
        mod_s = sem("mod_copied")
        u0, v0 = unit0[0], out0[0]
        unit0[0] += 96
        out0[0] += 24

        def fetches(sp):
            for l in range(2):
                w = a["mod_w"][l, :, :].rearrange("(k p) n -> p k n", p=P)
                with sp.Fori(0, 12) as i:
                    for s in range(4):
                        fetch(sp, s, i + (u0 // 4 + 12 * l), w[:, :, bass.ds(i * (4 * P) + s * P, P)], KD, P)

        def pe(pe):
            with pe.Fori(0, 12) as i:
                for o in range(2):
                    pe.wait_ge(psum_free[o], i + (v0 // 2 + 1))
                    for s in range(4):
                        pe.wait_ge(w_ready[s], i * 32 + (u0 // 4 + o) * 16 + 16)
                        for k in range(KD):
                            mm = E.matmul(pair[o][:, 2 * s:2 * s + 2], ring[:, s, k, :], cs_T[:, k, :],
                                          start=(k == 0), stop=(k == KD - 1))
                        mm.then_inc(unit_done, 1)

        def act(act):
            with turns(act, 12, []) as i:
                for o in range(2):
                    act.wait_ge(unit_done, i * 8 + (u0 + 4 * o + 4 + 4))
                    A.activation(mod[:, bass.ds(i * 8 + 4 * o, 4), :], pair[o][:, 0:8].rearrange("p (n s) -> p n s", s=2),
                                 ACT.Copy).then_inc(psum_free[o], 1)
            act.drain().then_inc(mod_s, 1)

        def dve(dve):
            dve.wait_ge(mod_s, 1)
            lv.done(V.tensor_tensor(mod[:, :, :], mod[:, :, :],
                                    vec[:, V_MODB:V_MODB + 96].unsqueeze(2).to_broadcast([P, 96, 2]), ALU.add))

        return pe, act, dve, fetches

    def col(v, n=1):
        return vec[:, v:v + n]

    def stage_norm(src, dst, kt, scale_at, weight, shift_at, name):
        sq_s, ss_s, m_s, rt_s, h_s = (sem(f"{name}_{n}") for n in ("squares", "sum", "mean", "root", "scaled"))
        sq = dst if kt == KD else take(2, T)
        ring2 = 0 if kt == KD else 2

        def act(act):
            for k in range(kt):
                if ring2 and k >= 2:
                    act.wait_ge(ss_s, k - 1)
                A.activation(sq[:, k % 2 if ring2 else k, :], src[:, k, :], ACT.Square).then_inc(sq_s, 1)
            act.wait_ge(m_s, 1)
            la.done(A.activation(rstd[:, :], rstd[:, :], ACT.Sqrt))
            act.sem_inc(rt_s, 1)
            if shift_at is not None:
                for k in range(kt):
                    act.wait_ge(h_s, k + 1)
                    for s, c in ((1, LAT), (0, CTX)):
                        A.activation(dst[:, k, c], dst[:, k, c], ACT.Identity,
                                     bias=mod[:, shift_at + k, s:s + 1])

        def pe(pe):
            for k in range(kt):
                pe.wait_ge(sq_s, k + 1)
                q = sq[:, k % 2 if ring2 else k, :]
                E.matmul(pairs[2][:, LAT], ones, q[:, LAT], start=(k == 0), stop=(k == kt - 1))
                E.matmul(pairs[2][:, CTX], ones, q[:, CTX], start=(k == 0), stop=(k == kt - 1)).then_inc(ss_s, 1)

        def dve(dve):
            if scale_at is not None:
                lv.done(V.scalar_tensor_tensor(amp[:, :, :], mod[:, scale_at:scale_at + KD, :], 1.0,
                                               weight.unsqueeze(2).to_broadcast([P, KD, 2]), ALU.add, ALU.mult))
            dve.wait_ge(ss_s, kt)
            lv.done(V.tensor_scalar(rstd[:, :], pairs[2][:, 0:T], 1.0 / (kt * P), EPS, ALU.mult, ALU.add))
            dve.sem_inc(m_s, 1)
            dve.wait_ge(rt_s, 1)
            lv.done(V.reciprocal(rstd[:, :], rstd[:, :]))
            for k in range(kt):
                if scale_at is not None:
                    for s, c in ((1, LAT), (0, CTX)):
                        ins = V.scalar_tensor_tensor(dst[:, k, c], src[:, k, c], amp[:, k, s:s + 1], rstd[:, c],
                                                     ALU.mult, ALU.mult)
                else:
                    ins = V.scalar_tensor_tensor(dst[:, k, :], src[:, k, :], weight[:, k:k + 1], rstd[:, :],
                                                 ALU.mult, ALU.mult)
                ins.then_inc(h_s, 1)

        return pe, act, dve

    def stage_even_in(h, qk, vo, pb, gates):
        gate_s = sem("gates_done")
        u0, v0 = unit0[0], out0[0]
        unit0[0] += 32
        out0[0] += 32
        w = a["ev_w_in"][0].rearrange("(k p) n -> p k n", p=P)
        loops = ((4, 0), (3, 4 * AH * P + 16))
        last = ((3600, P), (3792, P), (3728, 64), (2048, 16))

        def fetches(sp):
            q = u0 // 4
            for n, c0 in loops:
                with sp.Fori(0, n) as i:
                    for s in range(4):
                        fetch(sp, s, i + q, w[:, :, bass.ds(i * (4 * P) + (c0 + s * P), P)], KD, P)
                q += n
            for s, (c, m) in enumerate(last):
                fetch(sp, s, q, w[:, :, c:c + m], KD, m)

        def pe(pe):
            q, v = u0 // 4, v0 // 2
            for n, _ in loops:
                with pe.Fori(0, n) as i:
                    for s in range(4):
                        unit(s, i + q, s % 2, i * 2 + (v + s // 2), h, KD)
                q, v = q + n, v + 2 * n
            for s, (_, m) in enumerate(last):
                unit(s, q, s % 2, v + s // 2, h, KD, m)

        def act(act):
            q = u0 // 4
            def evac(i, q, s, tile, dst, padded):
                unit_wait(act, i + q, s)
                if padded:
                    A.activation(dst[:, tile, PLAT], pair[s % 2][:, LAT], ACT.Copy)
                    A.activation(dst[:, tile, PCTX], pair[s % 2][:, CTX], ACT.Copy).then_inc(psum_free[s % 2], 1)
                else:
                    A.activation(dst[:, tile, :], pair[s % 2][:, 0:T], ACT.Copy).then_inc(psum_free[s % 2], 1)
            one = lambda e: bass.ds(e, 1)
            for dst, padded in ((qk, True), (vo, False)):
                with turns(act, 2, []) as i:
                    for s in range(4):
                        evac(i, q, s, one(i * 4 + s), dst, padded)
                q += 2
            with turns(act, 3, []) as i:
                for s in range(4):
                    evac(i, q, s, one(i * 4 + s), pb, True)
            q += 3
            for s, t in ((0, 12), (1, 13)):
                evac(0, q, s, t, pb, True)
            unit_wait(act, q, 2)
            A.activation(pb[0:64, 14, PLAT], pair[0][0:64, LAT], ACT.Copy)
            A.activation(pb[0:64, 14, PCTX], pair[0][0:64, CTX], ACT.Copy).then_inc(psum_free[0], 1)
            unit_wait(act, q, 3)
            A.activation(gates[0:16, :], pair[1][0:16, 0:T], ACT.Copy).then_inc(psum_free[1], 1)

        def dve(dve):
            for buf in (qk, pb):
                for c in (slice(0, 1), slice(LATN + 1, LATN + 2), slice(PCTX.stop, PAD)):
                    lv.done(V.memset(buf[:, :, c], 0.0))
            lv.done(V.memset(pb[64:128, 14, :], 0.0))

        return pe, act, dve, fetches

    def conv(buf, k, tmp, w0, w1, w2, b):
        lv.done(V.tensor_scalar(tmp[:, 1:643], buf[:, k, 1:643], w1, b, ALU.mult, ALU.add))
        lv.done(V.scalar_tensor_tensor(tmp[:, 1:643], buf[:, k, 0:642], w0, tmp[:, 1:643], ALU.mult, ALU.add))
        lv.done(V.scalar_tensor_tensor(tmp[:, 1:643], buf[:, k, 2:644], w2, tmp[:, 1:643], ALU.mult, ALU.add))

    def stage_conv(qk, vo, pb):
        cv_s, si_s, g_s = sem("convolved"), sem("silu_done"), sem("scaled_k")
        tmp = take(4, PAD)
        mu = take(2, 16)

        def act(act):
            for k in range(8):
                act.wait_ge(cv_s, k + 1)
                A.activation(qk[:, k, PLAT], tmp[:, k % 2, PLAT], ACT.Silu)
                A.activation(qk[:, k, PCTX], tmp[:, k % 2, PCTX], ACT.Silu).then_inc(si_s, 1)
            A.activation(vo[:, 4:8, :], vo[:, 4:8, :], ACT.Sigmoid)
            act.wait_ge(si_s, 8)
            A.mul(qk[:, 4:8, PLAT], qk[:, 4:8, PLAT], P ** -0.5)
            A.mul(qk[:, 4:8, PCTX], qk[:, 4:8, PCTX], P ** -0.5)

        def dve(dve):
            for k in range(8):
                if k >= 2:
                    dve.wait_ge(si_s, k - 1)
                conv(qk, k, tmp[:, k % 2], col(V_CW + k), col(V_CW + 8 + k), col(V_CW + 16 + k), col(V_CB + k))
                dve.sem_inc(cv_s, 1)
            lv.done(V.tensor_scalar(mu[:, 0, 0:15], vec[:, V_MU:V_MU + 15], -1.0, 1.0, ALU.mult, ALU.add))
            lv.done(V.tensor_scalar(mu[:, 1, 0:15], vec[:, V_MU:V_MU + 15], 0.5, None, ALU.mult))
            for k in range(15):
                t = tmp[:, 2 + k % 2, 1:643]
                lv.done(V.tensor_tensor(t, pb[:, k, 0:642], pb[:, k, 2:644], ALU.add))
                lv.done(V.tensor_scalar(pb[:, k, 1:643], pb[:, k, 1:643], mu[:, 0, k:k + 1], None, ALU.mult))
                lv.done(V.scalar_tensor_tensor(pb[:, k, 1:643], t, mu[:, 1, k:k + 1], pb[:, k, 1:643],
                                               ALU.mult, ALU.add))

        return (lambda pe: None), act, dve

    def stage_mlstm(qk, vo, gates, ha, out_c, out_n, out_m):
        gl_s, ga_s, tp_s, tc_s = sem("g_abs"), sem("g_ln"), sem("gate_products"), sem("gate_copies")
        both = take(4, 4, P)
        work = both.rearrange("p a h t -> p (a h t)")[:, 0:3 * T].rearrange("p (a t) -> p a t", a=3)
        em, qw, kw, nd = (both[:, n] for n in range(4))
        gt, lt = take(NCH, 16), take(NCH, 16)
        bcol, acol, ecol, tot = (take(2, NCH, 4) for _ in range(4))
        mloc = take(2)
        dg = take(2, 20)
        ml, ms, me, dec, sc, wcol, tt = (take(2, NCH, 4) for _ in range(7))
        arow, brow, rrow, morow = (take(2, P) for _ in range(4))
        msrow = take(2)
        ktok, vtok = take(NCH, 4, P), take(NCH, 4, P + 1)
        Cst = take(2, 4, P + 1)
        ctmp = take(4, P + 1)
        tmp, wi = take(4, P), take(4, P)
        ee = pt = tmp
        nout = take(8)
        noutT = take(P)
        f2 = lambda v: v.rearrange("p d c h -> p d (c h)")
        fl = lambda v: v.rearrange("p h t -> p (h t)")
        kv_s, kvc_s = sem("kv_turned"), sem("kv_copied")
        r_s, n_s, c_s = sem("r_rows_spread"), sem("num_den"), sem("c_local")
        rd_s, p_s, kw_s, st_s, e_s = (sem(f"ml_{n}") for n in
                                       ("arg", "weights", "kw", "state", "exp"))
        ex_s, no_s, q_s = sem("m_exp"), sem("n_rows"), sem("ml_spread_free")
        st_l, co_s = sem("states_in"), sem("n_turned")
        ctxs = [(CT, d, None) for d in range(2)]
        order = ctxs + [(c if d == 0 else CT - 1 - c, d, c) for c in range(CT) for d in range(2)]

        def act(act):
            act.wait_ge(gl_s, 1)
            la.done(A.activation(work[0:16, 0, :], work[0:16, 0, :], ACT.Exp, scale=-1.0))
            la.done(A.activation(work[0:16, 0, :], work[0:16, 0, :], ACT.Ln, bias=1.0))
            act.sem_inc(ga_s, 1)
            act.wait_ge(ex_s, 1)
            for v in (dec, sc, wcol):
                last = A.activation(v[:, :, :, :], v[:, :, :, :], ACT.Exp)
            last.then_inc(ga_s, 1)
            for n, (c, d, k) in enumerate(order):
                if n:
                    act.wait_ge(st_s, n)
                act.wait_ge(rd_s, n + 1)
                for h in range(4):
                    A.activation(wi[:, h, :], bank[:, 0, h * P:(h + 1) * P], ACT.Exp,
                                 bias=ms[:, d, c, h:h + 1], scale=-1.0)
                A.activation(fl(em), bank[:, 1, :], ACT.Exp, scale=-1.0).then_inc(q_s, 1)
                A.activation(fl(ee), fl(tmp), ACT.Exp, scale=-1.0).then_inc(e_s, 1)
                if n == 1:
                    act.wait_ge(st_s, 2)
                    for dd in range(2):
                        store(out_c[0, 0, dd].rearrange("h k v -> k h v"), Cst[:, dd, :, 0:P])
                    for dd in range(2):
                        store(out_m[0, 0, dd:dd + 1, :], me[0:1, dd, CT, :])
                    act.wait_ge(no_s, 1)
                    store(out_n[0, 0].rearrange("d h k -> (d h) k"), noutT[0:8, :])
                    act.wait_ge(stored, 16 * nstores[0])
                    for dd in range(2):
                        act.dma_start(Cst[:, dd, :, 0:P], a["state_mlstm_c"][0, 0, dd].rearrange("h k v -> k h v")
                                      ).then_inc(st_l, 16)

        def pe(pe):
            g = Count(pe, tc_s)
            g.next()
            for c in range(NCH):
                E.transpose(bank[:, 4, c * 16:(c + 1) * 16], gates[0:16, chunk(c)], ident[0:16, 0:16])
                mm = E.transpose(bank[:, 5, c * 16:(c + 1) * 16], work[0:16, 1, chunk(c)], ident[0:16, 0:16])
            mm.then_inc(tp_s, 1)
            g.next()
            E.matmul(bank[:, 6, 0:20], upper, lt[:, :, 8:12], start=True, stop=True)
            E.matmul(bank[:, 6, 20:40], lower, lt[:, :, 12:16], start=True, stop=True)
            E.matmul(bank[:, 7, 0:40], ones, lt[:, :, 8:16], start=True, stop=True).then_inc(tp_s, 1)
            g.next()
            for d in range(2):
                for n, v in enumerate((ecol, acol, bcol)):
                    mm = E.transpose(bank[0:20, (4, 5, 6)[n], d * P:(d + 1) * P], f2(v)[:, d, :], ident)
            mm.then_inc(tp_s, 1)
            g.next()
            for d in range(2):
                mm = E.matmul(bank[:, 7, d * 20:(d + 1) * 20], ones[0:20, :], dg[0:20, d, :], start=True, stop=True)
            mm.then_inc(tp_s, 1)
            g.next()
            for d in range(2):
                mm = E.matmul(bank[0:20, 4, d:d + 1], f2(ms)[0:1, d, :], ones[0:1, 0:1], start=True, stop=True)
            mm.then_inc(tp_s, 1)
            for c in range(NCH):
                for n, (buf, t0, cols) in enumerate(((qk, 4, pchunk(c)), (vo, 0, chunk(c)))):
                    if 2 * c + n >= 2:
                        pe.wait_ge(kvc_s, 2 * c + n - 1)
                    for h in range(4):
                        mm = E.transpose(bank[:, n, h * P:(h + 1) * P], buf[:, t0 + h, cols], ident)
                    mm.then_inc(kv_s, 1)
            pe.wait_ge(kvc_s, 2 * NCH)
            g.next()
            for n, (c, d, k) in enumerate(order):
                if n:
                    pe.wait_ge(rd_s, n)
                    pe.wait_ge(q_s, n)
                for b, rows in ((0, rrow), (1, morow)):
                    for h in range(4):
                        sel = ident[0:20, c * 4 + h:c * 4 + h + 1].to_broadcast([20, P])
                        mm = E.matmul(bank[:, b, h * P:(h + 1) * P], sel, rows[0:20, d, :], start=True, stop=True)
                mm.then_inc(r_s, 1)
                if n:
                    pe.wait_ge(p_s, n)
                for h in range(4):
                    mm = E.matmul(bank[:, 2, h * P:(h + 1) * P], qk[:, 4 + h, pchunk(c)], qk[:, h, pchunk(c)],
                                  start=True, stop=True)
                pe.wait_ge(kw_s, n + 1)
                for h in range(4):
                    mm = E.matmul(bank[:, 5 + h // 2, (h % 2) * (P + 1):(h % 2 + 1) * (P + 1)], kw[:, h, :],
                                  vtok[:, c, h, :], start=True, stop=True)
                mm.then_inc(c_s, 1)
                pe.wait_ge(p_s, n + 1)
                for h in range(4):
                    E.matmul(bank[:, 3, h * P:(h + 1) * P], vtok[:, c, h, 0:P], pt[:, h, :], start=True, stop=False)
                    E.matmul(bank[:, 3, h * P:(h + 1) * P], Cst[:, d, h, 0:P], qw[:, h, :], start=False, stop=True)
                for h in range(4):
                    E.matmul(bank[:, 4, h * P:(h + 1) * P], ones, pt[:, h, :], start=True, stop=False)
                    mm = E.matmul(bank[:, 4, h * P:(h + 1) * P], Cst[:, d, h, P:P + 1].to_broadcast([P, P]), qw[:, h, :],
                                  start=False, stop=True)
                mm.then_inc(n_s, 1)
                if n == 1:
                    pe.wait_ge(co_s, 1)
                    E.transpose(bank[0:8, 7, 0:P], nout, ident).then_inc(kv_s, 1)

        def dve(dve):
            lv.done(V.tensor_scalar(gates[0:16, :], gates[0:16, :], small[0:16, 0:1], None, ALU.add))
            lv.done(V.tensor_scalar(work[0:16, 2, :], gates[0:16, :], -1.0, None, ALU.mult))
            lv.done(V.tensor_tensor(work[0:16, 0, :], work[0:16, 2, :], gates[0:16, :], ALU.max))
            dve.sem_inc(gl_s, 1)
            lv.done(V.tensor_scalar(work[0:16, 1, :], gates[0:16, :], 0.0, None, ALU.min))
            dve.wait_ge(ga_s, 1)
            lv.done(V.tensor_tensor(work[0:16, 1, :], work[0:16, 1, :], work[0:16, 0, :], ALU.subtract))
            dve.sem_inc(tc_s, 1)
            dve.wait_ge(tp_s, 1)
            lv.done(V.tensor_copy(gt[:, :, :], bank[:, 4, 0:80].rearrange("p (c r) -> p c r", r=16)))
            lv.done(V.tensor_copy(lt[:, :, :], bank[:, 5, 0:80].rearrange("p (c r) -> p c r", r=16)))
            dve.sem_inc(tc_s, 1)
            dve.wait_ge(tp_s, 2)
            lv.done(V.tensor_copy(f2(bcol), bank[:, 6, 0:40].rearrange("p (d x) -> p d x", d=2)))
            for d in range(2):
                lv.done(V.tensor_copy(tot[:, d, :, :], bank[:, 7, 0:40].rearrange("p (c r) -> p c r", r=8)[:, :, 4 * d:4 * d + 4]))
                lv.done(V.tensor_tensor(acol[:, d, :, :], gt[:, :, 4 * d:4 * d + 4], bcol[:, d, :, :], ALU.subtract))
            lv.done(V.tensor_tensor(f2(ecol), f2(acol), f2(tot), ALU.add))
            dve.sem_inc(tc_s, 1)
            dve.wait_ge(tp_s, 3)
            r2 = lambda b: bank[0:20, b, 0:2 * P].rearrange("p (d t) -> p d t", d=2)
            lv.done(V.tensor_copy(arow[0:20], r2(5)))
            lv.done(V.tensor_copy(brow[0:20], r2(6)))
            lv.done(V.tensor_reduce(mloc[0:20, :], r2(4), AX_X, ALU.max))
            for d in range(2):
                lv.done(V.tensor_scalar(dg[0:20, d, :], ident[0:20, 0:20], mloc[0:20, d:d + 1], None, ALU.mult))
            dve.sem_inc(tc_s, 1)
            dve.wait_ge(tp_s, 4)
            lv.done(V.tensor_copy(f2(ml), bank[:, 7, 0:40].rearrange("p (d x) -> p d x", d=2)))
            lv.done(V.memset(ms[:, :, CT, :], 0.0))
            for d in range(2):
                lv.done(V.tensor_copy(ms[:, d, 0 if d == 0 else CT - 1, :], small[:, 3 + 4 * d:7 + 4 * d]))
            for d in range(2):
                cs = [CT] + (list(range(CT)) if d == 0 else list(range(CT - 1, -1, -1)))
                for n, c in enumerate(cs):
                    lv.done(V.tensor_tensor(tt[:, d, c, :], tot[:, d, c, :], ms[:, d, c, :], ALU.add))
                    lv.done(V.tensor_tensor(me[:, d, c, :], tt[:, d, c, :], ml[:, d, c, :], ALU.max))
                    if 0 < n < CT:
                        lv.done(V.tensor_copy(ms[:, d, cs[n + 1], :], me[:, d, c, :]))
            dve.sem_inc(tc_s, 1)
            lv.done(V.tensor_tensor(f2(dec), f2(tt), f2(me), ALU.subtract))
            lv.done(V.tensor_tensor(f2(sc), f2(ml), f2(me), ALU.subtract))
            lv.done(V.tensor_tensor(f2(wcol), f2(ecol), f2(ml), ALU.subtract))
            dve.sem_inc(ex_s, 1)
            dve.wait_ge(tp_s, 5)
            lv.done(V.tensor_copy(msrow[0:20, :], bank[0:20, 4, 0:2]))
            lv.done(V.tensor_tensor_scan(rrow[0:20, 0, :], arow[0:20, 0, :], arow[0:20, 0, :], msrow[0:20, 0:1],
                                         ALU.max, ALU.max))
            lv.done(V.tensor_tensor_scan(rrow[0:20, 1, ::-1], arow[0:20, 1, ::-1], arow[0:20, 1, ::-1],
                                         msrow[0:20, 1:2], ALU.max, ALU.max))
            lv.done(V.tensor_tensor(morow[0:20], brow[0:20], rrow[0:20], ALU.add))
            lv.done(V.memset(vtok[:, :, :, P:P + 1], 1.0))
            for c in range(NCH):
                for n, buf in enumerate((ktok, vtok)):
                    dve.wait_ge(kv_s, 2 * c + n + 1)
                    V.tensor_copy(buf[:, c, :, 0:P], bank[:, n, :].rearrange("p (h t) -> p h t", h=4)).then_inc(kvc_s, 1)
            lv.done(V.memset(Cst[:, :, :, :], 0.0))
            dve.wait_ge(ga_s, 2)
            dve.sem_inc(tc_s, 1)
            hb = lambda b: bank[:, b, :].rearrange("p (h t) -> p h t", h=4)
            mask = (upper, lower)
            for n, (c, d, k) in enumerate(order):
                lv.done(V.tensor_tensor(kw[:, :, :], ktok[:, c, :, :], wcol[:, d, c, :].unsqueeze(2).to_broadcast([P, 4, P]),
                                        ALU.mult))
                dve.sem_inc(kw_s, 1)
                dve.wait_ge(r_s, n + 1)
                if n:
                    dve.wait_ge(e_s, n)
                for h in range(4):
                    ins = V.tensor_scalar(tmp[:, h, :], bank[:, 0, h * P:(h + 1) * P], acol[:, d, c, h:h + 1], 0.0,
                                          ALU.subtract, ALU.max)
                ins.then_inc(rd_s, 1)
                dve.wait_ge(q_s, n + 1)
                lv.done(V.tensor_tensor(qw[:, :, :], qk[:, 0:4, pchunk(c)], wi[:, :, :], ALU.mult))
                dve.wait_ge(e_s, n + 1)
                lv.done(V.tensor_tensor(ee[:, :, :], ee[:, :, :], mask[d].unsqueeze(1).to_broadcast([P, 4, P]), ALU.mult))
                dve.wait_ge(c_s, n + 1)
                if n == 2:
                    dve.wait_ge(st_l, 32)
                lv.done(V.tensor_tensor(pt[:, :, :], ee[:, :, :], hb(2), ALU.mult))
                dve.sem_inc(p_s, 1)
                dve.wait_ge(n_s, n + 1)
                lv.done(V.tensor_scalar(nd[:, :, :], hb(4), -1.0, None, ALU.mult))
                lv.done(V.tensor_tensor(nd[:, :, :], nd[:, :, :], hb(4), ALU.max))
                lv.done(V.tensor_tensor(nd[:, :, :], nd[:, :, :], em[:, :, :], ALU.max))
                lv.done(V.reciprocal(nd[:, :, :], nd[:, :, :]))
                tgt = ha[:, :, chunk(c)]
                if (c, d) in seen_first(order):
                    lv.done(V.tensor_tensor(tgt, nd[:, :, :], hb(3), ALU.mult))
                else:
                    lv.done(V.tensor_tensor(nd[:, :, :], nd[:, :, :], hb(3), ALU.mult))
                    lv.done(V.tensor_tensor(tgt, tgt, nd[:, :, :], ALU.add))
                b4 = lambda v: v[:, d, c, :].unsqueeze(2).to_broadcast([P, 4, P + 1])
                for hh in range(2):
                    lv.done(V.tensor_tensor(ctmp[:, 2 * hh:2 * hh + 2, :],
                                            bank[:, 5 + hh, 0:2 * (P + 1)].rearrange("p (h t) -> p h t", h=2),
                                            sc[:, d, c, 2 * hh:2 * hh + 2].unsqueeze(2).to_broadcast([P, 2, P + 1]), ALU.mult))
                lv.done(V.tensor_tensor(Cst[:, d], Cst[:, d], b4(dec), ALU.mult))
                lv.done(V.tensor_tensor(Cst[:, d], Cst[:, d], ctmp[:, :, :], ALU.add))
                dve.sem_inc(st_s, 1)
                if n == 1:
                    for dd in range(2):
                        lv.done(V.tensor_copy(nout[:, 4 * dd:4 * dd + 4], Cst[:, dd, :, P]))
                    dve.sem_inc(co_s, 1)
                    dve.wait_ge(kv_s, 2 * NCH + 1)
                    lv.done(V.tensor_copy(noutT[0:8, :], bank[0:8, 7, 0:P]))
                    dve.sem_inc(no_s, 1)
                    dve.wait_ge(st_l, 32)
                    for dd in range(2):
                        lv.done(V.tensor_copy(Cst[:, dd, :, P], vec[:, V_N + 4 * dd:V_N + 4 * dd + 4]))

        return pe, act, dve

    def seen_first(order):
        out, seen = set(), set()
        for c, d, _ in order:
            if c not in seen:
                seen.add(c)
                out.add((c, d))
        return out

    def stage_head_norm(y, onesm, n, eps, weight, bias, name, finish):
        s_s, x_s, v_s, r_s = (sem(f"{name}_{k}") for k in ("sum", "centred", "var", "root"))
        sq, rs = take(T), take(T)

        def pe(pe):
            for j in range(4):
                if j:
                    pe.wait_ge(x_s, 2 * j)
                for c in (LAT, CTX):
                    mm = E.matmul(pairs[0][:, c], onesm, y[:, j, c], start=True, stop=True)
                mm.then_inc(s_s, 1)
                pe.wait_ge(x_s, 2 * j + 1)
                for c in (LAT, CTX):
                    mm = E.matmul(pairs[1][:, c], onesm, sq[:, c], start=True, stop=True)
                mm.then_inc(v_s, 1)

        def act(act):
            for j in range(4):
                act.wait_ge(x_s, 2 * j + 2)
                A.activation(rs, rs, ACT.Sqrt).then_inc(r_s, 1)

        def dve(dve):
            for j in range(4):
                t = y[:, j, :]
                dve.wait_ge(s_s, j + 1)
                lv.done(V.scalar_tensor_tensor(t, pairs[0][:, 0:T], -1.0 / n, t, ALU.mult, ALU.add))
                lv.done(V.tensor_tensor(sq, t, t, ALU.mult))
                dve.sem_inc(x_s, 1)
                dve.wait_ge(v_s, j + 1)
                lv.done(V.tensor_scalar(rs, pairs[1][:, 0:T], 1.0 / n, eps, ALU.mult, ALU.add))
                dve.sem_inc(x_s, 1)
                dve.wait_ge(r_s, j + 1)
                lv.done(V.reciprocal(rs, rs))
                lv.done(V.scalar_tensor_tensor(t, t, weight[:, j:j + 1], rs, ALU.mult, ALU.mult))
                if bias is not None:
                    lv.done(V.tensor_scalar(t, t, bias[:, j:j + 1], None, ALU.add))
                finish(dve, j)

        return pe, act, dve

    def finish_mlstm(ha, vo):
        return lambda dve, j: lv.done(V.tensor_tensor(ha[:, j, :], ha[:, j, :], vo[:, 4 + j, :], ALU.mult))

    def stage_rwkv_in(pb, kk, av, ld, cum):
        wup, aup = take(512), take(512)
        tmp = take(2, T)
        p_s, c_s, n_s, t_s, l_s = (sem(f"ri_{k}") for k in ("products", "copied", "norm", "exp", "weights"))
        pad2 = ((LAT, PLAT), (CTX, PCTX))

        def act(act):
            act.dma_start(wup, a["ev_b_w_up"][0].rearrange("d r n -> (d r) n")).then_inc(l_s, 16)
            act.dma_start(aup[0:64, :], a["ev_b_a_up"][0]).then_inc(l_s, 16)
            A.activation(pb[:, 12, 1:643], pb[:, 12, 1:643], ACT.Tanh)
            A.activation(pb[:, 13, 1:643], pb[:, 13, 1:643], ACT.Sigmoid).then_inc(t_s, 1)
            n = 0
            for j in range(4):
                for kind in range(3):
                    act.wait_ge(p_s, n + 1)
                    src = pair[n % 2][:, 0:T]
                    if kind == 0:
                        ins = A.activation(av[:, j, :], src, ACT.Sigmoid, bias=col(V_A0 + j))
                    else:
                        ins = A.activation(ld[:, kind - 1, j, :], src, ACT.Sigmoid, bias=col(V_W0 + 4 * (kind - 1) + j))
                    ins.then_inc(c_s, 1)
                    n += 1
            for j in range(4):
                act.wait_ge(n_s, 2 * j + 2)
                A.activation(tmp[:, 1, :], tmp[:, 1, :], ACT.Sqrt).then_inc(t_s, 1)

        def pe(pe):
            pe.wait_ge(l_s, 32)
            pe.wait_ge(t_s, 1)
            n = 0
            for j in range(4):
                for kind in range(3):
                    if n >= 2:
                        pe.wait_ge(c_s, n - 1)
                    w = (aup[0:64], wup[0:64], wup[64:128])[kind][:, j * P:(j + 1) * P]
                    r = (pb[0:64, 14], pb[0:64, 12], pb[64:128, 12])[kind]
                    for c, pc in pad2:
                        mm = E.matmul(pair[n % 2][:, c], w, r[:, pc], start=True, stop=True)
                    mm.then_inc(p_s, 1)
                    n += 1
            for j in range(4):
                pe.wait_ge(n_s, 2 * j + 1)
                for c in (LAT, CTX):
                    mm = E.matmul(pairs[2][:, c], blk, tmp[:, 0, c], start=True, stop=True)
                mm.then_inc(p_s, 1)

        def dve(dve):
            for j in range(4):
                for c, pc in pad2:
                    lv.done(V.tensor_scalar(kk[:, j, c], pb[:, 4 + j, pc], col(V_KK + j), None, ALU.mult))
                lv.done(V.tensor_tensor(tmp[:, 0, :], kk[:, j, :], kk[:, j, :], ALU.mult))
                dve.sem_inc(n_s, 1)
                dve.wait_ge(p_s, 12 + j + 1)
                lv.done(V.tensor_copy(tmp[:, 1, :], pairs[2][:, 0:T]))
                dve.sem_inc(n_s, 1)
                dve.wait_ge(t_s, j + 2)
                lv.done(V.tensor_scalar(tmp[:, 1, :], tmp[:, 1, :], 1e-12, None, ALU.max))
                lv.done(V.reciprocal(tmp[:, 1, :], tmp[:, 1, :]))
                lv.done(V.tensor_tensor(kk[:, j, :], kk[:, j, :], tmp[:, 1, :], ALU.mult))
            dve.wait_ge(c_s, 12)
            for j in range(4):
                lv.done(V.tensor_scalar(tmp[:, 0, :], av[:, j, :], -1.0, col(V_KA + j), ALU.add, ALU.mult))
                for c, pc in pad2:
                    lv.done(V.scalar_tensor_tensor(pb[:, 4 + j, pc], tmp[:, 0, c], 1.0, pb[:, 4 + j, pc],
                                                   ALU.add, ALU.mult))
                lv.done(V.tensor_tensor(av[:, j, :], av[:, j, :], kk[:, j, :], ALU.mult))
                for d in range(2):
                    lv.done(V.tensor_scalar(ld[:, d, j, :], ld[:, d, j, :], -DECAY, None, ALU.mult))
                    lv.done(V.tensor_tensor_scan(cum[:, d, j, :], rst, ld[:, d, j, :], 0.0, ALU.mult, ALU.add))
                c64 = lambda v: v[:, 1, j, :].rearrange("p (c t) -> p c t", t=R64)
                end = c64(cum)[:, :, R64 - 1:R64]
                lv.done(V.tensor_copy(tmp[:, 0, 0:10].unsqueeze(2), end))
                lv.done(V.tensor_tensor(cum[:, 1, j, :], ld[:, 1, j, :], cum[:, 1, j, :], ALU.subtract))
                lv.done(V.tensor_tensor(c64(cum), c64(cum), tmp[:, 0, 0:10].unsqueeze(2).to_broadcast([P, 10, R64]), ALU.add))
                for d in range(2):
                    lv.done(V.tensor_tensor(ld[:, d, j, :], cum[:, d, j, :], ld[:, d, j, :], ALU.subtract))

        return pe, act, dve

    def stage_rwkv(pb, kk, av, ex, cum, y, out_s):
        pri = take(2, 4, 3 * R64)
        bb, kb = take(2, 4, R64), take(2, 4, R64)
        e4 = lambda v: v.rearrange("p (d j t) -> p d j t", d=2, j=4)
        e1, e2, e3 = e4(pb[:, 12, 0:512]), e4(pb[:, 14, 0:512]), e4(rstd[:, 0:512])
        gb, gk = take(2, 4, 3 * R64), take(2, 4, 3 * R64)
        vt = take(2, 4, R64)
        et = take(2, 4, R64)
        M, MT, W = (take(2, 4, R64) for _ in range(3))
        Z, U = W, et
        S = take(2, 4, R64)
        dend = take(2, 4)
        sin = pri[:, :, :, 0:R64]
        ex_s, x_s, g_s, gc_s = sem("rw_exp"), sem("rw_factors"), sem("rw_grams"), sem("rw_grams_copied")
        lw_s, lc_s, sq_s, sc_s = sem("rw_level"), sem("rw_level_copied"), sem("rw_seq"), sem("rw_seq_copied")
        fr_s, ld_s, io_s = sem("rw_factors_free"), sem("rw_state_in"), sem("rw_state_turned")
        hp = (slice(0, 64), slice(64, 128))
        dj = [(d, j) for d in range(2) for j in range(4)]
        flat = lambda v: v.rearrange("p d j t -> p (d j t)")
        gcol = lambda b0, d, j: bank[:, b0 + (d * 4 + j) // 2, ((d * 4 + j) % 2) * 192:((d * 4 + j) % 2) * 192 + 192]
        steps = [(8, 9)] + [(9, 8)] + [(k, 7 - k) for k in range(8)]
        NP = 4

        def small_products(out, lhs, rhs, dd, start=True, stop=True, acc=None):
            for d, j in dd:
                for h in hp:
                    mm = E.matmul(out[h, d, j, :], lhs[h, d, j, :], rhs[h, d, j, :], start=start, stop=stop)
            return mm

        b8 = lambda b: bank[:, b, :].rearrange("p (d j t) -> p d j t", d=2, j=4)

        def act(act):
            for dd in range(2):
                for e in range(2):
                    act.dma_start(sin[e * 64:e * 64 + 64, dd], a["state_rwkv"][0, 0, dd].rearrange(
                        "(j e) v k -> e v j k", e=2)[e]).then_inc(ld_s, 16)
            for n, cc in enumerate(steps):
                if n:
                    act.wait_ge(x_s, n)
                for d in range(2):
                    t = slice(cc[d] * R64, cc[d] * R64 + R64)
                    A.activation(e1[:, d], ex[:, d, :, t], ACT.Exp)
                    A.activation(e2[:, d], cum[:, d, :, t], ACT.Exp)
                    ins = A.activation(e3[:, d], cum[:, d, :, t], ACT.Exp, scale=-1.0)
                ins.then_inc(ex_s, 1)
                if n == 1:
                    act.wait_ge(sc_s, 4 * 2 + 2)
                    for dd in range(2):
                        for e in range(2):
                            store(out_s[0, 0, dd].rearrange("(j e) v k -> e v j k", e=2)[e],
                                  U[e * 64:e * 64 + 64, dd])
                    act.wait_ge(stored, 16 * nstores[0])
                    act.sem_inc(ld_s, 1)

        def pe(pe):
            pe.wait_ge(ld_s, 64)
            for d, j in dj:
                for h in hp:
                    mm = E.matmul(b8(7)[h, d, j, :], sin[h, d, j, :], i64[h, :], start=True, stop=True)
            mm.then_inc(io_s, 1)
            pe.wait_ge(sc_s, 1)
            lw, lc = 0, 0
            for n, cc in enumerate(steps):
                pe.wait_ge(x_s, n + 1)
                for d, j in dj:
                    for h in hp:
                        mm = E.matmul(gcol(0, d, j)[h], bb[h, d, j, :], pri[h, d, j, :], start=True, stop=True)
                mm.then_inc(g_s, 1)
                pe.wait_ge(gc_s, 3 * n + 1)
                pe.wait_ge(lc_s, 17 * n + 1)
                small_products(b8(4), et, M, dj).then_inc(lw_s, 1)
                for d, j in dj:
                    for h in hp:
                        mm = E.matmul(gcol(0, d, j)[h], kb[h, d, j, :], pri[h, d, j, :], start=True, stop=True)
                mm.then_inc(g_s, 1)
                for d, j in dj:
                    for h in hp:
                        mm = E.matmul(b8(7)[h, d, j, :], pb[h, 8 + j, p64(cc[d])], i64[h, :], start=True, stop=True)
                mm.then_inc(g_s, 1)
                for l in range(1, 6):
                    pe.wait_ge(lc_s, 17 * n + 2 + 3 * (l - 1))
                    small_products(b8(4), et, M, dj).then_inc(lw_s, 1)
                    pe.wait_ge(lc_s, 17 * n + 3 + 3 * (l - 1))
                    if l < 5:
                        small_products(b8(5), MT, W, dj)
                    small_products(b8(6), W, MT, dj).then_inc(lw_s, 1)
                pe.wait_ge(lc_s, 17 * n + 17)
                pe.wait_ge(gc_s, 3 * n + 3)
                for d, j in dj:
                    for h in hp:
                        E.matmul(b8(0)[h, d, j, :], pri[h, d, j, 0:64], S[h, d, j, :], start=True, stop=False)
                        mm = E.matmul(b8(0)[h, d, j, :], gk[h, d, j, 0:64], vt[h, d, j, :], start=False, stop=True)
                mm.then_inc(sq_s, 1)
                pe.wait_ge(sc_s, 4 * n + 2 + (n > 1))
                small_products(b8(1), MT, Z, dj).then_inc(sq_s, 1)
                pe.wait_ge(sc_s, 4 * n + 3 + (n > 1))
                for d, j in dj:
                    for h in hp:
                        o = b8(2)[h, d, j, :]
                        E.matmul(o, gk[h, d, j, 128:192], vt[h, d, j, :], start=True, stop=False)
                        mm = E.matmul(o, gb[h, d, j, 128:192], U[h, d, j, :], start=False, stop=True)
                mm.then_inc(sq_s, 1)
                for d, j in dj:
                    for h in hp:
                        o = b8(3)[h, d, j, :]
                        E.matmul(o, S[h, d, j, :], pri[h, d, j, 64:128], start=True, stop=False)
                        E.matmul(o, vt[h, d, j, :], gk[h, d, j, 64:128], start=False, stop=False)
                        mm = E.matmul(o, U[h, d, j, :], gb[h, d, j, 64:128], start=False, stop=True)
                mm.then_inc(sq_s, 1)
                pe.wait_ge(sc_s, 4 * n + 5 + (n > 1))
                if n == 1:
                    for d, j in dj:
                        for h in hp:
                            mm = E.matmul(b8(0)[h, d, j, :], S[h, d, j, :], i64[h, :], start=True, stop=True)
                    mm.then_inc(io_s, 1)
                    pe.wait_ge(sc_s, 4 * 2 + 2)

        def dve(dve):
            dve.wait_ge(io_s, 1)
            S0 = sav = take_saved[0]
            lv.done(V.tensor_copy(flat(sav), bank[:, 7, :]))
            lv.done(V.memset(flat(S), 0.0))
            for d in range(2):
                lv.done(V.tensor_copy(pri[:, d, :, 128:192], i64.unsqueeze(1).to_broadcast([P, 4, R64])))
            dve.sem_inc(sc_s, 1)
            seen = set()
            extra = 0
            for n, cc in enumerate(steps):
                dve.wait_ge(ex_s, n + 1)
                for d in range(2):
                    t = slice(cc[d] * R64, cc[d] * R64 + R64)
                    tp = p64(cc[d])
                    lv.done(V.tensor_tensor(pri[:, d, :, 0:64], e1[:, d], kk[:, :, t], ALU.mult))
                    lv.done(V.tensor_tensor(pri[:, d, :, 64:128], e2[:, d], pb[:, 0:4, tp], ALU.mult))
                    lv.done(V.tensor_tensor(bb[:, d], e3[:, d], av[:, :, t], ALU.mult))
                    lv.done(V.tensor_tensor(kb[:, d], e3[:, d], pb[:, 4:8, tp], ALU.mult))
                    e = R64 - 1 if d == 0 else 0
                    lv.done(V.tensor_copy(dend[:, d, :].unsqueeze(2), e2[:, d, :, e:e + 1]))
                dve.sem_inc(x_s, 1)
                dve.wait_ge(g_s, 3 * n + 1)
                def grams(dst, n):
                    for d in range(2):
                        for half in range(2):
                            src = bank[:, d * 2 + half, 0:384].rearrange("p (j m t) -> p j m t", j=2, m=3)
                            for m in range(2):
                                lv.done(V.tensor_tensor(
                                    dst[:, d, 2 * half:2 * half + 2, m * 64:m * 64 + 64], src[:, :, m, :],
                                    mk[:, d, m, :].unsqueeze(1).to_broadcast([P, 2, R64]), ALU.mult))
                            lv.done(V.tensor_copy(dst[:, d, 2 * half:2 * half + 2, 128:192], src[:, :, 2, :]))
                grams(gb, n)
                dve.sem_inc(gc_s, 1)
                def level(l):
                    for d in range(2):
                        lv.done(V.tensor_tensor(et[:, d], gb[:, d, :, 0:64],
                                                lvl[:, d, l, :].unsqueeze(1).to_broadcast([P, 4, R64]), ALU.mult))
                ib = i64.unsqueeze(1).to_broadcast([P, 8, R64])
                f8 = lambda v: v.rearrange("p d j t -> p (d j) t")
                level(0)
                lv.done(V.tensor_copy(f8(M), ib))
                dve.sem_inc(lc_s, 1)
                lv.done(V.tensor_tensor(f8(MT), f8(M), f8(et), ALU.subtract))
                dve.wait_ge(lw_s, 11 * n + 1)
                lv.done(V.tensor_tensor(flat(M), flat(M), bank[:, 4, :], ALU.subtract))
                for l in range(1, 6):
                    level(l)
                    dve.sem_inc(lc_s, 1)
                    if l == 1:
                        dve.wait_ge(g_s, 3 * n + 2)
                        grams(gk, n)
                        dve.sem_inc(gc_s, 1)
                        dve.wait_ge(g_s, 3 * n + 3)
                        lv.done(V.tensor_copy(flat(vt), bank[:, 7, :]))
                        dve.sem_inc(gc_s, 1)
                    dve.wait_ge(lw_s, 11 * n + 2 * l)
                    lv.done(V.tensor_copy(flat(W), bank[:, 4, :]))
                    dve.sem_inc(lc_s, 1)
                    dve.wait_ge(lw_s, 11 * n + 2 * l + 1)
                    if l < 5:
                        lv.done(V.tensor_tensor(flat(M), flat(M), bank[:, 5, :], ALU.subtract))
                    lv.done(V.tensor_tensor(flat(MT), flat(MT), bank[:, 6, :], ALU.subtract))
                    dve.sem_inc(lc_s, 1)
                dve.sem_inc(lc_s, 1)
                dve.wait_ge(sq_s, 4 * n + 1)
                lv.done(V.tensor_copy(flat(Z), bank[:, 0, :]))
                dve.sem_inc(sc_s, 1)
                dve.wait_ge(sq_s, 4 * n + 2)
                lv.done(V.tensor_scalar(flat(U), bank[:, 1, :], -1.0, None, ALU.mult))
                dve.sem_inc(sc_s, 1)
                dve.wait_ge(sq_s, 4 * n + 4)
                for d in range(2):
                    t = slice(cc[d] * R64, cc[d] * R64 + R64)
                    src = b8(3)[:, d]
                    if cc[d] in seen:
                        lv.done(V.tensor_tensor(y[:, :, t], y[:, :, t], src, ALU.add))
                    else:
                        lv.done(V.tensor_copy(y[:, :, t], src))
                        seen.add(cc[d])
                dve.sem_inc(sc_s, 1)
                lv.done(V.tensor_tensor(flat(S), flat(S), bank[:, 2, :], ALU.add))
                lv.done(V.tensor_tensor(f8(S), f8(S), dend.rearrange("p d j -> p (d j)").unsqueeze(2)
                                        .to_broadcast([P, 8, R64]), ALU.mult))
                dve.sem_inc(sc_s, 1)
                if n == 1:
                    dve.wait_ge(io_s, 2)
                    lv.done(V.tensor_copy(flat(U), bank[:, 0, :]))
                    lv.done(V.tensor_copy(flat(S), flat(sav)))
                    dve.sem_inc(sc_s, 1)
                    dve.wait_ge(ld_s, 65)

        return pe, act, dve

    take_saved = [sb("rwkv_saved", [P, 2, 4, R64])]

    def stage_rwkv_out(pb, y):
        gup, u, tmp, t2 = take(512), take(4), take(2, PAD), take(T)
        l_s, t_s, p_s, d_s = (sem(f"ro_{k}") for k in ("weights", "products_in", "products", "read"))

        def act(act):
            act.dma_start(gup, a["ev_b_g_up"][0]).then_inc(l_s, 16)

        def pe(pe):
            pe.wait_ge(l_s, 16)
            for j in range(4):
                if j:
                    pe.wait_ge(d_s, j)
                pe.wait_ge(t_s, j + 1)
                for c, pc in ((LAT, PLAT), (CTX, PCTX)):
                    E.matmul(pairs[0][:, c], blk, tmp[:, j % 2, pc], start=True, stop=True)
                    mm = E.matmul(pairs[1][:, c], gup[:, j * P:(j + 1) * P], pb[:, 13, pc], start=True, stop=True)
                mm.then_inc(p_s, 1)

        def dve(dve):
            lv.done(V.tensor_tensor(u, vec[:, V_U:V_U + 4], vec[:, V_U + 4:V_U + 8], ALU.add))
            for j in range(4):
                w = tmp[:, j % 2, 1:643]
                lv.done(V.tensor_scalar(w, pb[:, j, 1:643], u[:, j:j + 1], None, ALU.mult))
                lv.done(V.tensor_tensor(w, w, pb[:, 4 + j, 1:643], ALU.mult))
                dve.sem_inc(t_s, 1)
                dve.wait_ge(p_s, j + 1)
                for c, pc in ((LAT, PLAT), (CTX, PCTX)):
                    lv.done(V.tensor_tensor(t2[:, c], pb[:, 8 + j, pc], pairs[0][:, c], ALU.mult))
                lv.done(V.tensor_tensor(y[:, j, :], y[:, j, :], t2, ALU.add))
                lv.done(V.tensor_tensor(y[:, j, :], y[:, j, :], pairs[1][:, 0:T], ALU.mult))
                dve.sem_inc(d_s, 1)

        return pe, act, dve

    def stage_out(rhs, w, split, gate_at):
        per = {1: 4, 2: 2, 3: 4}[len(split)]
        nu = per * len(split)
        u0, v0 = unit0[0], out0[0]
        unit0[0] += 8 * len(split)
        out0[0] += 8
        wv = w.rearrange("(k p) n -> p k n", p=P)
        k0 = [sum(split[:n]) for n in range(len(split))]

        def fetches(sp):
            with sp.Fori(0, 8 // per) as i:
                for n in range(nu):
                    o, m = n // len(split), n % len(split)
                    fetch(sp, n % 4, i * (nu // 4) + (u0 // 4 + n // 4),
                          wv[:, k0[m]:k0[m] + split[m], bass.ds(i * (per * P) + o * P, P)], split[m], P)

        def pe(pe):
            with pe.Fori(0, 8 // per) as i:
                for n in range(nu):
                    o, m = n // len(split), n % len(split)
                    unit(n % 4, i * (nu // 4) + (u0 // 4 + n // 4), o % 2, i * (per // 2) + (v0 // 2 + o // 2),
                         rhs[:, k0[m]:k0[m] + split[m], :], split[m], P, m == 0, m == len(split) - 1)

        def dve(dve):
            with turns(dve, 8 // per, []) as i:
                for o in range(per):
                    n = o * len(split) + len(split) - 1
                    unit_wait(dve, i * (nu // 4) + (u0 // 4 + n // 4), n % 4)
                    for s, c in ((1, LAT), (0, CTX)):
                        xt = x[:, bass.ds(i * per + o, 1), c].rearrange("p o t -> p (o t)")
                        g = mod[:, bass.ds(i * per + (gate_at + o), 1), s:s + 1].rearrange("p o t -> p (o t)")
                        ins = V.scalar_tensor_tensor(xt, pair[o % 2][:, c], g, xt, ALU.mult, ALU.add)
                    ins.then_inc(psum_free[o % 2], 1)

        return pe, (lambda act: None), dve, fetches

    def stage_ffn_in(h, hid, w, name):
        gs = take(2, T)
        g_s, f_s = sem(f"{name}_gate_silu"), sem(f"{name}_hidden")
        u0, v0 = unit0[0], out0[0]
        unit0[0] += 2 * KF
        out0[0] += 2 * KF
        wv = w.rearrange("(k p) n -> p k n", p=P)

        def fetches(sp):
            with sp.Fori(0, KF // 2) as i:
                for s in range(4):
                    fetch(sp, s, i + u0 // 4, wv[:, :, bass.ds(i * (2 * P) + ((s // 2) * P + (s % 2) * FFN), P)], KD, P)

        def pe(pe):
            with pe.Fori(0, KF // 2) as i:
                for s in range(4):
                    unit(s, i + u0 // 4, s % 2, i * 2 + (v0 // 2 + s // 2), h, KD)

        def act(act):
            with turns(act, KF // 2, []) as i:
                for m in range(2):
                    unit_wait(act, i + u0 // 4, 2 * m)
                    act.wait_ge(f_s, i * 2 + (m + 1))
                    A.activation(gs[:, m, :], pair[0][:, 0:T], ACT.Silu).then_inc(psum_free[0], 1)
                    act.drain().then_inc(g_s, 1)

        def dve(dve):
            dve.sem_inc(f_s, 2)
            with turns(dve, KF // 2, []) as i:
                for m in range(2):
                    unit_wait(dve, i + u0 // 4, 2 * m + 1)
                    dve.wait_ge(g_s, i * 2 + (m + 1))
                    t = hid[:, bass.ds(i * 2 + m, 1), :].rearrange("p o t -> p (o t)")
                    V.tensor_tensor(t, gs[:, m, :], pair[1][:, 0:T], ALU.mult).then_inc(psum_free[1], 1)
                    dve.drain().then_inc(f_s, 1)

        return pe, act, dve, fetches

    def log1p(u, z, q, acc):
        lv.done(V.tensor_scalar(z, u, 2.0, None, ALU.add))
        lv.done(V.reciprocal(z, z))
        lv.done(V.tensor_tensor(z, z, u, ALU.mult))
        lv.done(V.tensor_tensor(q, z, z, ALU.mult))
        lv.done(V.tensor_scalar(acc, q, 1.0 / 17, None, ALU.mult))
        for n in range(15, 1, -2):
            lv.done(V.scalar_tensor_tensor(acc, acc, 1.0 / n, q, ALU.add, ALU.mult))
        lv.done(V.scalar_tensor_tensor(acc, acc, 1.0, z, ALU.add, ALU.mult))
        lv.done(V.tensor_scalar(acc, acc, 2.0, None, ALU.mult))

    def stage_dt(h, dtc, cumc, dece, cdec, scratch):
        wd = take(KD, 64)
        r = take(6, T)
        crow = take(T)
        dac = take(NCH, 64)
        tot = take(NCH, 64)
        l_s, p_s, v_s, e_s = (sem(f"dt_{k}") for k in ("weights", "products", "steps", "exp"))

        def act(act):
            act.dma_start(wd[:, :, :], a["od_w_in"][0].rearrange("(k p) n -> p k n", p=P)[:, :, 6144:6208]).then_inc(l_s, 16)
            A.activation(small[0:64, 11:12], small[0:64, 2:3], ACT.Exp)
            act.wait_ge(v_s, 1)
            A.activation(r[0:64, 1, :], r[0:64, 1, :], ACT.Exp, scale=-1.0).then_inc(e_s, 1)
            act.wait_ge(v_s, 4)
            act.dma_start(scratch[:, :], crow[0:64, :]).then_inc(l_s, 16)
            act.wait_ge(v_s, 5)
            A.activation(dece[:, :, :], dece[:, :, :], ACT.Exp)
            A.activation(cdec[:, :, :], tot[:, :, :], ACT.Exp)
            act.wait_ge(l_s, 32)

        def pe(pe):
            pe.wait_ge(l_s, 16)
            for k in range(KD):
                E.matmul(pairs[0][0:64, LAT], wd[:, k, :], h[:, k, LAT], start=(k == 0), stop=(k == KD - 1))
                mm = E.matmul(pairs[0][0:64, CTX], wd[:, k, :], h[:, k, CTX], start=(k == 0), stop=(k == KD - 1))
            mm.then_inc(p_s, 1)
            pe.wait_ge(v_s, 2)
            for c in range(NCH):
                E.transpose(bank[:, 2, c * 64:(c + 1) * 64], r[0:64, 0, chunk(c)], ident[0:64, 0:64])
                mm = E.transpose(bank[:, 3, c * 64:(c + 1) * 64], r[0:64, 2, chunk(c)], ident[0:64, 0:64])
            mm.then_inc(p_s, 1)
            pe.wait_ge(v_s, 3)
            for c in range(NCH):
                for d, tri in enumerate((upper, lower)):
                    mm = E.matmul(pairs[2][32 * d:32 * d + 32, chunk(c)], dac[:, c, 32 * d:32 * d + 32], tri, start=True, stop=True)
            E.matmul(bank[:, 6, 0:320], ones, dac.rearrange("p c r -> p (c r)"), start=True, stop=True).then_inc(p_s, 1)
            pe.wait_ge(v_s, 4)
            for c in range(NCH):
                mm = E.transpose(bank[:, 7, c * 64:(c + 1) * 64], crow[0:64, chunk(c)], ident[0:64, 0:64])
            mm.then_inc(p_s, 1)

        def dve(dve):
            R = lambda n: r[0:64, n, :]
            dve.wait_ge(p_s, 1)
            lv.done(V.tensor_scalar(R(0), pairs[0][0:64, 0:T], small[0:64, 1:2], None, ALU.add))
            lv.done(V.tensor_scalar(R(1), R(0), -1.0, None, ALU.mult))
            lv.done(V.tensor_tensor(R(1), R(1), R(0), ALU.max))
            dve.sem_inc(v_s, 1)
            dve.wait_ge(e_s, 1)
            log1p(R(1), R(3), R(4), R(5))
            lv.done(V.scalar_tensor_tensor(R(0), R(0), 0.0, R(5), ALU.max, ALU.add))
            lv.done(V.tensor_scalar(R(2), R(0), small[0:64, 11:12], -1.0, ALU.mult, ALU.mult))
            dve.sem_inc(v_s, 1)
            dve.wait_ge(p_s, 2)
            c5 = lambda b: bank[:, b, 0:320].rearrange("p (c r) -> p c r", r=64)
            lv.done(V.tensor_copy(dtc[:, :, :], c5(2)))
            lv.done(V.tensor_copy(dac[:, :, :], c5(3)))
            dve.sem_inc(v_s, 1)
            dve.wait_ge(p_s, 3)
            lv.done(V.tensor_copy(crow[0:64, :], pairs[2][0:64, 0:T]))
            lv.done(V.tensor_copy(tot[:, :, :], c5(6)))
            dve.sem_inc(v_s, 1)
            dve.wait_ge(p_s, 4)
            lv.done(V.tensor_copy(cumc[:, :, :], c5(7)))
            lv.done(V.tensor_tensor(dece[:, :, :], tot[:, :, :], cumc[:, :, :], ALU.subtract))
            dve.sem_inc(v_s, 1)

        return pe, act, dve

    def stage_ssd(h, yb, dtc, cumc, dece, cdec, scratch, dsk, out_s):
        raw = take(4, PAD)
        tmp = take(2, PAD)
        zb = take(2, T)
        xc = take(4, T)
        xt = take(NCH, 3 * P)
        cumb = take(2, 4, T)
        arg, ec = take(4, P), take(4, P)
        ee, cw = arg, ec
        dx, dxw = take(4, 64), take(4, 64)
        cbm = take(2, P)
        S = take(2, 256)
        sin = take(2, 2, P)
        so = take(2, 2, P)
        s0 = take(2, 256)
        names = ("cum_in", "state_in", "raw", "convolved", "silu", "turned", "turned_copied", "arg", "exp",
                 "weighted", "products", "used", "dx", "state_free", "state_turned", "state_copied", "state_out", "group_end", "cb")
        (ci_s, si_s, rw_s, cv_s, sl_s, tu_s, tc_s, ar_s, ex_s, wt_s, pr_s, us_s, dx_s, sf_s, st_s, sc_s, so_s, ge_s, cb_s) = (
            sem(f"ssd_{n}") for n in names)
        u0, v0 = unit0[0], out0[0]
        unit0[0] += 48
        out0[0] += 48
        w = a["od_w_in"][0].rearrange("(k p) n -> p k n", p=P)
        order = [(CT, 0), (CT, 1)] + [(c if d == 0 else CT - 1 - c, d) for c in range(CT) for d in range(2)]
        NS = len(order)
        first = set()
        seen = set()
        for c, d in order:
            if c not in seen:
                seen.add(c)
                first.add((c, d))
        cols = [[(256 * j + 0, 512), (256 * j + 128, 512), (2048 + 256 * j, 512), (2048 + 256 * j + 128, 512),
                 (4096 + 128 * j, 256), (5120 + 128 * j, 256)] for j in range(2)]

        def fetches(sp):
            with sp.Fori(0, 4) as i:
                for n in range(12):
                    b, st = cols[n // 6][n % 6]
                    fetch(sp, n % 4, i * 3 + (u0 // 4 + n // 4), w[:, :, bass.ds(i * st + b, P)], KD, P)

        def hs(v, i, j, c, d):
            return v[:, c, bass.ds(i * 8 + (32 * d + 4 * j), 4)]

        def act(act):
            cs_d = scratch.rearrange("(d g h) t -> d g (h t)", d=2, g=NG)
            st_d = a["state_ssd"][0, 0].rearrange("d (g a e) p n -> d g (e p) a n", g=NG, a=2)
            so_d = out_s[0, 0].rearrange("d (g a e) p n -> d g (e p) a n", g=NG, a=2)
            act.sem_inc(so_s, 16 * 2)
            uw = lambda i, n: unit_wait(act, i * 3 + (u0 // 4 + n // 4), n % 4)
            with turns(act, 4, []) as i:
                for j in range(2):
                    act.wait_ge(ge_s, i * 2 + (j + 1))
                    for d in range(2):
                        act.dma_start(cumb[:, d, :, :].rearrange("p h t -> p (h t)"),
                                      cs_d[d, bass.ds(i * 2 + j, 1), :].rearrange("g x -> (g x)").partition_broadcast(P)).then_inc(ci_s, 16)
                        act.dma_start(sin[:, d, :, :],
                                      st_d[d, bass.ds(i * 2 + j, 1), :, :, :].rearrange("g q a n -> q (g a) n")
                                      ).then_inc(si_s, 16)
                    for m in range(6):
                        n = 6 * j + m
                        uw(i, n)
                        src = pair[n % 2]
                        if m < 2:
                            A.activation(zb[:, m, :], src[:, 0:T], ACT.Silu).then_inc(psum_free[n % 2], 1)
                        else:
                            A.activation(raw[:, m - 2, PLAT], src[:, LAT], ACT.Copy)
                            A.activation(raw[:, m - 2, PCTX], src[:, CTX], ACT.Copy).then_inc(psum_free[n % 2], 1)
                            act.drain().then_inc(rw_s, 1)
                    for m in range(4):
                        act.wait_ge(cv_s, i * 8 + (4 * j + m + 1))
                        A.activation(xc[:, m, LAT], tmp[:, m % 2, PLAT], ACT.Silu)
                        A.activation(xc[:, m, CTX], tmp[:, m % 2, PCTX], ACT.Silu).then_inc(sl_s, 1)
                    act.wait_ge(ci_s, i * 64 + (32 * j + 32))
                    for n, (c, d) in enumerate(order):
                        if n:
                            act.wait_ge(pr_s, i * (2 * NS) + (NS * j + n))
                        A.activation(ec[:, :, :], cumb[:, d, :, chunk(c)], ACT.Exp)
                        act.wait_ge(ar_s, i * (2 * NS) + (NS * j + n + 1))
                        A.activation(ee[:, :, :], arg[:, :, :], ACT.Exp).then_inc(ex_s, 1)
                        if n == 1:
                            act.wait_ge(sc_s, i * 4 + (2 * j + 2))
                            for dd in range(2):
                                act.dma_start(so_d[dd, bass.ds(i * 2 + j, 1), :, :, :].rearrange("g q a n -> q (g a) n"),
                                              so[:, dd, :, :]).then_inc(so_s, 16)

        def pe(pe):
            with pe.Fori(0, 4) as i:
                for j in range(2):
                    for m in range(6):
                        n = 6 * j + m
                        unit(n % 4, i * 3 + (u0 // 4 + n // 4), n % 2, i * 6 + (v0 // 2 + n // 2), h, KD)
                    pe.wait_ge(si_s, i * 64 + (32 * j + 32))
                    for d in range(2):
                        for t in range(2):
                            mm = E.transpose(bank[:, 7, (2 * d + t) * P:(2 * d + t + 1) * P], sin[:, d, t, :], ident)
                    mm.then_inc(st_s, 1)
                    pe.wait_ge(sl_s, i * 8 + (4 * j + 4))
                    for c in range(NCH):
                        pe.wait_ge(tc_s, i * (2 * NCH) + (NCH * j + c + 1))
                        for m in range(3):
                            mm = E.transpose(bank[:, 4, m * P:(m + 1) * P], xc[:, m, chunk(c)], ident)
                        mm.then_inc(tu_s, 1)
                    pe.wait_ge(tc_s, i * (2 * NCH) + (NCH * j + NCH + 1))
                    for n, (c, d) in enumerate(order):
                        q = i * (2 * NS) + (NS * j + n)
                        pe.wait_ge(us_s, q + 1)
                        E.matmul(bank[:, 4, 0:P], xc[:, 2, chunk(c)], xc[:, 3, chunk(c)], start=True, stop=True).then_inc(cb_s, 1)
                        pe.wait_ge(wt_s, q + 1)
                        for hh in range(4):
                            o = bank[64 * (hh % 2):64 * (hh % 2) + 64, 5, (hh // 2) * P:(hh // 2 + 1) * P]
                            E.matmul(o, dx[:, hh, :], ee[:, hh, :], start=True, stop=False)
                            E.matmul(o, S[:, d, hh * 64:hh * 64 + 64], cw[:, hh, :], start=False, stop=True)
                        E.matmul(bank[:, 6, 0:256], xt[:, c, 2 * P:3 * P], dxw.rearrange("p h q -> p (h q)"),
                                 start=True, stop=True).then_inc(pr_s, 1)
                        if n == 1:
                            pe.wait_ge(sf_s, i * 2 + (j + 1))
                            for dd in range(2):
                                for t in range(2):
                                    mm = E.transpose(bank[:, 7, (2 * dd + t) * P:(2 * dd + t + 1) * P],
                                                     S[:, dd, t * P:(t + 1) * P], ident)
                            mm.then_inc(st_s, 1)

        def dve(dve):
            for c in (slice(0, 1), slice(LATN + 1, LATN + 2), slice(PCTX.stop, PAD)):
                lv.done(V.memset(raw[:, :, c], 0.0))
            dve.sem_inc(ge_s, 1)
            dve.sem_inc(tc_s, 1)
            dve.sem_inc(us_s, 1)
            with turns(dve, 4, [(lv, LV_SSD)]) as i:
                for j in range(2):
                    for m in range(4):
                        dve.wait_ge(rw_s, i * 8 + (4 * j + m + 1))
                        if m >= 2:
                            dve.wait_ge(sl_s, i * 8 + (4 * j + m - 1))
                        tile = (lambda v: vec[:, bass.ds(i * 4 + (v + 2 * j + m), 1)]) if m < 2 else \
                               (lambda v: vec[:, bass.ds(i * 2 + (v + 16 + 8 * (m - 2) + j), 1)])
                        conv(raw, m, tmp[:, m % 2], tile(V_OCW), tile(V_OCW + 32), tile(V_OCW + 64), tile(V_OCB))
                        dve.sem_inc(cv_s, 1)
                    dve.wait_ge(st_s, i * 4 + (2 * j + 1))
                    lv.done(V.tensor_copy(s0.rearrange("p d q -> p (d q)"), bank[:, 7, :]))
                    lv.done(V.memset(S[:, :, :], 0.0))
                    for c in range(NCH):
                        dve.wait_ge(tu_s, i * (2 * NCH) + (NCH * j + c + 1))
                        lv.done(V.tensor_copy(xt[:, c, :], bank[:, 4, 0:3 * P]))
                        dve.sem_inc(tc_s, 1)
                    dve.wait_ge(ci_s, i * 64 + (32 * j + 32))
                    for n, (c, d) in enumerate(order):
                        q = i * (2 * NS) + (NS * j + n)
                        x4 = xt[:, c, 0:256].rearrange("p (h q) -> p h q", h=4)
                        b64 = lambda v: hs(v, i, j, c, d).unsqueeze(2).to_broadcast([P, 4, 64])
                        for hh in range(4):
                            sc1 = cumc[:, c, bass.ds(i * 8 + (32 * d + 4 * j + hh), 1)]
                            ins = V.tensor_scalar(arg[:, hh, :], cumb[:, d, hh, chunk(c)], sc1, 0.0, ALU.subtract, ALU.min)
                        ins.then_inc(ar_s, 1)
                        lv.done(V.tensor_tensor(dx[:, :, :], x4, b64(dtc), ALU.mult))
                        lv.done(V.tensor_tensor(dxw[:, :, :], dx[:, :, :], b64(dece), ALU.mult))
                        dve.wait_ge(cb_s, q + 1)
                        lv.done(V.tensor_tensor(cbm[:, 0, :], bank[:, 4, 0:P], (upper, lower)[d], ALU.mult))
                        dve.wait_ge(ex_s, q + 1)
                        lv.done(V.tensor_tensor(ee[:, :, :], ee[:, :, :], cbm[:, 0, :].unsqueeze(1).to_broadcast([P, 4, P]), ALU.mult))
                        lv.done(V.tensor_tensor(cw[:, :, :], ec[:, :, :], xc[:, 3, chunk(c)].unsqueeze(1).to_broadcast([P, 4, P]), ALU.mult))
                        dve.sem_inc(wt_s, 1)
                        dve.wait_ge(pr_s, q + 1)
                        for t in range(2):
                            yt = yb[:, bass.ds(i * 4 + (2 * j + t), 1), chunk(c)].rearrange("p o t -> p (o t)")
                            pt = bank[:, 5, t * P:(t + 1) * P]
                            if (c, d) in first:
                                lv.done(V.scalar_tensor_tensor(yt, xc[:, t, chunk(c)], dsk[:, bass.ds(i * 4 + (2 * j + t), 1)],
                                                               pt, ALU.mult, ALU.add))
                            else:
                                lv.done(V.tensor_tensor(yt, yt, pt, ALU.add))
                        Sd = S[:, d, :].rearrange("p (h q) -> p h q", h=4)
                        lv.done(V.tensor_tensor(Sd, Sd, b64(cdec), ALU.mult))
                        lv.done(V.tensor_tensor(S[:, d, :], S[:, d, :], bank[:, 6, 0:256], ALU.add))
                        if n == 1:
                            dve.sem_inc(sf_s, 1)
                            dve.wait_ge(st_s, i * 4 + (2 * j + 2))
                            dve.wait_ge(so_s, i * 64 + (32 * j + 32))
                            lv.done(V.tensor_copy(so.rearrange("p d a n -> p (d a n)"), bank[:, 7, :]))
                            dve.sem_inc(sc_s, 2)
                            lv.done(V.tensor_copy(S[:, :, :], s0[:, :, :]))
                        dve.sem_inc(us_s, 1)
                    for t in range(2):
                        yt = yb[:, bass.ds(i * 4 + (2 * j + t), 1), :].rearrange("p o t -> p (o t)")
                        lv.done(V.tensor_tensor(yt, yt, zb[:, t, :], ALU.mult))
                    dve.sem_inc(ge_s, 1)
            dve.wait_ge(so_s, 32 * (NG + 1))

        return pe, act, dve, fetches

    def stage_store(hn, out_p, out_x):
        ot = take(NCH, DM)
        t_s, c_s = sem("y_turned"), sem("y_copied")

        def pe(pe):
            for c in range(NCH):
                for half in range(2):
                    n = 2 * c + half
                    if n >= 2:
                        pe.wait_ge(c_s, n - 1)
                    for f in range(4):
                        mm = E.transpose(bank[:, n % 2, f * P:(f + 1) * P], hn[:, 4 * half + f, chunk(c)], ident)
                    mm.then_inc(t_s, 1)

        def dve(dve):
            for n in range(2 * NCH):
                dve.wait_ge(t_s, n + 1)
                V.tensor_copy(ot[:, n // 2, (n % 2) * 512:(n % 2 + 1) * 512], bank[:, n % 2, :]).then_inc(c_s, 1)

        def act(act):
            for c in range(NCH):
                act.wait_ge(c_s, 2 * c + 2)
                store(out_p[0, :, :] if c == CT else out_x[0, c * P:(c + 1) * P, :], ot[:, c, :])
            act.wait_ge(stored, 16 * nstores[0])

        return pe, act, dve

    out_p, out_x, out_c, out_n, out_m, out_r, out_s = outs
    scratch = nc.dram_tensor("cumulative_decays", (64, T), F32, kind="Internal").ap()
    def region(*parts):
        mark = top[0]
        for make in parts:
            top[0] = mark
            stages.append(make())
        top[0] = mark

    region(stage_load)
    region(stage_mod)

    cat = take(KD, T)
    base = top[0]
    nw = lambda l, n: vec[:, V_NORM + 16 * l + 8 * n:V_NORM + 16 * l + 8 * n + 8]
    region(lambda: stage_norm(x, cat, KD, 8, nw(0, 0), 0, "n1"))
    pb = take(15, PAD)
    after_pb = top[0]
    qk, vo, gates = take(8, PAD), take(8, T), take(T)
    region(lambda: stage_even_in(cat, qk, vo, pb, gates),
           lambda: stage_conv(qk, vo, pb),
           lambda: stage_mlstm(qk, vo, gates, cat[:, 0:4, :], out_c, out_n, out_m),
           lambda: stage_head_norm(cat[:, 0:4, :], ones, P, EPS, vec[:, V_AN:V_AN + 4], None, "ha",
                                   finish_mlstm(cat[:, 0:4, :], vo)))
    top[0] = after_pb
    kk, av, ld, cum = take(4, T), take(4, T), take(2, 4, T), take(2, 4, T)
    yb = cat[:, 4:8, :]
    region(lambda: stage_rwkv_in(pb, kk, av, ld, cum),
           lambda: stage_rwkv(pb, kk, av, ld, cum, yb, out_r))
    top[0] = after_pb
    region(lambda: stage_head_norm(yb, blk, 64, LN_EPS, vec[:, V_LW:V_LW + 4], vec[:, V_LB:V_LB + 4], "hb",
                                   lambda dve, j: None),
           lambda: stage_rwkv_out(pb, yb))
    region(lambda: stage_out(cat, a["ev_w_out"][0], (8,), 16))

    def ffn(l):
        top[0] = base
        region(lambda: stage_norm(x, cat, KD, 48 * l + 32, nw(l, 1), 48 * l + 24, f"f{l}"))
        hid = take(KF, T)
        region(lambda: stage_ffn_in(cat, hid, a["ffn_w_in"][l], f"ffn{l}"),
               lambda: stage_out(hid, a["ffn_w_out"][l], (8, 8, 6), 48 * l + 40))
        top[0] = base

    ffn(0)

    region(lambda: stage_norm(x, cat, KD, 48 + 8, nw(1, 0), 48, "n3"))
    yc = take(KC, T)
    dtc, cumc, dece, cdec = (take(NCH, 64) for _ in range(4))
    region(lambda: stage_dt(cat, dtc, cumc, dece, cdec, scratch),
           lambda: stage_ssd(cat, yc, dtc, cumc, dece, cdec, scratch, dsk, out_s))
    region(lambda: stage_norm(yc, yc, KC, None, vec[:, V_ONW:V_ONW + KC], None, "n4"),
           lambda: stage_out(yc, a["od_w_out"][0], (8, 8), 48 + 16))
    top[0] = base
    ffn(1)
    region(lambda: stage_norm(x, cat, KD, None, vec[:, V_FIN:V_FIN + KD], None, "n5"),
           lambda: stage_store(cat, out_p, out_x))

    block = ctx.enter_context(nc.Block())

    @block.sync
    def _(sp):
        for st in stages:
            if len(st) == 4:
                st[3](sp)

    @block.scalar
    def _(act):
        eng_of["act"] = la.eng = act
        for st in stages:
            st[1](act)
            fence("act")

    @block.vector
    def _(dve):
        eng_of["dve"] = lv.eng = dve
        for st in stages:
            st[2](dve)
            fence("dve")

    @block.tensor
    def _(pe):
        eng_of["pe"] = pe
        pe.sem_inc(unit_done, 4)
        for p in range(2):
            pe.sem_inc(psum_free[p], 1)
        for st in stages:
            st[0](pe)
            fence("pe")


LV_SSD = 226


_INS = ['x_prompt', 'x_sample', 'state_mlstm_c', 'state_mlstm_n', 'state_mlstm_m', 'state_rwkv', 'state_ssd',
        'c', 'c_ctx', 'mod_w', 'mod_b', 'norm_w', 'ffn_w_in', 'ffn_w_out',
        'ev_w_in', 'ev_a_conv_w', 'ev_a_conv_b', 'ev_a_gate_b', 'ev_a_norm_w',
        'ev_b_mu', 'ev_b_w0', 'ev_b_w_up', 'ev_b_a0', 'ev_b_a_up', 'ev_b_g_up', 'ev_b_k_k', 'ev_b_k_a', 'ev_b_u',
        'ev_b_ln_w', 'ev_b_ln_b', 'ev_w_out',
        'od_w_in', 'od_conv_w', 'od_conv_b', 'od_dt_bias', 'od_a_log', 'od_d', 'od_norm_w', 'od_w_out',
        'final_norm_w']
_OUTS = [((1, 128, 1024), 'float32'), ((1, 512, 1024), 'float32'), ((1, 1, 2, 4, 128, 128), 'float32'),
         ((1, 1, 2, 4, 128), 'float32'), ((1, 1, 2, 4), 'float32'), ((1, 1, 2, 8, 64, 64), 'float32'),
         ((1, 1, 2, 32, 64, 128), 'float32')]


def _constants():
    import numpy as np
    c = np.zeros((P, NCONST), np.float32)
    i = np.arange(P)
    c[:, C_ID:C_ID + P] = np.eye(P)
    c[:, C_ONE:C_ONE + P] = 1
    c[:, C_UP:C_UP + P] = i[:, None] <= i[None, :]
    c[:, C_LO:C_LO + P] = i[:, None] >= i[None, :]
    c[:, C_BLK:C_BLK + P] = i[:, None] // 64 == i[None, :] // 64
    s, t = (i % 64)[:, None], np.arange(64)[None, :]
    for d in range(2):
        ss, tt = (s, t) if d == 0 else (63 - s, 63 - t)
        for l in range(6):
            b = 2 ** l
            at = C_LVL + (d * 6 + l) * 64
            c[:, at:at + 64] = (tt // b == ss // b + 1) & ((tt // b) % 2 == 1)
        c[:, C_MK + d * 128:C_MK + d * 128 + 64] = ss < tt
        c[:, C_MK + d * 128 + 64:C_MK + d * 128 + 128] = ss <= tt
    c[:, C_I64:C_I64 + 64] = s == t
    c[:, C_RST:C_RST + T] = (np.arange(T) % 64 != 0)[None]
    nf = DM // 4
    freq = np.exp(-np.log(10000.0).astype(np.float32) * np.arange(nf, dtype=np.float32) / nf)
    for f in range(8):
        fr = freq[(f % 2) * P:(f % 2 + 1) * P][:, None]
        fn = np.sin if f % 4 < 2 else np.cos
        if f < 4:
            c[:, C_POSR + f * 8:C_POSR + f * 8 + 8] = fn(np.arange(8, dtype=np.float32)[None] * fr)
        else:
            c[:, C_POSC + (f - 4) * 64:C_POSC + (f - 3) * 64] = fn(np.arange(64, dtype=np.float32)[None] * fr)
    return c


def kernel(**inputs):
    import numpy as _np
    import concourse.bacc as _bacc
    from concourse import mybir as _mybir
    from concourse.bass_utils import run_bass_kernel_spmd as _run

    nc = _bacc.Bacc("TRN2", target_bir_lowering=False, num_devices=1)
    arrays, args = {}, {}
    for name in _INS + ["consts"]:
        arr = _constants() if name == "consts" else _np.ascontiguousarray(inputs[name])
        arrays[f"in_{name}_dram"] = arr
        args[name] = nc.dram_tensor(f"in_{name}_dram", arr.shape, _mybir.dt.from_np(arr.dtype), kind="ExternalInput").ap()
    outs = []
    for i, (shape, dtype) in enumerate(_OUTS):
        dt = _mybir.dt.from_np(_np.dtype(dtype))
        outs.append(nc.dram_tensor(f"out_{i}_dram", shape, dt, kind="ExternalOutput").ap())
    build(nc, args, outs)
    r = _run(nc, [arrays], core_ids=[0])
    return tuple(r.results[0][f"out_{i}_dram"] for i in range(len(_OUTS)))
```

```python
from contextlib import ExitStack, contextmanager

import concourse.bass as bass
from concourse import mybir

ALU = mybir.AluOpType
ACT = mybir.ActivationFunctionType
AX_X = mybir.AxisListType.X
F32 = mybir.dt.float32

P = 128
DM = 1024
KD = DM // P
LATN, CTXN = 512, 128
T = LATN + CTXN
LAT, CTX = slice(0, LATN), slice(LATN, T)
PAD = 644
PLAT, PCTX = slice(1, 1 + LATN), slice(LATN + 2, LATN + 2 + CTXN)
NCH = T // P
CT = NCH - 1
AH = 4
FFN = 2816
KF = FFN // P
CI = 2048
KC = CI // P
NG = 8
EPS = 1e-6
LN_EPS = 64e-5
DECAY = 0.606531
R64 = 64


def chunk(c):
    return slice(c * P, (c + 1) * P)


def pchunk(c):
    a = 1 + c * P if c < CT else PCTX.start
    return slice(a, a + P)


def p64(c):
    a = 1 + c * R64 if c < 8 else PCTX.start + (c - 8) * R64
    return slice(a, a + R64)


C_ID, C_ONE, C_UP, C_LO, C_BLK = 0, 128, 256, 384, 512
C_LVL = 640
C_MK = C_LVL + 2 * 6 * 64
C_I64 = C_MK + 2 * 2 * 64
C_RST = C_I64 + 64
C_POSR = C_RST + T
C_POSC = C_POSR + 4 * 8
NCONST = C_POSC + 4 * 64

V_MODB, V_NORM = 0, 96
V_CW, V_CB, V_AN, V_MU, V_W0, V_A0, V_KK, V_KA, V_U, V_LW, V_LB, V_FIN = (
    128, 152, 160, 164, 179, 187, 191, 195, 199, 207, 211, 215)
V_OCW, V_OCB = 256, 352
V_ONW, V_C, V_N = 384, 400, 416
NVT = 4


class Count:

    def __init__(self, eng, sem, n=0):
        self.eng, self.sem, self.n, self.turn = eng, sem, n, 0

    def next(self, by=1):
        self.n += by
        self.eng.wait_ge(self.sem, self.turn + self.n)

    def done(self, ins):
        ins.then_inc(self.sem, 1)
        self.next()


@contextmanager
def turns(eng, n, counts):
    start = [c.n for c, _ in counts]
    with eng.Fori(0, n) as i:
        for c, per in counts:
            c.turn = i * per
        yield i
    for (c, per), s in zip(counts, start):
        assert c.n - s == per, (c.sem, c.n - s, per)
        c.n, c.turn = s + n * per, 0


def build(nc, a, outs):
    with ExitStack() as ctx:
        _build(ctx, nc, a, outs)


def _build(ctx, nc, a, outs):
    V, A, E = nc.vector, nc.scalar, nc.tensor

    def sb(name, shape):
        return ctx.enter_context(nc.sbuf_tensor(name, shape, F32))

    def sem(name):
        return ctx.enter_context(nc.semaphore(name))

    const = sb("const", [P, NCONST])
    ident, ones = const[:, C_ID:C_ID + P], const[:, C_ONE:C_ONE + P]
    upper, lower = const[:, C_UP:C_UP + P], const[:, C_LO:C_LO + P]
    blk = const[:, C_BLK:C_BLK + P]
    lvl = const[:, C_LVL:C_MK].rearrange("p (d l t) -> p d l t", d=2, l=6)
    mk = const[:, C_MK:C_I64].rearrange("p (d m t) -> p d m t", d=2, m=2)
    i64 = const[:, C_I64:C_RST]
    rst = const[:, C_RST:C_POSR]
    posr = const[:, C_POSR:C_POSC].rearrange("p (f r) -> p f r", f=4)
    posc = const[:, C_POSC:NCONST].rearrange("p (f r) -> p f r", f=4)
    vec = sb("vec", [P, NVT * P])
    mod = sb("mod", [P, 96, 2])
    x = sb("x", [P, KD, T])
    ring = sb("ring", [P, 4, KD, P])
    amp = sb("amp", [P, KD, 2])
    rstd = sb("rstd", [P, T])
    small = sb("small", [P, 16])
    cs_T = sb("cs_T", [P, KD, 2])
    dsk = sb("dsk", [P, KC])
    NAR = 39000
    NSPLIT = 4 * 2 * KD * P + 2 * KD * LATN
    with nc.sbuf_tensor("below_splits", [P, NAR - NSPLIT], F32):
        with nc.sbuf_tensor("w_split", [P, 4, 2, KD, P], mybir.dt.float32r) as w_split, \
                nc.sbuf_tensor("h_split", [P, 2, KD, LATN], mybir.dt.float32r) as h_split:
            pass
    arena = sb("arena", [P, NAR])
    top = [0]

    def take(*shape):
        n = 1
        for s in shape:
            n *= s
        v = arena[:, top[0]:top[0] + n]
        top[0] += n
        assert top[0] <= NAR, top[0]
        if len(shape) == 2:
            v = v.rearrange("p (a b) -> p a b", a=shape[0])
        elif len(shape) == 3:
            v = v.rearrange("p (a b c) -> p a b c", a=shape[0], b=shape[1])
        elif len(shape) == 4:
            v = v.rearrange("p (a b c d) -> p a b c d", a=shape[0], b=shape[1], c=shape[2])
        return v

    bank = ctx.enter_context(nc.psum_tensor("bank", [P, 8, 512], F32))
    pair = [bank[:, 0:2, :].rearrange("p b n -> p (b n)"), bank[:, 2:4, :].rearrange("p b n -> p (b n)")]
    pairs = pair + [bank[:, 4:6, :].rearrange("p b n -> p (b n)"), bank[:, 6:8, :].rearrange("p b n -> p (b n)")]

    w_ready = [sem(f"w_ready{s}") for s in range(4)]
    unit_done = sem("unit_done")
    psum_free = [sem(f"psum_free{s}") for s in range(2)]
    act_chain, dve_chain = sem("act_chain"), sem("dve_chain")
    at_end = {e: sem(f"{e}_stage_end") for e in ("pe", "act", "dve")}
    loaded, stored = sem("loaded"), sem("stored")
    stage_no = {"pe": 0, "act": 0, "dve": 0}
    eng_of = {}
    la, lv = Count(None, act_chain), Count(None, dve_chain)

    def fence(me):
        eng = eng_of[me]
        eng.drain().then_inc(at_end[me], 1)
        stage_no[me] += 1
        for e in at_end:
            eng.wait_ge(at_end[e], stage_no[me])

    nloads = [0]

    def load(dst, src):
        eng_of["act"].dma_start(dst, src).then_inc(loaded, 16)
        nloads[0] += 1

    nstores = [0]

    def store(dst, src):
        eng_of["act"].dma_start(dst, src).then_inc(stored, 16)
        nstores[0] += 1

    stages = []
    unit0, out0 = [0], [0]

    def fetch(sp, s, q, src, kt, cols):
        sp.wait_ge(unit_done, q * 4 + s + 1)
        sp.dma_start(ring[:, s, 0:kt, 0:cols], src).then_inc(w_ready[s], 16)

    def unit(s, q, pr, v, rhs, kt, m=P, first=True, last=True):
        pe = eng_of["pe"]
        pe.wait_ge(w_ready[s], q * 16 + 16)
        if first:
            pe.wait_ge(psum_free[pr], v + 1)
        for k in range(kt):
            st, en = first and k == 0, last and k == kt - 1
            E.matmul(pair[pr][0:m, 0:LATN], ring[:, s, k, 0:m], rhs[:, k, LAT], start=st, stop=en)
            mm = E.matmul(pair[pr][0:m, LATN:T], ring[:, s, k, 0:m], rhs[:, k, CTX], start=st, stop=en)
        mm.then_inc(unit_done, 1)

    def unit_split(s, ws, pr, rhs, v, low_done):
        pe = eng_of["pe"]
        pe.wait_ge(*low_done)
        pe.wait_ge(psum_free[pr], v + 1)
        for k in range(KD):
            st, en = k == 0, k == KD - 1
            o = pair[pr][:, LAT]
            E.matmul(o, w_split[:, ws, 0, k, :], h_split[:, 0, k, :], start=st, stop=False)
            E.matmul(o, w_split[:, ws, 0, k, :], h_split[:, 1, k, :], start=False, stop=False)
            E.matmul(o, w_split[:, ws, 1, k, :], h_split[:, 0, k, :], start=False, stop=en)
            mm = E.matmul(pair[pr][:, CTX], ring[:, s, k, :], rhs[:, k, CTX], start=st, stop=en)
        mm.then_inc(unit_done, 1)

    def high_of(s, ws):
        return A.activation(w_split[:, ws, 0], ring[:, s], ACT.Copy)

    def low_of(s, ws):
        return V.tensor_tensor(w_split[:, ws, 1], ring[:, s], w_split[:, ws, 0].bitcast(F32), ALU.subtract)

    def high_of_rhs(rhs, high_s):
        for k in range(KD):
            A.activation(h_split[:, 0, k, :], rhs[:, k, LAT], ACT.Copy).then_inc(high_s, 1)

    def low_of_rhs(dve, rhs, high_s, low_s):
        for k in range(KD):
            dve.wait_ge(high_s, k + 1)
            V.tensor_tensor(h_split[:, 1, k, :], rhs[:, k, LAT], h_split[:, 0, k, :].bitcast(F32),
                            ALU.subtract).then_inc(low_s, 1)

    def unit_wait(eng, q, s):
        eng.wait_ge(unit_done, q * 4 + s + 1 + 4)

    def stage_load():
        rows = take(NVT, P)
        xin = take(NCH, DM)
        d_all = take(2 * KC)
        vt_s, x_s, c_s = sem("vectors_transposed"), sem("x_transposed"), sem("bank_copied")
        cs = take(2, 2, 8)

        def act(act):
            load(const[:, :], a["consts"])
            act.wait_ge(c_s, 1)

            def put(row, src, n):
                t, r = row // P, row % P
                load(rows[r:r + n, t, :], src)
            put(V_MODB, a["mod_b"].rearrange("l (r c) -> (l r) c", c=P), 96)
            put(V_NORM, a["norm_w"].rearrange("l j (r c) -> (l j r) c", c=P), 32)
            put(V_CW, a["ev_a_conv_w"].rearrange("e w (r c) -> (e w r) c", c=P), 24)
            put(V_CB, a["ev_a_conv_b"].rearrange("e (r c) -> (e r) c", c=P), 8)
            put(V_AN, a["ev_a_norm_w"].rearrange("e (r c) -> (e r) c", c=P), 4)
            put(V_MU, a["ev_b_mu"][0, 0:13 * P].rearrange("(r c) -> r c", c=P), 13)
            put(V_MU + 13, a["ev_b_mu"][0, 13 * P + 64:14 * P + 64].rearrange("(r c) -> r c", c=P), 1)
            load(rows[(V_MU + 14) % P:(V_MU + 14) % P + 1, 1, 0:64],
                 a["ev_b_mu"][0, 13 * P:13 * P + 64].rearrange("(r c) -> r c", c=64))
            put(V_W0, a["ev_b_w0"].rearrange("e d (r c) -> (e d r) c", c=P), 8)
            for v, n in ((V_A0, "ev_b_a0"), (V_KK, "ev_b_k_k"), (V_KA, "ev_b_k_a"), (V_LW, "ev_b_ln_w"), (V_LB, "ev_b_ln_b")):
                put(v, a[n].rearrange("e (r c) -> (e r) c", c=P), 4)
            put(V_U, a["ev_b_u"].rearrange("e d (r c) -> (e d r) c", c=P), 8)
            put(V_FIN, a["final_norm_w"].rearrange("(r c) -> r c", c=P), 8)
            put(V_OCW, a["od_conv_w"].rearrange("e w (r c) -> (e w r) c", c=P), 96)
            put(V_OCB, a["od_conv_b"].rearrange("e (r c) -> (e r) c", c=P), 32)
            put(V_ONW, a["od_norm_w"].rearrange("e (r c) -> (e r) c", c=P), 16)
            put(V_C, a["c_ctx"].rearrange("(r c) -> r c", c=P), 8)
            put(V_C + 8, a["c"].rearrange("b (r c) -> (b r) c", c=P), 8)
            put(V_N, a["state_mlstm_n"].rearrange("b e d h k -> (b e d h) k"), 8)
            load(xin[:, 0:4, :], a["x_sample"].rearrange("b (c p) f -> p (b c) f", p=P))
            load(xin[:, 4, :], a["x_prompt"].rearrange("b p f -> p (b f)"))
            load(small[0:16, 0:1], a["ev_a_gate_b"].rearrange("e t d h -> (e t d h)").rearrange("(r c) -> r c", c=1))
            load(small[0:64, 1:2], a["od_dt_bias"].rearrange("e d h -> (e d h)").rearrange("(r c) -> r c", c=1))
            load(small[0:64, 2:3], a["od_a_log"].rearrange("e d h -> (e d h)").rearrange("(r c) -> r c", c=1))
            load(small[:, 3:11], a["state_mlstm_m"].rearrange("b e d h -> (b e d h)").partition_broadcast(P))
            load(d_all, a["od_d"][0].partition_broadcast(P))
            act.wait_ge(loaded, 16 * nloads[0])
            for e in range(2):
                A.activation(dsk[64 * e:64 * e + 64, :], d_all[64 * e:64 * e + 64, e::2], ACT.Copy)
            act.wait_ge(c_s, 2)
            for s in range(2):
                la.done(A.activation(cs_T[:, :, s], vec[:, V_C + 8 * s:V_C + 8 * s + 8], ACT.Silu))

        def dve(dve):
            V.memset(rows[:, :, :], 0.0).then_inc(c_s, 1)
            dve.wait_ge(vt_s, 1)
            V.tensor_copy(vec[:, :], bank[:, 4, :]).then_inc(c_s, 1)
            lv.done(V.memset(rstd[:, :], 0.0))
            for f in range(KD):
                pr = pairs[f % 2]
                dve.wait_ge(x_s, f + 1)
                if f < 4:
                    pos = posr[:, f, :].unsqueeze(2).to_broadcast([P, 8, 64])
                else:
                    pos = posc[:, f - 4, :].unsqueeze(1).to_broadcast([P, 8, 64])
                V.tensor_tensor(x[:, f, LAT].rearrange("p (r c) -> p r c", r=8),
                                pr[:, LAT].rearrange("p (r c) -> p r c", r=8), pos, ALU.add)
                V.tensor_copy(x[:, f, CTX], pr[:, CTX]).then_inc(c_s, 1)

        def pe(pe):
            pe.wait_ge(c_s, 1)
            pe.wait_ge(loaded, 16 * nloads[0])
            for t in range(NVT):
                mm = E.transpose(bank[:, 4, t * P:(t + 1) * P], rows[:, t, :], ident)
            mm.then_inc(vt_s, 1)
            for f in range(KD):
                if f >= 2:
                    pe.wait_ge(c_s, f + 1)
                for c in range(NCH):
                    mm = E.transpose(pairs[f % 2][:, c * P:(c + 1) * P], xin[:, c, f * P:(f + 1) * P], ident)
                mm.then_inc(x_s, 1)

        return pe, act, dve


    MOD0 = 2 * KD
    mod_tiles = [0]

    def mod_fetches(sp, u0, t0, n):
        for l in range(2):
            a0, a1 = max(t0, 48 * l), min(t0 + n, 48 * l + 48)
            if a0 < a1:
                w = a["mod_w"][l, :, :].rearrange("(k p) n -> p k n", p=P)
                with sp.Fori(0, (a1 - a0) // 4) as i:
                    for s in range(4):
                        fetch(sp, s, i + (u0 + a0 - t0) // 4, w[:, :, bass.ds(i * (4 * P) + (a0 - 48 * l + s) * P, P)], KD, P)

    def mod_unit(out, s):
        for k in range(KD):
            mm = E.matmul(out, ring[:, s, k, :], cs_T[:, k, :], start=(k == 0), stop=(k == KD - 1))
        mm.then_inc(unit_done, 1)

    def mod_bias(t0, n, src):
        return V.tensor_tensor(mod[:, t0:t0 + n, :], src.rearrange("p (n s) -> p n s", s=2),
                               vec[:, V_MODB + t0:V_MODB + t0 + n].unsqueeze(2).to_broadcast([P, n, 2]), ALU.add)

    def mod_share(n, out):
        u0, t0 = unit0[0], mod_tiles[0]
        unit0[0] += n
        mod_tiles[0] += n
        made = [0]

        def fetches(sp):
            mod_fetches(sp, u0, t0, n)

        def make(pe, k):
            for u in range(made[0], made[0] + k):
                pe.wait_ge(w_ready[u % 4], (u0 + u) // 4 * 16 + 16)
                mod_unit(out[:, 2 * u:2 * u + 2], u % 4)
            made[0] += k

        def end(dve):
            assert made[0] in (0, n)
            dve.wait_ge(unit_done, u0 + n + 4)
            lv.done(mod_bias(t0, n, out[:, 0:2 * n]))

        return fetches, make, end

    def stage_mod():
        fetches, make, mod_end = mod_share(MOD0, bank[:, 4, :])
        return (lambda pe: make(pe, MOD0)), (lambda act: None), mod_end, fetches

    def col(v, n=1):
        return vec[:, v:v + n]

    def stage_norm(src, dst, kt, scale_at, weight, shift_at, name):
        sq_s, ss_s, m_s, rt_s, h_s = (sem(f"{name}_{n}") for n in ("squares", "sum", "mean", "root", "scaled"))
        sq = dst if kt == KD else take(2, T)
        ring2 = 0 if kt == KD else 2

        def act(act):
            for k in range(kt):
                if ring2 and k >= 2:
                    act.wait_ge(ss_s, k - 1)
                A.activation(sq[:, k % 2 if ring2 else k, :], src[:, k, :], ACT.Square).then_inc(sq_s, 1)
            act.wait_ge(m_s, 1)
            la.done(A.activation(rstd[:, :], rstd[:, :], ACT.Sqrt))
            act.sem_inc(rt_s, 1)
            if shift_at is not None:
                for k in range(kt):
                    act.wait_ge(h_s, k + 1)
                    for s, c in ((1, LAT), (0, CTX)):
                        A.activation(dst[:, k, c], dst[:, k, c], ACT.Identity,
                                     bias=mod[:, shift_at + k, s:s + 1])

        def pe(pe):
            for k in range(kt):
                pe.wait_ge(sq_s, k + 1)
                q = sq[:, k % 2 if ring2 else k, :]
                E.matmul(pairs[2][:, LAT], ones, q[:, LAT], start=(k == 0), stop=(k == kt - 1))
                E.matmul(pairs[2][:, CTX], ones, q[:, CTX], start=(k == 0), stop=(k == kt - 1)).then_inc(ss_s, 1)

        def dve(dve):
            if scale_at is not None:
                lv.done(V.scalar_tensor_tensor(amp[:, :, :], mod[:, scale_at:scale_at + KD, :], 1.0,
                                               weight.unsqueeze(2).to_broadcast([P, KD, 2]), ALU.add, ALU.mult))
            dve.wait_ge(ss_s, kt)
            lv.done(V.tensor_scalar(rstd[:, :], pairs[2][:, 0:T], 1.0 / (kt * P), EPS, ALU.mult, ALU.add))
            dve.sem_inc(m_s, 1)
            dve.wait_ge(rt_s, 1)
            lv.done(V.reciprocal(rstd[:, :], rstd[:, :]))
            for k in range(kt):
                if scale_at is not None:
                    for s, c in ((1, LAT), (0, CTX)):
                        ins = V.scalar_tensor_tensor(dst[:, k, c], src[:, k, c], amp[:, k, s:s + 1], rstd[:, c],
                                                     ALU.mult, ALU.mult)
                else:
                    ins = V.scalar_tensor_tensor(dst[:, k, :], src[:, k, :], weight[:, k:k + 1], rstd[:, :],
                                                 ALU.mult, ALU.mult)
                ins.then_inc(h_s, 1)

        return pe, act, dve

    def stage_even_in(h, qk, vo, pb, gates):
        assert top[0] <= NAR - NSPLIT + 2 * 2 * KD * P
        hh_s, hl_s = sem("ei_h_high"), sem("ei_h_low")
        wh_s, wl_s = sem("ei_w_high"), sem("ei_w_low")
        u0, v0 = unit0[0], out0[0]
        unit0[0] += 32
        out0[0] += 32
        w = a["ev_w_in"][0].rearrange("(k p) n -> p k n", p=P)
        loops = ((4, 0), (3, 4 * AH * P + 16))
        NSP = 4 + 3
        last = ((3600, P), (3792, P), (3728, 64), (2048, 16))

        def fetches(sp):
            q = u0 // 4
            for n, c0 in loops:
                with sp.Fori(0, n) as i:
                    for s in range(4):
                        fetch(sp, s, i + q, w[:, :, bass.ds(i * (4 * P) + (c0 + s * P), P)], KD, P)
                q += n
            for s, (c, m) in enumerate(last):
                fetch(sp, s, q, w[:, :, c:c + m], KD, m)

        def pe(pe):
            q, v = u0 // 4, v0 // 2
            pe.wait_ge(hl_s, KD)
            with pe.Fori(0, NSP) as i:
                for s in range(4):
                    unit_split(s, 2 + s % 2, s % 2, h, i * 2 + (v + s // 2), (wl_s, i * 4 + (s + 1)))
            q, v = q + NSP, v + 2 * NSP
            for s, (_, m) in enumerate(last):
                unit(s, q, s % 2, v + s // 2, h, KD, m)

        def act(act):
            q = u0 // 4

            def high(t, s):
                act.wait_ge(w_ready[s], t * 16 + (u0 // 4 * 16 + 16))
                act.wait_ge(unit_done, t * 4 + (u0 + 4 + s - 1))
                high_of(s, 2 + s % 2).then_inc(wh_s, 1)

            def ahead(t, s):
                high(t + (s + 2) // 4, (s + 2) % 4)

            high_of_rhs(h, hh_s)
            for s in range(2):
                high(0, s)

            def evac(i, q, s, tile, dst, padded):
                unit_wait(act, i + q, s)
                if padded:
                    A.activation(dst[:, tile, PLAT], pair[s % 2][:, LAT], ACT.Copy)
                    A.activation(dst[:, tile, PCTX], pair[s % 2][:, CTX], ACT.Copy).then_inc(psum_free[s % 2], 1)
                else:
                    A.activation(dst[:, tile, :], pair[s % 2][:, 0:T], ACT.Copy).then_inc(psum_free[s % 2], 1)
            one = lambda e: bass.ds(e, 1)
            for dst, padded, n in ((qk, True, 2), (vo, False, 2), (pb, True, 2)):
                with turns(act, n, []) as i:
                    for s in range(4):
                        evac(i, q, s, one(i * 4 + s), dst, padded)
                        ahead(i + (q - u0 // 4), s)
                q += n
            for s in range(4):
                evac(0, q, s, 8 + s, pb, True)
                if s < 2:
                    ahead(q - u0 // 4, s)
            q += 1
            for s, t in ((0, 12), (1, 13)):
                evac(0, q, s, t, pb, True)
            unit_wait(act, q, 2)
            A.activation(pb[0:64, 14, PLAT], pair[0][0:64, LAT], ACT.Copy)
            A.activation(pb[0:64, 14, PCTX], pair[0][0:64, CTX], ACT.Copy).then_inc(psum_free[0], 1)
            unit_wait(act, q, 3)
            A.activation(gates[0:16, :], pair[1][0:16, 0:T], ACT.Copy).then_inc(psum_free[1], 1)

        def dve(dve):
            for buf in (qk, pb):
                for c in (slice(0, 1), slice(LATN + 1, LATN + 2), slice(PCTX.stop, PAD)):
                    lv.done(V.memset(buf[:, :, c], 0.0))
            lv.done(V.memset(pb[64:128, 14, :], 0.0))
            low_of_rhs(dve, h, hh_s, hl_s)
            with dve.Fori(0, NSP) as i:
                for s in range(4):
                    dve.wait_ge(wh_s, i * 4 + (s + 1))
                    low_of(s, 2 + s % 2).then_inc(wl_s, 1)

        return pe, act, dve, fetches

    def conv(buf, k, tmp, w0, w1, w2, b):
        lv.done(V.tensor_scalar(tmp[:, 1:643], buf[:, k, 1:643], w1, b, ALU.mult, ALU.add))
        lv.done(V.scalar_tensor_tensor(tmp[:, 1:643], buf[:, k, 0:642], w0, tmp[:, 1:643], ALU.mult, ALU.add))
        lv.done(V.scalar_tensor_tensor(tmp[:, 1:643], buf[:, k, 2:644], w2, tmp[:, 1:643], ALU.mult, ALU.add))

    def stage_conv(qk, vo, pb):
        cv_s, si_s, g_s = sem("convolved"), sem("silu_done"), sem("scaled_k")
        tmp = take(4, PAD)
        mu = take(2, 16)
        fetches, make, mod_end = mod_share(16, bank[:, 3, :])

        def act(act):
            for k in range(8):
                act.wait_ge(cv_s, k + 1)
                A.activation(qk[:, k, PLAT], tmp[:, k % 2, PLAT], ACT.Silu)
                A.activation(qk[:, k, PCTX], tmp[:, k % 2, PCTX], ACT.Silu).then_inc(si_s, 1)
            A.activation(vo[:, 4:8, :], vo[:, 4:8, :], ACT.Sigmoid)
            act.wait_ge(si_s, 8)
            A.mul(qk[:, 4:8, PLAT], qk[:, 4:8, PLAT], P ** -0.5)
            A.mul(qk[:, 4:8, PCTX], qk[:, 4:8, PCTX], P ** -0.5)

        def dve(dve):
            for k in range(8):
                if k >= 2:
                    dve.wait_ge(si_s, k - 1)
                conv(qk, k, tmp[:, k % 2], col(V_CW + k), col(V_CW + 8 + k), col(V_CW + 16 + k), col(V_CB + k))
                dve.sem_inc(cv_s, 1)
            lv.done(V.tensor_scalar(mu[:, 0, 0:15], vec[:, V_MU:V_MU + 15], -1.0, 1.0, ALU.mult, ALU.add))
            lv.done(V.tensor_scalar(mu[:, 1, 0:15], vec[:, V_MU:V_MU + 15], 0.5, None, ALU.mult))
            for k in range(15):
                t = tmp[:, 2 + k % 2, 1:643]
                lv.done(V.tensor_tensor(t, pb[:, k, 0:642], pb[:, k, 2:644], ALU.add))
                lv.done(V.tensor_scalar(pb[:, k, 1:643], pb[:, k, 1:643], mu[:, 0, k:k + 1], None, ALU.mult))
                lv.done(V.scalar_tensor_tensor(pb[:, k, 1:643], t, mu[:, 1, k:k + 1], pb[:, k, 1:643],
                                               ALU.mult, ALU.add))
            mod_end(dve)

        return (lambda pe: make(pe, 16)), act, dve, fetches

    def stage_mlstm(qk, vo, gates, ha, out_c, out_n, out_m):
        gl_s, ga_s, tp_s, tc_s = sem("g_abs"), sem("g_ln"), sem("gate_products"), sem("gate_copies")
        both = take(4, 4, P)
        work = both.rearrange("p a h t -> p (a h t)")[:, 0:3 * T].rearrange("p (a t) -> p a t", a=3)
        em, qw, kw, nd = (both[:, n] for n in range(4))
        gt, lt = take(NCH, 16), take(NCH, 16)
        bcol, acol, ecol, tot = (take(2, NCH, 4) for _ in range(4))
        mloc = take(2)
        dg = take(2, 20)
        ml, ms, me, dec, sc, wcol, tt = (take(2, NCH, 4) for _ in range(7))
        arow, brow, rrow, morow = (take(2, P) for _ in range(4))
        msrow = take(2)
        ktok, vtok = take(NCH, 4, P), take(NCH, 4, P + 1)
        Cst = take(2, 4, P + 1)
        ctmp = take(4, P + 1)
        tmp, wi = take(4, P), take(4, P)
        ee = pt = tmp
        nout = take(8)
        noutT = take(P)
        f2 = lambda v: v.rearrange("p d c h -> p d (c h)")
        fl = lambda v: v.rearrange("p h t -> p (h t)")
        kv_s, kvc_s = sem("kv_turned"), sem("kv_copied")
        r_s, n_s, c_s = sem("r_rows_spread"), sem("num_den"), sem("c_local")
        rd_s, p_s, kw_s, st_s, e_s = (sem(f"ml_{n}") for n in
                                       ("arg", "weights", "kw", "state", "exp"))
        ex_s, no_s, q_s = sem("m_exp"), sem("n_rows"), sem("ml_spread_free")
        st_l, co_s = sem("states_in"), sem("n_turned")
        ctxs = [(CT, d, None) for d in range(2)]
        order = ctxs + [(c if d == 0 else CT - 1 - c, d, c) for c in range(CT) for d in range(2)]
        fetch_a, make_a, end_a = mod_share(8, bank[:, 3, :])
        fetch_b, make_b, end_b = mod_share(24, bank[:, 7, 256:])

        def fetches(sp):
            fetch_a(sp)
            fetch_b(sp)

        def act(act):
            act.wait_ge(gl_s, 1)
            la.done(A.activation(work[0:16, 0, :], work[0:16, 0, :], ACT.Exp, scale=-1.0))
            la.done(A.activation(work[0:16, 0, :], work[0:16, 0, :], ACT.Ln, bias=1.0))
            act.sem_inc(ga_s, 1)
            act.wait_ge(ex_s, 1)
            for v in (dec, sc, wcol):
                last = A.activation(v[:, :, :, :], v[:, :, :, :], ACT.Exp)
            last.then_inc(ga_s, 1)
            for n, (c, d, k) in enumerate(order):
                if n:
                    act.wait_ge(st_s, n)
                act.wait_ge(rd_s, n + 1)
                for h in range(4):
                    A.activation(wi[:, h, :], bank[:, 0, h * P:(h + 1) * P], ACT.Exp,
                                 bias=ms[:, d, c, h:h + 1], scale=-1.0)
                A.activation(fl(em), bank[:, 1, :], ACT.Exp, scale=-1.0).then_inc(q_s, 1)
                A.activation(fl(ee), fl(tmp), ACT.Exp, scale=-1.0).then_inc(e_s, 1)
                if n == 1:
                    act.wait_ge(st_s, 2)
                    for dd in range(2):
                        store(out_c[0, 0, dd].rearrange("h k v -> k h v"), Cst[:, dd, :, 0:P])
                    for dd in range(2):
                        store(out_m[0, 0, dd:dd + 1, :], me[0:1, dd, CT, :])
                    act.wait_ge(no_s, 1)
                    store(out_n[0, 0].rearrange("d h k -> (d h) k"), noutT[0:8, :])
                    act.wait_ge(stored, 16 * nstores[0])
                    for dd in range(2):
                        act.dma_start(Cst[:, dd, :, 0:P], a["state_mlstm_c"][0, 0, dd].rearrange("h k v -> k h v")
                                      ).then_inc(st_l, 16)

        def pe(pe):
            g = Count(pe, tc_s)
            g.next()
            for c in range(NCH):
                E.transpose(bank[:, 4, c * 16:(c + 1) * 16], gates[0:16, chunk(c)], ident[0:16, 0:16])
                mm = E.transpose(bank[:, 5, c * 16:(c + 1) * 16], work[0:16, 1, chunk(c)], ident[0:16, 0:16])
            mm.then_inc(tp_s, 1)
            g.next()
            E.matmul(bank[:, 6, 0:20], upper, lt[:, :, 8:12], start=True, stop=True)
            E.matmul(bank[:, 6, 20:40], lower, lt[:, :, 12:16], start=True, stop=True)
            E.matmul(bank[:, 7, 0:40], ones, lt[:, :, 8:16], start=True, stop=True).then_inc(tp_s, 1)
            make_a(pe, 2)
            g.next()
            for d in range(2):
                for n, v in enumerate((ecol, acol, bcol)):
                    mm = E.transpose(bank[0:20, (4, 5, 6)[n], d * P:(d + 1) * P], f2(v)[:, d, :], ident)
            mm.then_inc(tp_s, 1)
            g.next()
            for d in range(2):
                mm = E.matmul(bank[:, 7, d * 20:(d + 1) * 20], ones[0:20, :], dg[0:20, d, :], start=True, stop=True)
            mm.then_inc(tp_s, 1)
            make_a(pe, 2)
            g.next()
            for d in range(2):
                mm = E.matmul(bank[0:20, 4, d:d + 1], f2(ms)[0:1, d, :], ones[0:1, 0:1], start=True, stop=True)
            mm.then_inc(tp_s, 1)
            for c in range(NCH):
                for n, (buf, t0, cols) in enumerate(((qk, 4, pchunk(c)), (vo, 0, chunk(c)))):
                    if 2 * c + n >= 2:
                        pe.wait_ge(kvc_s, 2 * c + n - 1)
                    for h in range(4):
                        mm = E.transpose(bank[:, n, h * P:(h + 1) * P], buf[:, t0 + h, cols], ident)
                    mm.then_inc(kv_s, 1)
                make_a(pe, 1 if c < CT else 0)
            pe.wait_ge(kvc_s, 2 * NCH)
            g.next()
            for n, (c, d, k) in enumerate(order):
                if n:
                    pe.wait_ge(rd_s, n)
                    pe.wait_ge(q_s, n)
                for b, rows in ((0, rrow), (1, morow)):
                    for h in range(4):
                        sel = ident[0:20, c * 4 + h:c * 4 + h + 1].to_broadcast([20, P])
                        mm = E.matmul(bank[:, b, h * P:(h + 1) * P], sel, rows[0:20, d, :], start=True, stop=True)
                mm.then_inc(r_s, 1)
                if n:
                    pe.wait_ge(p_s, n)
                for h in range(4):
                    mm = E.matmul(bank[:, 2, h * P:(h + 1) * P], qk[:, 4 + h, pchunk(c)], qk[:, h, pchunk(c)],
                                  start=True, stop=True)
                pe.wait_ge(kw_s, n + 1)
                for h in range(4):
                    mm = E.matmul(bank[:, 5 + h // 2, (h % 2) * (P + 1):(h % 2 + 1) * (P + 1)], kw[:, h, :],
                                  vtok[:, c, h, :], start=True, stop=True)
                mm.then_inc(c_s, 1)
                make_b(pe, 1 if n > 2 else 0)
                pe.wait_ge(p_s, n + 1)
                for h in range(4):
                    E.matmul(bank[:, 3, h * P:(h + 1) * P], vtok[:, c, h, 0:P], pt[:, h, :], start=True, stop=False)
                    E.matmul(bank[:, 3, h * P:(h + 1) * P], Cst[:, d, h, 0:P], qw[:, h, :], start=False, stop=True)
                for h in range(4):
                    E.matmul(bank[:, 4, h * P:(h + 1) * P], ones, pt[:, h, :], start=True, stop=False)
                    mm = E.matmul(bank[:, 4, h * P:(h + 1) * P], Cst[:, d, h, P:P + 1].to_broadcast([P, P]), qw[:, h, :],
                                  start=False, stop=True)
                mm.then_inc(n_s, 1)
                make_b(pe, 3 if n == 2 else 2 if n > 2 else 0)
                if n == 1:
                    pe.wait_ge(co_s, 1)
                    E.transpose(bank[0:8, 7, 0:P], nout, ident).then_inc(kv_s, 1)

        def dve(dve):
            lv.done(V.tensor_scalar(gates[0:16, :], gates[0:16, :], small[0:16, 0:1], None, ALU.add))
            lv.done(V.tensor_scalar(work[0:16, 2, :], gates[0:16, :], -1.0, None, ALU.mult))
            lv.done(V.tensor_tensor(work[0:16, 0, :], work[0:16, 2, :], gates[0:16, :], ALU.max))
            dve.sem_inc(gl_s, 1)
            lv.done(V.tensor_scalar(work[0:16, 1, :], gates[0:16, :], 0.0, None, ALU.min))
            dve.wait_ge(ga_s, 1)
            lv.done(V.tensor_tensor(work[0:16, 1, :], work[0:16, 1, :], work[0:16, 0, :], ALU.subtract))
            dve.sem_inc(tc_s, 1)
            dve.wait_ge(tp_s, 1)
            lv.done(V.tensor_copy(gt[:, :, :], bank[:, 4, 0:80].rearrange("p (c r) -> p c r", r=16)))
            lv.done(V.tensor_copy(lt[:, :, :], bank[:, 5, 0:80].rearrange("p (c r) -> p c r", r=16)))
            dve.sem_inc(tc_s, 1)
            dve.wait_ge(tp_s, 2)
            lv.done(V.tensor_copy(f2(bcol), bank[:, 6, 0:40].rearrange("p (d x) -> p d x", d=2)))
            for d in range(2):
                lv.done(V.tensor_copy(tot[:, d, :, :], bank[:, 7, 0:40].rearrange("p (c r) -> p c r", r=8)[:, :, 4 * d:4 * d + 4]))
                lv.done(V.tensor_tensor(acol[:, d, :, :], gt[:, :, 4 * d:4 * d + 4], bcol[:, d, :, :], ALU.subtract))
            lv.done(V.tensor_tensor(f2(ecol), f2(acol), f2(tot), ALU.add))
            dve.sem_inc(tc_s, 1)
            dve.wait_ge(tp_s, 3)
            r2 = lambda b: bank[0:20, b, 0:2 * P].rearrange("p (d t) -> p d t", d=2)
            lv.done(V.tensor_copy(arow[0:20], r2(5)))
            lv.done(V.tensor_copy(brow[0:20], r2(6)))
            lv.done(V.tensor_reduce(mloc[0:20, :], r2(4), AX_X, ALU.max))
            for d in range(2):
                lv.done(V.tensor_scalar(dg[0:20, d, :], ident[0:20, 0:20], mloc[0:20, d:d + 1], None, ALU.mult))
            dve.sem_inc(tc_s, 1)
            dve.wait_ge(tp_s, 4)
            lv.done(V.tensor_copy(f2(ml), bank[:, 7, 0:40].rearrange("p (d x) -> p d x", d=2)))
            lv.done(V.memset(ms[:, :, CT, :], 0.0))
            for d in range(2):
                lv.done(V.tensor_copy(ms[:, d, 0 if d == 0 else CT - 1, :], small[:, 3 + 4 * d:7 + 4 * d]))
            for d in range(2):
                cs = [CT] + (list(range(CT)) if d == 0 else list(range(CT - 1, -1, -1)))
                for n, c in enumerate(cs):
                    lv.done(V.tensor_tensor(tt[:, d, c, :], tot[:, d, c, :], ms[:, d, c, :], ALU.add))
                    lv.done(V.tensor_tensor(me[:, d, c, :], tt[:, d, c, :], ml[:, d, c, :], ALU.max))
                    if 0 < n < CT:
                        lv.done(V.tensor_copy(ms[:, d, cs[n + 1], :], me[:, d, c, :]))
            dve.sem_inc(tc_s, 1)
            lv.done(V.tensor_tensor(f2(dec), f2(tt), f2(me), ALU.subtract))
            lv.done(V.tensor_tensor(f2(sc), f2(ml), f2(me), ALU.subtract))
            lv.done(V.tensor_tensor(f2(wcol), f2(ecol), f2(ml), ALU.subtract))
            dve.sem_inc(ex_s, 1)
            dve.wait_ge(tp_s, 5)
            lv.done(V.tensor_copy(msrow[0:20, :], bank[0:20, 4, 0:2]))
            lv.done(V.tensor_tensor_scan(rrow[0:20, 0, :], arow[0:20, 0, :], arow[0:20, 0, :], msrow[0:20, 0:1],
                                         ALU.max, ALU.max))
            lv.done(V.tensor_tensor_scan(rrow[0:20, 1, ::-1], arow[0:20, 1, ::-1], arow[0:20, 1, ::-1],
                                         msrow[0:20, 1:2], ALU.max, ALU.max))
            lv.done(V.tensor_tensor(morow[0:20], brow[0:20], rrow[0:20], ALU.add))
            lv.done(V.memset(vtok[:, :, :, P:P + 1], 1.0))
            for c in range(NCH):
                for n, buf in enumerate((ktok, vtok)):
                    dve.wait_ge(kv_s, 2 * c + n + 1)
                    V.tensor_copy(buf[:, c, :, 0:P], bank[:, n, :].rearrange("p (h t) -> p h t", h=4)).then_inc(kvc_s, 1)
            lv.done(V.memset(Cst[:, :, :, :], 0.0))
            end_a(dve)
            dve.wait_ge(ga_s, 2)
            dve.sem_inc(tc_s, 1)
            hb = lambda b: bank[:, b, :].rearrange("p (h t) -> p h t", h=4)
            mask = (upper, lower)
            for n, (c, d, k) in enumerate(order):
                lv.done(V.tensor_tensor(kw[:, :, :], ktok[:, c, :, :], wcol[:, d, c, :].unsqueeze(2).to_broadcast([P, 4, P]),
                                        ALU.mult))
                dve.sem_inc(kw_s, 1)
                dve.wait_ge(r_s, n + 1)
                if n:
                    dve.wait_ge(e_s, n)
                for h in range(4):
                    ins = V.tensor_scalar(tmp[:, h, :], bank[:, 0, h * P:(h + 1) * P], acol[:, d, c, h:h + 1], 0.0,
                                          ALU.subtract, ALU.max)
                ins.then_inc(rd_s, 1)
                dve.wait_ge(q_s, n + 1)
                lv.done(V.tensor_tensor(qw[:, :, :], qk[:, 0:4, pchunk(c)], wi[:, :, :], ALU.mult))
                dve.wait_ge(e_s, n + 1)
                lv.done(V.tensor_tensor(ee[:, :, :], ee[:, :, :], mask[d].unsqueeze(1).to_broadcast([P, 4, P]), ALU.mult))
                dve.wait_ge(c_s, n + 1)
                if n == 2:
                    dve.wait_ge(st_l, 32)
                lv.done(V.tensor_tensor(pt[:, :, :], ee[:, :, :], hb(2), ALU.mult))
                dve.sem_inc(p_s, 1)
                dve.wait_ge(n_s, n + 1)
                lv.done(V.tensor_scalar(nd[:, :, :], hb(4), -1.0, None, ALU.mult))
                lv.done(V.tensor_tensor(nd[:, :, :], nd[:, :, :], hb(4), ALU.max))
                lv.done(V.tensor_tensor(nd[:, :, :], nd[:, :, :], em[:, :, :], ALU.max))
                lv.done(V.reciprocal(nd[:, :, :], nd[:, :, :]))
                tgt = ha[:, :, chunk(c)]
                if (c, d) in seen_first(order):
                    lv.done(V.tensor_tensor(tgt, nd[:, :, :], hb(3), ALU.mult))
                else:
                    lv.done(V.tensor_tensor(nd[:, :, :], nd[:, :, :], hb(3), ALU.mult))
                    lv.done(V.tensor_tensor(tgt, tgt, nd[:, :, :], ALU.add))
                b4 = lambda v: v[:, d, c, :].unsqueeze(2).to_broadcast([P, 4, P + 1])
                for hh in range(2):
                    lv.done(V.tensor_tensor(ctmp[:, 2 * hh:2 * hh + 2, :],
                                            bank[:, 5 + hh, 0:2 * (P + 1)].rearrange("p (h t) -> p h t", h=2),
                                            sc[:, d, c, 2 * hh:2 * hh + 2].unsqueeze(2).to_broadcast([P, 2, P + 1]), ALU.mult))
                lv.done(V.tensor_tensor(Cst[:, d], Cst[:, d], b4(dec), ALU.mult))
                lv.done(V.tensor_tensor(Cst[:, d], Cst[:, d], ctmp[:, :, :], ALU.add))
                dve.sem_inc(st_s, 1)
                if n == 1:
                    for dd in range(2):
                        lv.done(V.tensor_copy(nout[:, 4 * dd:4 * dd + 4], Cst[:, dd, :, P]))
                    dve.sem_inc(co_s, 1)
                    dve.wait_ge(kv_s, 2 * NCH + 1)
                    lv.done(V.tensor_copy(noutT[0:8, :], bank[0:8, 7, 0:P]))
                    dve.sem_inc(no_s, 1)
                    dve.wait_ge(st_l, 32)
                    for dd in range(2):
                        lv.done(V.tensor_copy(Cst[:, dd, :, P], vec[:, V_N + 4 * dd:V_N + 4 * dd + 4]))
            end_b(dve)

        return pe, act, dve, fetches

    def seen_first(order):
        out, seen = set(), set()
        for c, d, _ in order:
            if c not in seen:
                seen.add(c)
                out.add((c, d))
        return out

    def stage_head_norm(y, onesm, n, eps, weight, bias, name, finish):
        s_s, x_s, v_s, r_s = (sem(f"{name}_{k}") for k in ("sum", "centred", "var", "root"))
        sq, rs = take(T), take(T)
        fetches, make, mod_end = mod_share(8, bank[:, 7, :])

        def pe(pe):
            for j in range(4):
                if j:
                    pe.wait_ge(x_s, 2 * j)
                for c in (LAT, CTX):
                    mm = E.matmul(pairs[0][:, c], onesm, y[:, j, c], start=True, stop=True)
                mm.then_inc(s_s, 1)
                make(pe, 1)
                pe.wait_ge(x_s, 2 * j + 1)
                for c in (LAT, CTX):
                    mm = E.matmul(pairs[1][:, c], onesm, sq[:, c], start=True, stop=True)
                mm.then_inc(v_s, 1)
                make(pe, 1)

        def act(act):
            for j in range(4):
                act.wait_ge(x_s, 2 * j + 2)
                A.activation(rs, rs, ACT.Sqrt).then_inc(r_s, 1)

        def dve(dve):
            for j in range(4):
                t = y[:, j, :]
                dve.wait_ge(s_s, j + 1)
                lv.done(V.scalar_tensor_tensor(t, pairs[0][:, 0:T], -1.0 / n, t, ALU.mult, ALU.add))
                lv.done(V.tensor_tensor(sq, t, t, ALU.mult))
                dve.sem_inc(x_s, 1)
                dve.wait_ge(v_s, j + 1)
                lv.done(V.tensor_scalar(rs, pairs[1][:, 0:T], 1.0 / n, eps, ALU.mult, ALU.add))
                dve.sem_inc(x_s, 1)
                dve.wait_ge(r_s, j + 1)
                lv.done(V.reciprocal(rs, rs))
                lv.done(V.scalar_tensor_tensor(t, t, weight[:, j:j + 1], rs, ALU.mult, ALU.mult))
                if bias is not None:
                    lv.done(V.tensor_scalar(t, t, bias[:, j:j + 1], None, ALU.add))
                finish(dve, j)
            mod_end(dve)

        return pe, act, dve, fetches

    def finish_mlstm(ha, vo):
        return lambda dve, j: lv.done(V.tensor_tensor(ha[:, j, :], ha[:, j, :], vo[:, 4 + j, :], ALU.mult))

    def stage_rwkv_in(pb, kk, av, ld, cum):
        wup, aup = take(512), take(512)
        tmp = take(2, T)
        p_s, c_s, n_s, t_s, l_s = (sem(f"ri_{k}") for k in ("products", "copied", "norm", "exp", "weights"))
        pad2 = ((LAT, PLAT), (CTX, PCTX))
        fetches, make, mod_end = mod_share(8, bank[:, 7, :])

        def act(act):
            act.dma_start(wup, a["ev_b_w_up"][0].rearrange("d r n -> (d r) n")).then_inc(l_s, 16)
            act.dma_start(aup[0:64, :], a["ev_b_a_up"][0]).then_inc(l_s, 16)
            A.activation(pb[:, 12, 1:643], pb[:, 12, 1:643], ACT.Tanh)
            A.activation(pb[:, 13, 1:643], pb[:, 13, 1:643], ACT.Sigmoid).then_inc(t_s, 1)
            n = 0
            for j in range(4):
                for kind in range(3):
                    act.wait_ge(p_s, n + 1)
                    src = pair[n % 2][:, 0:T]
                    if kind == 0:
                        ins = A.activation(av[:, j, :], src, ACT.Sigmoid, bias=col(V_A0 + j))
                    else:
                        ins = A.activation(ld[:, kind - 1, j, :], src, ACT.Sigmoid, bias=col(V_W0 + 4 * (kind - 1) + j))
                    ins.then_inc(c_s, 1)
                    n += 1
            for j in range(4):
                act.wait_ge(n_s, 2 * j + 2)
                A.activation(tmp[:, 1, :], tmp[:, 1, :], ACT.Sqrt).then_inc(t_s, 1)

        def pe(pe):
            pe.wait_ge(l_s, 32)
            pe.wait_ge(t_s, 1)
            n = 0
            for j in range(4):
                for kind in range(3):
                    if n >= 2:
                        pe.wait_ge(c_s, n - 1)
                    w = (aup[0:64], wup[0:64], wup[64:128])[kind][:, j * P:(j + 1) * P]
                    r = (pb[0:64, 14], pb[0:64, 12], pb[64:128, 12])[kind]
                    for c, pc in pad2:
                        mm = E.matmul(pair[n % 2][:, c], w, r[:, pc], start=True, stop=True)
                    mm.then_inc(p_s, 1)
                    n += 1
            for j in range(4):
                pe.wait_ge(n_s, 2 * j + 1)
                for c in (LAT, CTX):
                    mm = E.matmul(pairs[2][:, c], blk, tmp[:, 0, c], start=True, stop=True)
                mm.then_inc(p_s, 1)
                make(pe, 2)

        def dve(dve):
            for j in range(4):
                for c, pc in pad2:
                    lv.done(V.tensor_scalar(kk[:, j, c], pb[:, 4 + j, pc], col(V_KK + j), None, ALU.mult))
                lv.done(V.tensor_tensor(tmp[:, 0, :], kk[:, j, :], kk[:, j, :], ALU.mult))
                dve.sem_inc(n_s, 1)
                dve.wait_ge(p_s, 12 + j + 1)
                lv.done(V.tensor_copy(tmp[:, 1, :], pairs[2][:, 0:T]))
                dve.sem_inc(n_s, 1)
                dve.wait_ge(t_s, j + 2)
                lv.done(V.tensor_scalar(tmp[:, 1, :], tmp[:, 1, :], 1e-12, None, ALU.max))
                lv.done(V.reciprocal(tmp[:, 1, :], tmp[:, 1, :]))
                lv.done(V.tensor_tensor(kk[:, j, :], kk[:, j, :], tmp[:, 1, :], ALU.mult))
            dve.wait_ge(c_s, 12)
            for j in range(4):
                lv.done(V.tensor_scalar(tmp[:, 0, :], av[:, j, :], -1.0, col(V_KA + j), ALU.add, ALU.mult))
                for c, pc in pad2:
                    lv.done(V.scalar_tensor_tensor(pb[:, 4 + j, pc], tmp[:, 0, c], 1.0, pb[:, 4 + j, pc],
                                                   ALU.add, ALU.mult))
                lv.done(V.tensor_tensor(av[:, j, :], av[:, j, :], kk[:, j, :], ALU.mult))
                for d in range(2):
                    lv.done(V.tensor_scalar(ld[:, d, j, :], ld[:, d, j, :], -DECAY, None, ALU.mult))
                    lv.done(V.tensor_tensor_scan(cum[:, d, j, :], rst, ld[:, d, j, :], 0.0, ALU.mult, ALU.add))
                c64 = lambda v: v[:, 1, j, :].rearrange("p (c t) -> p c t", t=R64)
                end = c64(cum)[:, :, R64 - 1:R64]
                lv.done(V.tensor_copy(tmp[:, 0, 0:10].unsqueeze(2), end))
                lv.done(V.tensor_tensor(cum[:, 1, j, :], ld[:, 1, j, :], cum[:, 1, j, :], ALU.subtract))
                lv.done(V.tensor_tensor(c64(cum), c64(cum), tmp[:, 0, 0:10].unsqueeze(2).to_broadcast([P, 10, R64]), ALU.add))
                for d in range(2):
                    lv.done(V.tensor_tensor(ld[:, d, j, :], cum[:, d, j, :], ld[:, d, j, :], ALU.subtract))
            mod_end(dve)

        return pe, act, dve, fetches

    def stage_rwkv(pb, kk, av, ex, cum, y, out_s):
        pri = take(2, 4, 3 * R64)
        bb, kb = take(2, 4, R64), take(2, 4, R64)
        e4 = lambda v: v.rearrange("p (d j t) -> p d j t", d=2, j=4)
        e1, e2, e3 = e4(pb[:, 12, 0:512]), e4(pb[:, 14, 0:512]), e4(rstd[:, 0:512])
        gb, gk = take(2, 4, 3 * R64), take(2, 4, 3 * R64)
        vt = take(2, 4, R64)
        et = take(2, 4, R64)
        M, MT, W = (take(2, 4, R64) for _ in range(3))
        Z, U = W, et
        S = take(2, 4, R64)
        dend = take(2, 4)
        sin = pri[:, :, :, 0:R64]
        two = lambda name: [sem(f"rw_{name}_{d}") for d in "fb"]
        ex_s, x_s = two("exp"), two("factors")
        g_s, gc_s, lw_s, lc_s, sq_s, sc_s = (two(k) for k in (
            "grams", "grams_copied", "level", "level_copied", "seq", "seq_copied"))
        wc_s = two("w_copied")
        ld_s, io_s = sem("rw_state_in"), sem("rw_state_turned")
        hp = (slice(0, 64), slice(64, 128))
        js = range(4)
        flat = lambda v: v.rearrange("p j t -> p (j t)")
        steps = [(8, 9)] + [(9, 8)] + [(k, 7 - k) for k in range(8)]
        def gcol(d, j):
            return bank[:, 4 * d + j // 2, (j % 2) * 192:(j % 2) * 192 + 192]
        def vcol(d, j):
            return bank[:, 4 * d + j // 2, 384 + (j % 2) * 64:384 + (j % 2) * 64 + 64]
        wb = [bank[:, 4 * d + 2, 0:256].rearrange("p (j t) -> p j t", j=4) for d in range(2)]
        xb = [bank[:, 4 * d + 3, :].rearrange("p (m j t) -> p m j t", m=2, j=4) for d in range(2)]

        def products(out, lhs, rhs):
            for h in hp:
                for j in js:
                    mm = E.matmul(out[h, j, :], lhs[h, j, :], rhs[h, j, :], start=True, stop=True)
            return mm

        def act(act):
            for dd in range(2):
                for e in range(2):
                    act.dma_start(sin[e * 64:e * 64 + 64, dd], a["state_rwkv"][0, 0, dd].rearrange(
                        "(j e) v k -> e v j k", e=2)[e]).then_inc(ld_s, 16)

            def exps(n, d):
                t = slice(steps[n][d] * R64, steps[n][d] * R64 + R64)
                A.activation(e1[:, d], ex[:, d, :, t], ACT.Exp)
                A.activation(e2[:, d], cum[:, d, :, t], ACT.Exp)
                A.activation(e3[:, d], cum[:, d, :, t], ACT.Exp, scale=-1.0).then_inc(ex_s[d], 1)
            for d in range(2):
                exps(0, d)
            for n in range(len(steps)):
                for l in range(1, 6):
                    for d in range(2):
                        if l == 1 and n + 1 < len(steps):
                            act.wait_ge(x_s[d], n + 1)
                            exps(n + 1, d)
                        act.wait_ge(lw_s[d], 10 * n + 2 * l - 1)
                        A.activation(W[:, d], wb[d], ACT.Copy).then_inc(wc_s[d], 1)
                if n == 1:
                    for dd in range(2):
                        act.wait_ge(sc_s[dd], 4 * 2 + 2)
                        for e in range(2):
                            store(out_s[0, 0, dd].rearrange("(j e) v k -> e v j k", e=2)[e],
                                  U[e * 64:e * 64 + 64, dd])
                    act.wait_ge(stored, 16 * nstores[0])
                    act.sem_inc(ld_s, 1)

        def pe(pe):
            pe.wait_ge(ld_s, 64)
            for d in range(2):
                for h in hp:
                    for j in js:
                        mm = E.matmul(wb[d][h, j, :], sin[h, d, j, :], i64[h, :], start=True, stop=True)
            mm.then_inc(io_s, 1)
            for n, cc in enumerate(steps):
                more = 1 if n > 1 else 0
                for d in range(2):
                    if n == 0:
                        pe.wait_ge(sc_s[d], 1)
                    pe.wait_ge(x_s[d], n + 1)
                    for h in hp:
                        for j in js:
                            E.matmul(vcol(d, j)[h], pb[h, 8 + j, p64(cc[d])], i64[h, :], start=True, stop=True)
                            mm = E.matmul(gcol(d, j)[h], bb[h, d, j, :], pri[h, d, j, :], start=True, stop=True)
                    mm.then_inc(g_s[d], 1)
                for d in range(2):
                    pe.wait_ge(gc_s[d], 2 * n + 1)
                    for h in hp:
                        for j in js:
                            mm = E.matmul(gcol(d, j)[h], kb[h, d, j, :], pri[h, d, j, :], start=True, stop=True)
                    mm.then_inc(g_s[d], 1)
                for l in range(1, 6):
                    for d in range(2):
                        pe.wait_ge(lc_s[d], 10 * n + max(2 * l - 2, 1))
                        products(wb[d], et[:, d], M[:, d]).then_inc(lw_s[d], 1)
                    for d in range(2):
                        pe.wait_ge(wc_s[d], 5 * n + l)
                        pe.wait_ge(lc_s[d], 10 * n + 2 * l - 1)
                        if l < 5:
                            products(xb[d][:, 0], MT[:, d], W[:, d]).then_inc(lw_s[d], 1)
                        else:
                            products(xb[d][:, 1], W[:, d], MT[:, d]).then_inc(lw_s[d], 1)
                for d in range(2):
                    pe.wait_ge(lc_s[d], 10 * n + 10)
                    pe.wait_ge(gc_s[d], 2 * n + 2)
                    for h in hp:
                        for j in js:
                            E.matmul(wb[d][h, j, :], pri[h, d, j, 0:64], S[h, d, j, :], start=True, stop=False)
                            mm = E.matmul(wb[d][h, j, :], gk[h, d, j, 0:64], vt[h, d, j, :], start=False, stop=True)
                    mm.then_inc(sq_s[d], 1)
                for d in range(2):
                    pe.wait_ge(sc_s[d], 4 * n + 2 + more)
                    products(wb[d], MT[:, d], Z[:, d]).then_inc(sq_s[d], 1)
                for d in range(2):
                    pe.wait_ge(sc_s[d], 4 * n + 3 + more)
                    for h in hp:
                        for j in js:
                            o = xb[d][h, 0, j, :]
                            E.matmul(o, gk[h, d, j, 128:192], vt[h, d, j, :], start=True, stop=False)
                            E.matmul(o, gb[h, d, j, 128:192], U[h, d, j, :], start=False, stop=True)
                            o = xb[d][h, 1, j, :]
                            E.matmul(o, S[h, d, j, :], pri[h, d, j, 64:128], start=True, stop=False)
                            E.matmul(o, vt[h, d, j, :], gk[h, d, j, 64:128], start=False, stop=False)
                            mm = E.matmul(o, U[h, d, j, :], gb[h, d, j, 64:128], start=False, stop=True)
                    mm.then_inc(sq_s[d], 1)
                if n == 1:
                    for d in range(2):
                        pe.wait_ge(sc_s[d], 4 * n + 5)
                        for h in hp:
                            for j in js:
                                mm = E.matmul(wb[d][h, j, :], S[h, d, j, :], i64[h, :], start=True, stop=True)
                    mm.then_inc(io_s, 1)

        def dve(dve):
            dve.wait_ge(io_s, 1)
            sav = rwkv_saved
            for d in range(2):
                lv.done(V.tensor_copy(sav[:, d], wb[d]))
                lv.done(V.memset(flat(S[:, d]), 0.0))
                lv.done(V.tensor_copy(pri[:, d, :, 128:192], i64.unsqueeze(1).to_broadcast([P, 4, R64])))
                dve.sem_inc(sc_s[d], 1)
            seen = set()
            ib = i64.unsqueeze(1).to_broadcast([P, 4, R64])

            def factors(n, d):
                c = steps[n][d]
                t, tp = slice(c * R64, c * R64 + R64), p64(c)
                e = R64 - 1 if d == 0 else 0
                dve.wait_ge(ex_s[d], n + 1)
                V.tensor_tensor(pri[:, d, :, 0:64], e1[:, d], kk[:, :, t], ALU.mult)
                V.tensor_tensor(bb[:, d], e3[:, d], av[:, :, t], ALU.mult)
                V.tensor_tensor(pri[:, d, :, 64:128], e2[:, d], pb[:, 0:4, tp], ALU.mult)
                V.tensor_tensor(kb[:, d], e3[:, d], pb[:, 4:8, tp], ALU.mult)
                V.tensor_copy(dend[:, d, :].unsqueeze(2), e2[:, d, :, e:e + 1]).then_inc(x_s[d], 1)

            def grams(dst, d, v):
                for half in range(2):
                    src = bank[:, d * 4 + half, 0:384].rearrange("p (j m t) -> p j m t", j=2, m=3)
                    V.tensor_tensor(dst[:, d, 2 * half:2 * half + 2, 0:128].rearrange("p j (m t) -> p j m t", m=2),
                                    src[:, :, 0:2, :], mk[:, d, :, :].unsqueeze(1).to_broadcast([P, 2, 2, R64]), ALU.mult)
                    if v:
                        V.tensor_copy(vt[:, d, 2 * half:2 * half + 2, :],
                                      bank[:, d * 4 + half, 384:512].rearrange("p (j t) -> p j t", j=2))
                    ins = V.tensor_copy(dst[:, d, 2 * half:2 * half + 2, 128:192], src[:, :, 2, :])
                return ins

            def level(d, l):
                return V.tensor_tensor(et[:, d], gb[:, d, :, 0:64],
                                       lvl[:, d, l, :].unsqueeze(1).to_broadcast([P, 4, R64]), ALU.mult)

            for d in range(2):
                factors(0, d)
            for n, cc in enumerate(steps):
                for d in range(2):
                    dve.wait_ge(g_s[d], 2 * n + 1)
                    grams(gb, d, True).then_inc(gc_s[d], 1)
                    dve.wait_ge(gc_s[d], 2 * n + 1)
                    lv.done(level(d, 0))
                    lv.done(V.tensor_tensor(MT[:, d], ib, et[:, d], ALU.subtract))
                    V.transpose(flat(M[:, d]), flat(MT[:, d]))
                    level(d, 1).then_inc(lc_s[d], 1)
                for d in range(2):
                    dve.wait_ge(g_s[d], 2 * n + 2)
                    grams(gk, d, False).then_inc(gc_s[d], 1)
                for l in range(1, 6):
                    for d in range(2):
                        dve.wait_ge(lw_s[d], 10 * n + 2 * l)
                        dve.wait_ge(lc_s[d], 10 * n + 2 * l - 1)
                        if l < 5:
                            V.tensor_tensor(M[:, d], M[:, d], xb[d][:, 0], ALU.subtract)
                            level(d, l + 1).then_inc(lc_s[d], 1)
                            dve.wait_ge(lc_s[d], 10 * n + 2 * l)
                            V.transpose(flat(MT[:, d]), flat(M[:, d])).then_inc(lc_s[d], 1)
                        else:
                            V.tensor_tensor(MT[:, d], MT[:, d], xb[d][:, 1], ALU.subtract).then_inc(lc_s[d], 1)
                for d in range(2):
                    dve.wait_ge(sq_s[d], 3 * n + 1)
                    V.tensor_copy(Z[:, d], wb[d]).then_inc(sc_s[d], 1)
                for d in range(2):
                    dve.wait_ge(sq_s[d], 3 * n + 2)
                    V.tensor_scalar(U[:, d], wb[d], -1.0, None, ALU.mult).then_inc(sc_s[d], 1)
                for d in range(2):
                    dve.wait_ge(sq_s[d], 3 * n + 3)
                    if n == 1:
                        dve.wait_ge(sc_s[d], 4 * n + 3)
                    lv.done(V.tensor_tensor(S[:, d], S[:, d], xb[d][:, 0], ALU.add))
                    V.tensor_tensor(S[:, d], S[:, d], dend[:, d, :].unsqueeze(2).to_broadcast([P, 4, R64]),
                                    ALU.mult).then_inc(sc_s[d], 1)
                    t = slice(cc[d] * R64, cc[d] * R64 + R64)
                    if cc[d] in seen:
                        V.tensor_tensor(y[:, :, t], y[:, :, t], xb[d][:, 1], ALU.add).then_inc(sc_s[d], 1)
                    else:
                        V.tensor_copy(y[:, :, t], xb[d][:, 1]).then_inc(sc_s[d], 1)
                        seen.add(cc[d])
                    if n + 1 < len(steps):
                        dve.wait_ge(sc_s[d], 4 * n + 5 + (1 if n > 1 else 0))
                        factors(n + 1, d)
                if n == 1:
                    dve.wait_ge(io_s, 2)
                    for d in range(2):
                        lv.done(V.tensor_copy(U[:, d], wb[d]))
                        lv.done(V.tensor_copy(S[:, d], sav[:, d]))
                        dve.sem_inc(sc_s[d], 1)
                    dve.wait_ge(ld_s, 65)

        return pe, act, dve

    rwkv_saved = sb("rwkv_saved", [P, 2, 4, R64])

    def stage_rwkv_out(pb, y):
        gup, u, tmp, t2 = take(512), take(4), take(2, PAD), take(T)
        l_s, t_s, p_s, d_s = (sem(f"ro_{k}") for k in ("weights", "products_in", "products", "read"))
        fetches, make, mod_end = mod_share(8, bank[:, 7, :])

        def act(act):
            act.dma_start(gup, a["ev_b_g_up"][0]).then_inc(l_s, 16)

        def pe(pe):
            pe.wait_ge(l_s, 16)
            for j in range(4):
                if j:
                    pe.wait_ge(d_s, j)
                pe.wait_ge(t_s, j + 1)
                for c, pc in ((LAT, PLAT), (CTX, PCTX)):
                    E.matmul(pairs[0][:, c], blk, tmp[:, j % 2, pc], start=True, stop=True)
                    mm = E.matmul(pairs[1][:, c], gup[:, j * P:(j + 1) * P], pb[:, 13, pc], start=True, stop=True)
                mm.then_inc(p_s, 1)
                make(pe, 2)

        def dve(dve):
            lv.done(V.tensor_tensor(u, vec[:, V_U:V_U + 4], vec[:, V_U + 4:V_U + 8], ALU.add))
            for j in range(4):
                w = tmp[:, j % 2, 1:643]
                lv.done(V.tensor_scalar(w, pb[:, j, 1:643], u[:, j:j + 1], None, ALU.mult))
                lv.done(V.tensor_tensor(w, w, pb[:, 4 + j, 1:643], ALU.mult))
                dve.sem_inc(t_s, 1)
                dve.wait_ge(p_s, j + 1)
                for c, pc in ((LAT, PLAT), (CTX, PCTX)):
                    lv.done(V.tensor_tensor(t2[:, c], pb[:, 8 + j, pc], pairs[0][:, c], ALU.mult))
                lv.done(V.tensor_tensor(y[:, j, :], y[:, j, :], t2, ALU.add))
                lv.done(V.tensor_tensor(y[:, j, :], y[:, j, :], pairs[1][:, 0:T], ALU.mult))
                dve.sem_inc(d_s, 1)
            mod_end(dve)

        return pe, act, dve, fetches

    def stage_out(rhs, w, split, gate_at):
        per = {1: 4, 2: 2, 3: 4}[len(split)]
        nu = per * len(split)
        u0, v0 = unit0[0], out0[0]
        unit0[0] += 8 * len(split)
        out0[0] += 8
        wv = w.rearrange("(k p) n -> p k n", p=P)
        k0 = [sum(split[:n]) for n in range(len(split))]

        def fetches(sp):
            with sp.Fori(0, 8 // per) as i:
                for n in range(nu):
                    o, m = n // len(split), n % len(split)
                    fetch(sp, n % 4, i * (nu // 4) + (u0 // 4 + n // 4),
                          wv[:, k0[m]:k0[m] + split[m], bass.ds(i * (per * P) + o * P, P)], split[m], P)

        def pe(pe):
            with pe.Fori(0, 8 // per) as i:
                for n in range(nu):
                    o, m = n // len(split), n % len(split)
                    unit(n % 4, i * (nu // 4) + (u0 // 4 + n // 4), o % 2, i * (per // 2) + (v0 // 2 + o // 2),
                         rhs[:, k0[m]:k0[m] + split[m], :], split[m], P, m == 0, m == len(split) - 1)

        def dve(dve):
            with turns(dve, 8 // per, []) as i:
                for o in range(per):
                    n = o * len(split) + len(split) - 1
                    unit_wait(dve, i * (nu // 4) + (u0 // 4 + n // 4), n % 4)
                    for s, c in ((1, LAT), (0, CTX)):
                        xt = x[:, bass.ds(i * per + o, 1), c].rearrange("p o t -> p (o t)")
                        g = mod[:, bass.ds(i * per + (gate_at + o), 1), s:s + 1].rearrange("p o t -> p (o t)")
                        ins = V.scalar_tensor_tensor(xt, pair[o % 2][:, c], g, xt, ALU.mult, ALU.add)
                    ins.then_inc(psum_free[o % 2], 1)

        return pe, (lambda act: None), dve, fetches

    def stage_ffn_in(h, hid, w, name):
        assert top[0] + 2 * T <= NAR - NSPLIT
        gs = take(2, T)
        g_s, f_s = sem(f"{name}_gate_silu"), sem(f"{name}_hidden")
        hh_s, hl_s = sem(f"{name}_h_high"), sem(f"{name}_h_low")
        wh_s, wl_s = sem(f"{name}_w_high"), sem(f"{name}_w_low")
        u0, v0 = unit0[0], out0[0]
        unit0[0] += 2 * KF
        out0[0] += 2 * KF
        wv = w.rearrange("(k p) n -> p k n", p=P)
        turns_n = KF // 2

        def fetches(sp):
            with sp.Fori(0, turns_n) as i:
                for s in range(4):
                    fetch(sp, s, i + u0 // 4, wv[:, :, bass.ds(i * (2 * P) + ((s // 2) * P + (s % 2) * FFN), P)], KD, P)

        def pe(pe):
            pe.wait_ge(hl_s, KD)
            with pe.Fori(0, turns_n) as i:
                for s in range(4):
                    unit_split(s, s, s % 2, h, i * 2 + (v0 // 2 + s // 2), (wl_s, i * 4 + (s + 1)))

        def over_turns(eng, turn):
            with eng.Fori(0, turns_n - 1) as i:
                turn(i, True)
            turn(turns_n - 1, False)

        def act(act):
            def high(i, s):
                act.wait_ge(w_ready[s], i * 16 + (u0 // 4 * 16 + 16))
                act.wait_ge(unit_done, i * 4 + (u0 + s + 1))
                high_of(s, s).then_inc(wh_s, 1)

            def turn(i, more):
                for m in range(2):
                    unit_wait(act, i + u0 // 4, 2 * m)
                    act.wait_ge(f_s, i * 2 + (m + 1))
                    A.activation(gs[:, m, :], pair[0][:, 0:T], ACT.Silu).then_inc(psum_free[0], 1)
                    act.drain().then_inc(g_s, 1)
                    if more:
                        high(i + 1, 2 * m)
                        high(i + 1, 2 * m + 1)

            high_of_rhs(h, hh_s)
            for s in range(4):
                high(0, s)
            over_turns(act, turn)

        def dve(dve):
            def low(i, s):
                dve.wait_ge(wh_s, i * 4 + (s + 1))
                low_of(s, s).then_inc(wl_s, 1)

            def turn(i, more):
                for m in range(2):
                    unit_wait(dve, i + u0 // 4, 2 * m + 1)
                    dve.wait_ge(g_s, i * 2 + (m + 1))
                    t = hid[:, bass.ds(i * 2 + m, 1), :].rearrange("p o t -> p (o t)")
                    V.tensor_tensor(t, gs[:, m, :], pair[1][:, 0:T], ALU.mult).then_inc(psum_free[1], 1)
                    dve.drain().then_inc(f_s, 1)
                    if more:
                        low(i + 1, 2 * m)
                        low(i + 1, 2 * m + 1)

            dve.sem_inc(f_s, 2)
            low_of_rhs(dve, h, hh_s, hl_s)
            for s in range(4):
                low(0, s)
            over_turns(dve, turn)

        return pe, act, dve, fetches

    def log1p(u, z, q, acc):
        lv.done(V.tensor_scalar(z, u, 2.0, None, ALU.add))
        lv.done(V.reciprocal(z, z))
        lv.done(V.tensor_tensor(z, z, u, ALU.mult))
        lv.done(V.tensor_tensor(q, z, z, ALU.mult))
        lv.done(V.tensor_scalar(acc, q, 1.0 / 17, None, ALU.mult))
        for n in range(15, 1, -2):
            lv.done(V.scalar_tensor_tensor(acc, acc, 1.0 / n, q, ALU.add, ALU.mult))
        lv.done(V.scalar_tensor_tensor(acc, acc, 1.0, z, ALU.add, ALU.mult))
        lv.done(V.tensor_scalar(acc, acc, 2.0, None, ALU.mult))

    def stage_dt(h, dtc, cumc, dece, cdec, scratch):
        wd = take(KD, 64)
        r = take(6, T)
        crow = take(T)
        dac = take(NCH, 64)
        tot = take(NCH, 64)
        l_s, p_s, v_s, e_s = (sem(f"dt_{k}") for k in ("weights", "products", "steps", "exp"))

        def act(act):
            act.dma_start(wd[:, :, :], a["od_w_in"][0].rearrange("(k p) n -> p k n", p=P)[:, :, 6144:6208]).then_inc(l_s, 16)
            A.activation(small[0:64, 11:12], small[0:64, 2:3], ACT.Exp)
            act.wait_ge(v_s, 1)
            A.activation(r[0:64, 1, :], r[0:64, 1, :], ACT.Exp, scale=-1.0).then_inc(e_s, 1)
            act.wait_ge(v_s, 4)
            act.dma_start(scratch[:, :], crow[0:64, :]).then_inc(l_s, 16)
            act.wait_ge(v_s, 5)
            A.activation(dece[:, :, :], dece[:, :, :], ACT.Exp)
            A.activation(cdec[:, :, :], tot[:, :, :], ACT.Exp)
            act.wait_ge(l_s, 32)

        def pe(pe):
            pe.wait_ge(l_s, 16)
            for k in range(KD):
                E.matmul(pairs[0][0:64, LAT], wd[:, k, :], h[:, k, LAT], start=(k == 0), stop=(k == KD - 1))
                mm = E.matmul(pairs[0][0:64, CTX], wd[:, k, :], h[:, k, CTX], start=(k == 0), stop=(k == KD - 1))
            mm.then_inc(p_s, 1)
            pe.wait_ge(v_s, 2)
            for c in range(NCH):
                E.transpose(bank[:, 2, c * 64:(c + 1) * 64], r[0:64, 0, chunk(c)], ident[0:64, 0:64])
                mm = E.transpose(bank[:, 3, c * 64:(c + 1) * 64], r[0:64, 2, chunk(c)], ident[0:64, 0:64])
            mm.then_inc(p_s, 1)
            pe.wait_ge(v_s, 3)
            for c in range(NCH):
                for d, tri in enumerate((upper, lower)):
                    mm = E.matmul(pairs[2][32 * d:32 * d + 32, chunk(c)], dac[:, c, 32 * d:32 * d + 32], tri, start=True, stop=True)
            E.matmul(bank[:, 6, 0:320], ones, dac.rearrange("p c r -> p (c r)"), start=True, stop=True).then_inc(p_s, 1)
            pe.wait_ge(v_s, 4)
            for c in range(NCH):
                mm = E.transpose(bank[:, 7, c * 64:(c + 1) * 64], crow[0:64, chunk(c)], ident[0:64, 0:64])
            mm.then_inc(p_s, 1)

        def dve(dve):
            R = lambda n: r[0:64, n, :]
            dve.wait_ge(p_s, 1)
            lv.done(V.tensor_scalar(R(0), pairs[0][0:64, 0:T], small[0:64, 1:2], None, ALU.add))
            lv.done(V.tensor_scalar(R(1), R(0), -1.0, None, ALU.mult))
            lv.done(V.tensor_tensor(R(1), R(1), R(0), ALU.max))
            dve.sem_inc(v_s, 1)
            dve.wait_ge(e_s, 1)
            log1p(R(1), R(3), R(4), R(5))
            lv.done(V.scalar_tensor_tensor(R(0), R(0), 0.0, R(5), ALU.max, ALU.add))
            lv.done(V.tensor_scalar(R(2), R(0), small[0:64, 11:12], -1.0, ALU.mult, ALU.mult))
            dve.sem_inc(v_s, 1)
            dve.wait_ge(p_s, 2)
            c5 = lambda b: bank[:, b, 0:320].rearrange("p (c r) -> p c r", r=64)
            lv.done(V.tensor_copy(dtc[:, :, :], c5(2)))
            lv.done(V.tensor_copy(dac[:, :, :], c5(3)))
            dve.sem_inc(v_s, 1)
            dve.wait_ge(p_s, 3)
            lv.done(V.tensor_copy(crow[0:64, :], pairs[2][0:64, 0:T]))
            lv.done(V.tensor_copy(tot[:, :, :], c5(6)))
            dve.sem_inc(v_s, 1)
            dve.wait_ge(p_s, 4)
            lv.done(V.tensor_copy(cumc[:, :, :], c5(7)))
            lv.done(V.tensor_tensor(dece[:, :, :], tot[:, :, :], cumc[:, :, :], ALU.subtract))
            dve.sem_inc(v_s, 1)

        return pe, act, dve

    def stage_ssd(h, yb, dtc, cumc, dece, cdec, scratch, dsk, out_s):
        raw = take(4, PAD)
        tmp = take(2, PAD)
        zb = [take(2, T) for _ in range(2)]
        xc = [take(4, T) for _ in range(2)]
        xt = take(NCH, 3 * P)
        cumb = [take(4, P) for _ in range(4)]
        ee, cw = ([take(4, P) for _ in range(2)] for _ in range(2))
        dx, dxw = ([take(4, 64) for _ in range(2)] for _ in range(2))
        cbm = take(2, NCH, P)
        S, sfin = take(2, 256), take(2, 256)
        sin, so = take(2, 2, P), take(2, 2, P)
        (si_s, rw_s, cv_s, sl_s, tu_s, tc_s, ar_s, ex_s, wt_s, pr_s, us_s, st_s, sc_s, cb_s, cc_s, sf_s, ft_s, fc_s,
         so_s, z_s) = (sem(f"ssd_{n}") for n in (
             "state_in", "raw", "convolved", "silu", "turned", "turned_copied", "arg", "exp", "weighted", "products",
             "step_done", "state_turned", "state_copied", "cb", "cb_copied", "final_state", "final_turned",
             "final_copied", "state_out", "gated"))
        ci_s = [sem(f"ssd_cum_in{n}") for n in range(4)]
        u0, v0 = unit0[0], out0[0]
        unit0[0] += 48
        out0[0] += 48
        w = a["od_w_in"][0].rearrange("(k p) n -> p k n", p=P)
        order = [(CT, 0), (CT, 1)] + [(c if d == 0 else CT - 1 - c, d) for c in range(CT) for d in range(2)]
        NS = len(order)
        first = set()
        seen = set()
        for c, d in order:
            if c not in seen:
                seen.add(c)
                first.add((c, d))
        cols = ((2048, 256), (2048 + P, 256), (4096, P), (5120, P), (0, 256), (P, 256))
        halves = (2, 2, 1, 1, 1, 1, 1, 1, 1, 1)
        evac_at = {0: [0], 1: [1], 3: [2], 5: [3], 7: [4], 9: [5]}
        conv_at = {1: 0, 2: 1, 4: 2, 6: 3}
        silu_at = {3: (0, 1), 7: (2, 3)}

        def at(g, k, c=0):
            i, b = g
            return k * b + c if i is None else i * (2 * k) + (k * b + c)

        par = lambda g: g[1] % 2
        nxt = lambda g: (g[0], g[1] + 1)

        def slot_of(g, m):
            n = 6 * g[1] + m
            return n % 4

        def q_of(g, m):
            n = 6 * g[1] + m
            return n // 4 + u0 // 4 if g[0] is None else g[0] * 3 + (n // 4 + u0 // 4)

        def fetches(sp):
            def group(g):
                for m in range(6):
                    b, st = cols[m]
                    fetch(sp, slot_of(g, m), q_of(g, m), w[:, :, bass.ds(at(g, st, b), P)], KD, P)
            group((None, 0))
            with sp.Fori(0, 3) as i:
                group((i, 1))
                group((i, 2))
            group((None, 7))

        def over_groups(eng, counts, head, body, tail):
            head()
            with turns(eng, 3, counts) as i:
                for j in range(2):
                    body((i, j), True)
            body((None, 6), True)
            body((None, 7), False)

        def hs(v, g, c, d):
            return v[:, c, bass.ds(at(g, 4, 32 * d), 4)]

        def act(act):
            cs_d = scratch.rearrange("(d g h) t -> d g h t", d=2, g=NG)
            st_d = a["state_ssd"][0, 0].rearrange("d (g a e) p n -> d g (e p) a n", g=NG, a=2)
            so_d = out_s[0, 0].rearrange("d (g a e) p n -> d g (e p) a n", g=NG, a=2)

            def load_cum(g, n):
                c, d = order[n]
                k = 10 * g[1] + n
                act.dma_start(cumb[k % 4][:, :, :],
                              cs_d[d, bass.ds(at(g, 1), 1), :, chunk(c)].rearrange("g h t -> (g h) t").partition_broadcast(P)
                              ).then_inc(ci_s[k % 4], 16)

            def load_state(g):
                for d in range(2):
                    act.dma_start(sin[:, d, :, :], st_d[d, bass.ds(at(g, 1), 1), :, :, :].rearrange("g q a n -> q (g a) n")
                                  ).then_inc(si_s, 16)

            def evac(g, m):
                n = 6 * g[1] + m
                unit_wait(act, q_of(g, m), slot_of(g, m))
                src, free = pair[n % 2], psum_free[n % 2]
                if m >= 4:
                    A.activation(zb[par(g)][:, m - 4, :], src[:, 0:T], ACT.Silu).then_inc(free, 1)
                    return
                A.activation(raw[:, m, PLAT], src[:, LAT], ACT.Copy)
                A.activation(raw[:, m, PCTX], src[:, CTX], ACT.Copy).then_inc(free, 1)
                act.drain().then_inc(rw_s, 1)

            def silu(g, m):
                act.wait_ge(cv_s, at(g, 4, m + 1))
                A.activation(xc[par(g)][:, m, LAT], tmp[:, m % 2, PLAT], ACT.Silu)
                A.activation(xc[par(g)][:, m, CTX], tmp[:, m % 2, PCTX], ACT.Silu).then_inc(sl_s, 1)

            def head():
                act.sem_inc(so_s, 32)
                act.sem_inc(fc_s, 1)
                load_state((None, 0))
                for n in range(3):
                    load_cum((None, 0), n)
                for m in range(4):
                    evac((None, 0), m)
                for m in range(4):
                    silu((None, 0), m)
                for m in range(4, 6):
                    evac((None, 0), m)

            def exps(g, n, more):
                c, d = order[n]
                k = 10 * g[1] + n
                act.wait_ge(ex_s, at(g, NS, n + 1))
                act.wait_ge(ar_s, at(g, NS, n + 1))
                A.activation(ee[k % 2][:, :, :], ee[k % 2][:, :, :], ACT.Exp)
                A.activation(cw[k % 2][:, :, :], cumb[k % 4][:, :, :], ACT.Exp).then_inc(ex_s, 1)
                if n + 3 < NS:
                    load_cum(g, n + 3)
                elif more:
                    load_cum(nxt(g), n + 3 - NS)

            def body(g, more):
                exps(g, 0, more)
                for n in range(NS):
                    if n + 1 < NS:
                        exps(g, n + 1, more)
                    if n == 3 and more:
                        act.wait_ge(sc_s, at(g, 1, 1))
                        load_state(nxt(g))
                    if n == 5:
                        act.wait_ge(ft_s, at(g, 1, 1))
                        act.wait_ge(so_s, at(g, 32, 32))
                        A.activation(so.rearrange("p d a n -> p (d a n)"), bank[:, 7, :], ACT.Copy).then_inc(fc_s, 1)
                        act.wait_ge(fc_s, at(g, 1, 2))
                        for dd in range(2):
                            act.dma_start(so_d[dd, bass.ds(at(g, 1), 1), :, :, :].rearrange("g q a n -> q (g a) n"),
                                          so[:, dd, :, :]).then_inc(so_s, 16)
                    if more:
                        for m in evac_at.get(n, ()):
                            if m == 4:
                                act.wait_ge(z_s, at(g, 1, 1))
                            evac(nxt(g), m)
                        for m in silu_at.get(n, ()):
                            silu(nxt(g), m)

            act.sem_inc(ex_s, 1)
            over_groups(act, [], head, body, None)
            act.wait_ge(so_s, 32 * (NG + 1))

        def pe(pe):
            def half(g, m, hh):
                n = 6 * g[1] + m
                s, pr = n % 4, n % 2
                if hh == 0:
                    pe.wait_ge(w_ready[s], q_of(g, m) * 16 + 16)
                    v = n // 2 + v0 // 2 if g[0] is None else g[0] * 6 + (n // 2 + v0 // 2)
                    pe.wait_ge(psum_free[pr], v + 1)
                for k in range(4 * hh, 4 * hh + 4):
                    st, en = k == 0, k == KD - 1
                    E.matmul(pair[pr][:, 0:LATN], ring[:, s, k, :], h[:, k, LAT], start=st, stop=en)
                    mm = E.matmul(pair[pr][:, LATN:T], ring[:, s, k, :], h[:, k, CTX], start=st, stop=en)
                if hh:
                    mm.then_inc(unit_done, 1)

            def head():
                for m in range(6):
                    half((None, 0), m, 0)
                    half((None, 0), m, 1)

            def body(g, more):
                p = par(g)
                pe.wait_ge(si_s, at(g, 32, 32))
                pe.wait_ge(fc_s, at(g, 1, 1))
                for d in range(2):
                    for t in range(2):
                        mm = E.transpose(bank[:, 7, (2 * d + t) * P:(2 * d + t + 1) * P], sin[:, d, t, :], ident)
                mm.then_inc(st_s, 1)
                pe.wait_ge(sl_s, at(g, 4, 4))
                pe.wait_ge(us_s, at(g, NS, 2))
                for c in range(NCH):
                    if c >= 3:
                        pe.wait_ge(tc_s, at(g, NCH, c - 2))
                    for m in range(3):
                        mm = E.transpose(bank[:, 4 + c % 3, m * P:(m + 1) * P], xc[p][:, m, chunk(c)], ident)
                    mm.then_inc(tu_s, 1)
                pe.wait_ge(tc_s, at(g, NCH, 4))
                for c in range(CT):
                    E.matmul(bank[:, 6, chunk(c)], xc[p][:, 2, chunk(c)], xc[p][:, 3, chunk(c)], start=True, stop=True)
                E.matmul(bank[:, 4, 0:P], xc[p][:, 2, chunk(CT)], xc[p][:, 3, chunk(CT)], start=True, stop=True).then_inc(cb_s, 1)
                pe.wait_ge(tc_s, at(g, NCH, NCH))
                pe.wait_ge(cc_s, at(g, 1, 1))
                todo = [(m, hh) for m in range(6) for hh in range(2)]
                for n, (c, d) in enumerate(order):
                    k = 10 * g[1] + n
                    pe.wait_ge(us_s, at(g, NS, n + 1))
                    pe.wait_ge(wt_s, at(g, NS, n + 1))
                    b = 5 + n % 2
                    for hh in range(4):
                        o = bank[64 * (hh % 2):64 * (hh % 2) + 64, b, (hh // 2) * P:(hh // 2 + 1) * P]
                        E.matmul(o, dx[k % 2][:, hh, :], ee[k % 2][:, hh, :], start=True, stop=n < 2)
                        if n >= 2:
                            E.matmul(o, S[:, d, hh * 64:hh * 64 + 64], cw[k % 2][:, hh, :], start=False, stop=True)
                    E.matmul(bank[:, b, 256:512], xt[:, c, 2 * P:3 * P], dxw[k % 2].rearrange("p h q -> p (h q)"),
                             start=True, stop=True).then_inc(pr_s, 1)
                    if n == 4:
                        pe.wait_ge(sf_s, at(g, 1, 1))
                        for dd in range(2):
                            for t in range(2):
                                mm = E.transpose(bank[:, 7, (2 * dd + t) * P:(2 * dd + t + 1) * P],
                                                 sfin[:, dd, t * P:(t + 1) * P], ident)
                        mm.then_inc(ft_s, 1)
                    if more:
                        for _ in range(halves[n]):
                            half(nxt(g), *todo.pop(0))

            over_groups(pe, [], head, body, None)

        def dve(dve):
            def conv_tile(g, m):
                dve.wait_ge(rw_s, at(g, 4, m + 1))
                if m >= 2:
                    dve.wait_ge(sl_s, at(g, 4, m - 1))
                elif g[0] is not None or g[1]:
                    dve.wait_ge(sl_s, at(g, 4, m - 1))
                tile = (lambda v: vec[:, bass.ds(at(g, 2, v + m), 1)]) if m < 2 else \
                       (lambda v: vec[:, bass.ds(at(g, 1, v + 16 + 8 * (m - 2)), 1)])
                conv(raw, m, tmp[:, m % 2], tile(V_OCW), tile(V_OCW + 32), tile(V_OCW + 64), tile(V_OCB))
                dve.sem_inc(cv_s, 1)

            def prepare(g, n):
                c, d = order[n]
                k = 10 * g[1] + n
                dve.wait_ge(ci_s[k % 4], (k // 4 + 1) * 16 if g[0] is None else g[0] * 80 + (k // 4 + 1) * 16)
                for hh in range(4):
                    sc1 = cumc[:, c, bass.ds(at(g, 4, 32 * d + hh), 1)]
                    ins = V.tensor_scalar(ee[k % 2][:, hh, :], cumb[k % 4][:, hh, :], sc1, 0.0, ALU.subtract, ALU.min)
                ins.then_inc(ar_s, 1)
                x4 = xt[:, c, 0:256].rearrange("p (h q) -> p h q", h=4)
                b64 = lambda v: hs(v, g, c, d).unsqueeze(2).to_broadcast([P, 4, 64])
                lv.done(V.tensor_tensor(dx[k % 2][:, :, :], x4, b64(dtc), ALU.mult))
                V.tensor_tensor(dxw[k % 2][:, :, :], dx[k % 2][:, :, :], b64(dece), ALU.mult)

            def weights(g, n):
                c, d = order[n]
                k = 10 * g[1] + n
                dve.wait_ge(ex_s, at(g, NS, n + 2))
                V.tensor_tensor(ee[k % 2][:, :, :], ee[k % 2][:, :, :],
                                cbm[:, d, c, :].unsqueeze(1).to_broadcast([P, 4, P]), ALU.mult)
                V.tensor_tensor(cw[k % 2][:, :, :], cw[k % 2][:, :, :],
                                xc[par(g)][:, 3, chunk(c)].unsqueeze(1).to_broadcast([P, 4, P]), ALU.mult).then_inc(wt_s, 1)

            def finish(g, n):
                c, d = order[n]
                b = 5 + n % 2
                dve.wait_ge(pr_s, at(g, NS, n + 1))
                Sd = S[:, d, :].rearrange("p (h q) -> p h q", h=4)
                if n >= 2:
                    lv.done(V.tensor_tensor(Sd, Sd, hs(cdec, g, c, d).unsqueeze(2).to_broadcast([P, 4, 64]), ALU.mult))
                for t in range(2):
                    yt = yb[:, bass.ds(at(g, 2, t), 1), chunk(c)].rearrange("p o t -> p (o t)")
                    pt = bank[:, b, t * P:(t + 1) * P]
                    if (c, d) in first:
                        V.scalar_tensor_tensor(yt, xc[par(g)][:, t, chunk(c)], dsk[:, bass.ds(at(g, 2, t), 1)],
                                               pt, ALU.mult, ALU.add)
                    else:
                        V.tensor_tensor(yt, yt, pt, ALU.add)
                if n >= 2:
                    lv.done(V.tensor_tensor(S[:, d, :], S[:, d, :], bank[:, b, 256:512], ALU.add))
                else:
                    lv.done(V.tensor_copy(sfin[:, d, :], bank[:, b, 256:512]))
                dve.sem_inc(us_s, 1)
                if n == 1:
                    dve.sem_inc(sf_s, 1)

            def head():
                for c in (slice(0, 1), slice(LATN + 1, LATN + 2), slice(PCTX.stop, PAD)):
                    lv.done(V.memset(raw[:, :, c], 0.0))
                dve.sem_inc(us_s, 2)
                dve.sem_inc(z_s, 1)
                for m in range(4):
                    conv_tile((None, 0), m)

            def body(g, more):
                dve.wait_ge(st_s, at(g, 1, 1))
                V.tensor_copy(S.rearrange("p d q -> p (d q)"), bank[:, 7, :]).then_inc(sc_s, 1)
                for c in range(NCH):
                    dve.wait_ge(tu_s, at(g, NCH, c + 1))
                    V.tensor_copy(xt[:, c, :], bank[:, 4 + c % 3, 0:3 * P]).then_inc(tc_s, 1)
                dve.wait_ge(tc_s, at(g, NCH, NCH))
                prepare(g, 0)
                dve.wait_ge(cb_s, at(g, 1, 1))
                for d in range(2):
                    mask = (upper, lower)[d]
                    V.tensor_tensor(cbm[:, d, 0:CT, :], bank[:, 6, :].rearrange("p (c t) -> p c t", c=CT),
                                    mask.unsqueeze(1).to_broadcast([P, CT, P]), ALU.mult)
                    ins = V.tensor_tensor(cbm[:, d, CT, :], bank[:, 4, 0:P], mask, ALU.mult)
                ins.then_inc(cc_s, 1)
                dve.wait_ge(cc_s, at(g, 1, 1))
                for n in range(NS):
                    weights(g, n)
                    if n + 1 < NS:
                        prepare(g, n + 1)
                    finish(g, n)
                    if more and n in conv_at:
                        conv_tile(nxt(g), conv_at[n])
                for t in range(2):
                    yt = yb[:, bass.ds(at(g, 2, t), 1), :].rearrange("p o t -> p (o t)")
                    lv.done(V.tensor_tensor(yt, yt, zb[par(g)][:, t, :], ALU.mult))
                dve.sem_inc(z_s, 1)

            over_groups(dve, [(lv, LV_SSD)], head, body, None)

        return pe, act, dve, fetches

    def stage_store(hn, out_p, out_x):
        ot = take(NCH, DM)
        t_s, c_s = sem("y_turned"), sem("y_copied")

        def pe(pe):
            for c in range(NCH):
                for half in range(2):
                    n = 2 * c + half
                    if n >= 2:
                        pe.wait_ge(c_s, n - 1)
                    for f in range(4):
                        mm = E.transpose(bank[:, n % 2, f * P:(f + 1) * P], hn[:, 4 * half + f, chunk(c)], ident)
                    mm.then_inc(t_s, 1)

        def dve(dve):
            for n in range(2 * NCH):
                dve.wait_ge(t_s, n + 1)
                V.tensor_copy(ot[:, n // 2, (n % 2) * 512:(n % 2 + 1) * 512], bank[:, n % 2, :]).then_inc(c_s, 1)

        def act(act):
            for c in range(NCH):
                act.wait_ge(c_s, 2 * c + 2)
                store(out_p[0, :, :] if c == CT else out_x[0, c * P:(c + 1) * P, :], ot[:, c, :])
            act.wait_ge(stored, 16 * nstores[0])

        return pe, act, dve

    out_p, out_x, out_c, out_n, out_m, out_r, out_s = outs
    scratch = nc.dram_tensor("cumulative_decays", (64, T), F32, kind="Internal").ap()
    def region(*parts):
        mark = top[0]
        for make in parts:
            top[0] = mark
            stages.append(make())
        top[0] = mark

    region(stage_load)
    region(stage_mod)

    cat = take(KD, T)
    base = top[0]
    nw = lambda l, n: vec[:, V_NORM + 16 * l + 8 * n:V_NORM + 16 * l + 8 * n + 8]
    region(lambda: stage_norm(x, cat, KD, 8, nw(0, 0), 0, "n1"))
    pb = take(15, PAD)
    after_pb = top[0]
    qk, vo, gates = take(8, PAD), take(8, T), take(T)
    region(lambda: stage_even_in(cat, qk, vo, pb, gates),
           lambda: stage_conv(qk, vo, pb),
           lambda: stage_mlstm(qk, vo, gates, cat[:, 0:4, :], out_c, out_n, out_m),
           lambda: stage_head_norm(cat[:, 0:4, :], ones, P, EPS, vec[:, V_AN:V_AN + 4], None, "ha",
                                   finish_mlstm(cat[:, 0:4, :], vo)))
    top[0] = after_pb
    kk, av, ld, cum = take(4, T), take(4, T), take(2, 4, T), take(2, 4, T)
    yb = cat[:, 4:8, :]
    region(lambda: stage_rwkv_in(pb, kk, av, ld, cum),
           lambda: stage_rwkv(pb, kk, av, ld, cum, yb, out_r))
    top[0] = after_pb
    region(lambda: stage_head_norm(yb, blk, 64, LN_EPS, vec[:, V_LW:V_LW + 4], vec[:, V_LB:V_LB + 4], "hb",
                                   lambda dve, j: None),
           lambda: stage_rwkv_out(pb, yb))
    region(lambda: stage_out(cat, a["ev_w_out"][0], (8,), 16))

    def ffn(l):
        top[0] = base
        region(lambda: stage_norm(x, cat, KD, 48 * l + 32, nw(l, 1), 48 * l + 24, f"f{l}"))
        hid = take(KF, T)
        region(lambda: stage_ffn_in(cat, hid, a["ffn_w_in"][l], f"ffn{l}"),
               lambda: stage_out(hid, a["ffn_w_out"][l], (8, 8, 6), 48 * l + 40))
        top[0] = base

    ffn(0)

    region(lambda: stage_norm(x, cat, KD, 48 + 8, nw(1, 0), 48, "n3"))
    yc = take(KC, T)
    dtc, cumc, dece, cdec = (take(NCH, 64) for _ in range(4))
    region(lambda: stage_dt(cat, dtc, cumc, dece, cdec, scratch),
           lambda: stage_ssd(cat, yc, dtc, cumc, dece, cdec, scratch, dsk, out_s))
    region(lambda: stage_norm(yc, yc, KC, None, vec[:, V_ONW:V_ONW + KC], None, "n4"),
           lambda: stage_out(yc, a["od_w_out"][0], (8, 8), 48 + 16))
    top[0] = base
    ffn(1)
    region(lambda: stage_norm(x, cat, KD, None, vec[:, V_FIN:V_FIN + KD], None, "n5"),
           lambda: stage_store(cat, out_p, out_x))

    block = ctx.enter_context(nc.Block())

    @block.sync
    def _(sp):
        for st in stages:
            if len(st) == 4:
                st[3](sp)

    @block.scalar
    def _(act):
        eng_of["act"] = la.eng = act
        for st in stages:
            st[1](act)
            fence("act")

    @block.vector
    def _(dve):
        eng_of["dve"] = lv.eng = dve
        for st in stages:
            st[2](dve)
            fence("dve")

    @block.tensor
    def _(pe):
        eng_of["pe"] = pe
        pe.sem_inc(unit_done, 4)
        for p in range(2):
            pe.sem_inc(psum_free[p], 1)
        for st in stages:
            st[0](pe)
            fence("pe")


LV_SSD = 84


_INS = ['x_prompt', 'x_sample', 'state_mlstm_c', 'state_mlstm_n', 'state_mlstm_m', 'state_rwkv', 'state_ssd',
        'c', 'c_ctx', 'mod_w', 'mod_b', 'norm_w', 'ffn_w_in', 'ffn_w_out',
        'ev_w_in', 'ev_a_conv_w', 'ev_a_conv_b', 'ev_a_gate_b', 'ev_a_norm_w',
        'ev_b_mu', 'ev_b_w0', 'ev_b_w_up', 'ev_b_a0', 'ev_b_a_up', 'ev_b_g_up', 'ev_b_k_k', 'ev_b_k_a', 'ev_b_u',
        'ev_b_ln_w', 'ev_b_ln_b', 'ev_w_out',
        'od_w_in', 'od_conv_w', 'od_conv_b', 'od_dt_bias', 'od_a_log', 'od_d', 'od_norm_w', 'od_w_out',
        'final_norm_w']
_OUTS = [((1, 128, 1024), 'float32'), ((1, 512, 1024), 'float32'), ((1, 1, 2, 4, 128, 128), 'float32'),
         ((1, 1, 2, 4, 128), 'float32'), ((1, 1, 2, 4), 'float32'), ((1, 1, 2, 8, 64, 64), 'float32'),
         ((1, 1, 2, 32, 64, 128), 'float32')]


def _constants():
    import numpy as np
    c = np.zeros((P, NCONST), np.float32)
    i = np.arange(P)
    c[:, C_ID:C_ID + P] = np.eye(P)
    c[:, C_ONE:C_ONE + P] = 1
    c[:, C_UP:C_UP + P] = i[:, None] <= i[None, :]
    c[:, C_LO:C_LO + P] = i[:, None] >= i[None, :]
    c[:, C_BLK:C_BLK + P] = i[:, None] // 64 == i[None, :] // 64
    s, t = (i % 64)[:, None], np.arange(64)[None, :]
    for d in range(2):
        ss, tt = (s, t) if d == 0 else (63 - s, 63 - t)
        for l in range(6):
            b = 2 ** l
            at = C_LVL + (d * 6 + l) * 64
            c[:, at:at + 64] = (tt // b == ss // b + 1) & ((tt // b) % 2 == 1)
        c[:, C_MK + d * 128:C_MK + d * 128 + 64] = ss < tt
        c[:, C_MK + d * 128 + 64:C_MK + d * 128 + 128] = ss <= tt
    c[:, C_I64:C_I64 + 64] = s == t
    c[:, C_RST:C_RST + T] = (np.arange(T) % 64 != 0)[None]
    nf = DM // 4
    freq = np.exp(-np.log(10000.0).astype(np.float32) * np.arange(nf, dtype=np.float32) / nf)
    for f in range(8):
        fr = freq[(f % 2) * P:(f % 2 + 1) * P][:, None]
        fn = np.sin if f % 4 < 2 else np.cos
        if f < 4:
            c[:, C_POSR + f * 8:C_POSR + f * 8 + 8] = fn(np.arange(8, dtype=np.float32)[None] * fr)
        else:
            c[:, C_POSC + (f - 4) * 64:C_POSC + (f - 3) * 64] = fn(np.arange(64, dtype=np.float32)[None] * fr)
    return c


def kernel(**inputs):
    import numpy as _np
    import concourse.bacc as _bacc
    from concourse import mybir as _mybir
    from concourse.bass_utils import run_bass_kernel_spmd as _run

    nc = _bacc.Bacc("TRN2", target_bir_lowering=False, num_devices=1)
    arrays, args = {}, {}
    for name in _INS + ["consts"]:
        arr = _constants() if name == "consts" else _np.ascontiguousarray(inputs[name])
        arrays[f"in_{name}_dram"] = arr
        args[name] = nc.dram_tensor(f"in_{name}_dram", arr.shape, _mybir.dt.from_np(arr.dtype), kind="ExternalInput").ap()
    outs = []
    for i, (shape, dtype) in enumerate(_OUTS):
        dt = _mybir.dt.from_np(_np.dtype(dtype))
        outs.append(nc.dram_tensor(f"out_{i}_dram", shape, dt, kind="ExternalOutput").ap())
    build(nc, args, outs)
    r = _run(nc, [arrays], core_ids=[0])
    return tuple(r.results[0][f"out_{i}_dram"] for i in range(len(_OUTS)))
```
